# Optimizing a Trainium2 kernel written in Bass

```python
import math
import jax, jax.numpy as jnp
from jax import lax
import numpy as np
import jax
import jax.numpy as jnp

D_MODEL = 1024
BATCH = 1
SEQ = 256
DEPTH = 1

SSD_D_INNER = 1024
SSD_HEAD_DIM = 64
SSD_HEADS = SSD_D_INNER // SSD_HEAD_DIM
SSD_GROUPS = 2
SSD_STATE = 128
SSD_CONV = 4
SSD_CHUNK = 128
SSD_CONV_DIM = SSD_D_INNER + 2 * SSD_GROUPS * SSD_STATE

ATTN_HEAD_DIM = 128
ATTN_HEADS_PER_GROUP = 4
DILATED_GROUPS = ((128, 1), (512, 4), (2048, 16))
ATTN_HEADS = ATTN_HEADS_PER_GROUP * len(DILATED_GROUPS)
ATTN_WIDTH = ATTN_HEADS * ATTN_HEAD_DIM
ATTN_OUT_WIDTH = ATTN_HEADS_PER_GROUP * ATTN_HEAD_DIM

POOL_WINDOWS = (2, 4, 8, 16)
POOL_WIDTH = 1024
POOL_GROUP_WIDTH = POOL_WIDTH // len(POOL_WINDOWS)

N_BRANCHES = 3
D_FF = 4 * D_MODEL
EPS = 1e-6
IN_SIZES = (SSD_D_INNER, SSD_CONV_DIM, SSD_HEADS, ATTN_WIDTH, ATTN_WIDTH, ATTN_WIDTH, POOL_WIDTH, N_BRANCHES * D_MODEL)
IN_WIDTH = SSD_D_INNER + SSD_CONV_DIM + SSD_HEADS + 3 * ATTN_WIDTH + POOL_WIDTH + N_BRANCHES * D_MODEL


def _rms(x, w):
    xf = x.astype(jnp.float32)
    y = xf * lax.rsqrt(jnp.mean(xf * xf, axis=-1, keepdims=True) + EPS)
    return (y * w.astype(jnp.float32)).astype(x.dtype)

def _alibi_slopes(n):
    def pow2(k):
        start = 2.0 ** (-8.0 / k)
        return [start ** (i + 1) for i in range(k)]
    if math.log2(n).is_integer():
        s = pow2(n)
    else:
        c = 2 ** math.floor(math.log2(n))
        s = pow2(c) + pow2(2 * c)[0::2][: n - c]
    return np.sort(np.asarray(s, np.float32))[::-1].copy()

def _causal_dwconv(x, w, bias):
    ch = x.shape[-1]
    y = lax.conv_general_dilated(x, w[:, None, :].astype(x.dtype), window_strides=(1,),
                                 padding=[(SSD_CONV - 1, 0)],
                                 dimension_numbers=('NWC', 'WIO', 'NWC'),
                                 feature_group_count=ch)
    return y + bias

def _ssd(xs, dt, A, B, C, D):
    b, S, H, P = xs.shape
    G, N, L = SSD_GROUPS, SSD_STATE, SSD_CHUNK
    J = H // G
    nc = S // L
    xc = xs.reshape(b, nc, L, G, J, P)
    X = xc * dt.reshape(b, nc, L, G, J)[..., None]
    a_cum = jnp.cumsum((dt * A).reshape(b, nc, L, G, J), axis=2)
    Bc = B.reshape(b, nc, L, G, N)
    Cc = C.reshape(b, nc, L, G, N)
    seg = a_cum[:, :, :, None] - a_cum[:, :, None, :]
    causal = jnp.tril(jnp.ones((L, L), bool))[:, :, None, None]
    decay = jnp.exp(jnp.where(causal, seg, -jnp.inf))
    cb = jnp.einsum('bclgn,bcsgn->bclsg', Cc, Bc)
    y_diag = jnp.einsum('bclsgj,bcsgjp->bclgjp', cb[..., None] * decay, X)
    Xd = X * jnp.exp(a_cum[:, :, -1:] - a_cum)[..., None]
    states = jnp.einsum('bclgn,bclgjp->bcgjpn', Bc, Xd)
    chunk_decay = jnp.exp(a_cum[:, :, -1])

    def step(h, inp):
        st, dec = inp
        return dec[..., None, None] * h + st, h

    h0 = jnp.zeros((b, G, J, P, N), X.dtype)
    _, prev = lax.scan(step, h0, (jnp.moveaxis(states, 1, 0), jnp.moveaxis(chunk_decay, 1, 0)))
    prev = jnp.moveaxis(prev, 0, 1)
    y_off = jnp.einsum('bclgn,bcgjpn->bclgjp', Cc, prev) * jnp.exp(a_cum)[..., None]
    y = y_diag + y_off + D.reshape(G, J)[:, :, None] * xc
    return y.reshape(b, S, H * P)

def _dilated_window_attn(q, k, v, steps, dilation, slopes):
    b, S, h, e = q.shape
    n = S // dilation
    nb = -(-n // steps)
    n_pad = nb * steps

    def to_sub(t):
        t = t.reshape(b, n, dilation, h, e).transpose(0, 3, 2, 1, 4)
        return jnp.pad(t, ((0, 0), (0, 0), (0, 0), (0, n_pad - n), (0, 0)))

    qs, ks, vs = to_sub(q), to_sub(k), to_sub(v)
    qb = qs.reshape(b, h, dilation, nb, steps, e)

    def band(t):
        tp = jnp.pad(t, ((0, 0), (0, 0), (0, 0), (steps, 0), (0, 0)))
        prev = tp[:, :, :, :n_pad].reshape(b, h, dilation, nb, steps, e)
        cur = t.reshape(b, h, dilation, nb, steps, e)
        return jnp.concatenate([prev, cur], axis=4)

    kb, vb = band(ks), band(vs)
    s = jnp.einsum('bhdnqe,bhdnke->bhdnqk', qb, kb) * (e ** -0.5)
    qi = jnp.arange(steps)[:, None]
    kj = jnp.arange(2 * steps)[None, :]
    rel = qi + steps - kj
    blk = jnp.arange(nb)[:, None, None]
    valid = (rel >= 0) & (rel <= steps) & (blk * steps + kj - steps >= 0)
    alibi = -slopes[:, None, None] * (rel * dilation).astype(jnp.float32)
    s = jnp.where(valid, s + alibi[:, None, None], -jnp.inf)
    lse = jax.nn.logsumexp(s, axis=-1)
    p = jnp.exp(s - lse[..., None])
    o = jnp.einsum('bhdnqk,bhdnke->bhdnqe', p, vb)
    o = o.reshape(b, h, dilation, n_pad, e)[:, :, :, :n].transpose(0, 3, 2, 1, 4).reshape(b, S, h, e)
    lse = lse.reshape(b, h, dilation, n_pad)[:, :, :, :n].transpose(0, 3, 2, 1).reshape(b, S, h)
    return o, lse

def _multi_scale_pool(u, w_mix):
    b, S, _ = u.shape
    ug = u.reshape(b, S, len(POOL_WINDOWS), POOL_GROUP_WIDTH)
    cs = jnp.cumsum(ug, axis=1)
    t = jnp.arange(S)
    outs = []
    for gi, w in enumerate(POOL_WINDOWS):
        csg = cs[:, :, gi]
        shifted = jnp.pad(csg, ((0, 0), (w, 0), (0, 0)))[:, :S]
        count = jnp.minimum(t + 1, w).astype(jnp.float32)[None, :, None]
        outs.append((csg - shifted) / count - ug[:, :, gi])
    pooled = jnp.stack(outs, axis=2)
    return jnp.einsum('bsgi,gio->bsgo', pooled, w_mix).reshape(b, S, POOL_WIDTH)

def _hybrid_mixer(h, w_in, conv_w, conv_b, dt_bias, a_log, d_skip, ssd_norm_w, w_ssd_out,
                  q_norm_w, k_norm_w, w_attn_out, w_pool_mix, pool_scale, w_pool_out, w_out, slopes):
    f32 = jnp.float32
    dtype = h.dtype
    b, S, _ = h.shape
    splits = np.cumsum(IN_SIZES)[:-1].tolist()
    z, xbc, dt_raw, q, k, v, u, gates = jnp.split(h @ w_in, splits, axis=-1)

    xbc = jax.nn.silu(_causal_dwconv(xbc, conv_w, conv_b)).astype(f32)
    xs, Bm, Cm = jnp.split(xbc, [SSD_D_INNER, SSD_D_INNER + SSD_GROUPS * SSD_STATE], axis=-1)
    dt = jax.nn.softplus(dt_raw.astype(f32) + dt_bias.astype(f32))
    A = -jnp.exp(a_log.astype(f32))
    y = _ssd(xs.reshape(b, S, SSD_HEADS, SSD_HEAD_DIM), dt, A,
             Bm.reshape(b, S, SSD_GROUPS, SSD_STATE), Cm.reshape(b, S, SSD_GROUPS, SSD_STATE),
             d_skip.astype(f32))
    y = (y * jax.nn.silu(z.astype(f32))).reshape(b, S, SSD_GROUPS, SSD_D_INNER // SSD_GROUPS)
    y = (y * lax.rsqrt(jnp.mean(y * y, axis=-1, keepdims=True) + EPS)).reshape(b, S, SSD_D_INNER)
    y_ssd = (y * ssd_norm_w.astype(f32)).astype(dtype) @ w_ssd_out

    qh = _rms(q.reshape(b, S, ATTN_HEADS, ATTN_HEAD_DIM).astype(f32), q_norm_w)
    kh = _rms(k.reshape(b, S, ATTN_HEADS, ATTN_HEAD_DIM).astype(f32), k_norm_w)
    vh = v.reshape(b, S, ATTN_HEADS, ATTN_HEAD_DIM).astype(f32)
    outs, lses = [], []
    for gi, (win, dil) in enumerate(DILATED_GROUPS):
        sl = slice(gi * ATTN_HEADS_PER_GROUP, (gi + 1) * ATTN_HEADS_PER_GROUP)
        o, lse = _dilated_window_attn(qh[:, :, sl], kh[:, :, sl], vh[:, :, sl], win // dil, dil, slopes[gi])
        outs.append(o)
        lses.append(lse)
    wts = jax.nn.softmax(jnp.stack(lses, axis=0), axis=0)
    o = jnp.sum(wts[..., None] * jnp.stack(outs, axis=0), axis=0).reshape(b, S, ATTN_OUT_WIDTH)
    y_attn = o.astype(dtype) @ w_attn_out

    y_pool = (_multi_scale_pool(u.astype(f32), w_pool_mix) * pool_scale).astype(dtype) @ w_pool_out

    g_ssd, g_attn, g_pool = jnp.split(jax.nn.sigmoid(gates.astype(f32)).astype(dtype), N_BRANCHES, axis=-1)
    return (g_ssd * y_ssd + g_attn * y_attn + g_pool * y_pool) @ w_out

def first_inputs(seed: int = 0) -> dict:
    key = jax.random.key(seed)
    ks = jax.random.split(key, 24)
    n = jax.random.normal
    L, D = DEPTH, D_MODEL
    u01 = jax.random.uniform(ks[9], (L, SSD_HEADS))
    dt0 = jnp.exp(u01 * (math.log(0.1) - math.log(0.001)) + math.log(0.001))
    return {
        "x": n(ks[0], (BATCH, SEQ, D), jnp.float32),
        "c": n(ks[1], (BATCH, D), jnp.float32),
        "w_ada": n(ks[2], (L, D, 6 * D)) * D ** -0.5,
        "b_ada": n(ks[3], (L, 6 * D)) * 0.01,
        "norm1_w": 1.0 + 0.05 * n(ks[4], (L, D)),
        "norm2_w": 1.0 + 0.05 * n(ks[5], (L, D)),
        "w_in": n(ks[6], (L, D, IN_WIDTH)) * D ** -0.5,
        "conv_w": n(ks[7], (L, SSD_CONV, SSD_CONV_DIM)) * SSD_CONV ** -0.5,
        "conv_b": n(ks[8], (L, SSD_CONV_DIM)) * 0.01,
        "dt_bias": dt0 + jnp.log(-jnp.expm1(-dt0)),
        "a_log": jnp.log(jax.random.uniform(ks[10], (L, SSD_HEADS), minval=1.0, maxval=16.0)),
        "d_skip": 1.0 + 0.05 * n(ks[11], (L, SSD_HEADS)),
        "ssd_norm_w": 1.0 + 0.05 * n(ks[12], (L, SSD_D_INNER)),
        "w_ssd_out": n(ks[13], (L, SSD_D_INNER, D)) * SSD_D_INNER ** -0.5,
        "q_norm_w": 1.0 + 0.05 * n(ks[14], (L, ATTN_HEAD_DIM)),
        "k_norm_w": 1.0 + 0.05 * n(ks[15], (L, ATTN_HEAD_DIM)),
        "w_attn_out": n(ks[16], (L, ATTN_OUT_WIDTH, D)) * ATTN_OUT_WIDTH ** -0.5,
        "w_pool_mix": n(ks[17], (L, len(POOL_WINDOWS), POOL_GROUP_WIDTH, POOL_GROUP_WIDTH)) * POOL_GROUP_WIDTH ** -0.5,
        "pool_scale": 1.0 + 0.05 * n(ks[18], (L, POOL_WIDTH)),
        "w_pool_out": n(ks[19], (L, POOL_WIDTH, D)) * POOL_WIDTH ** -0.5,
        "w_out": n(ks[20], (L, D, D)) * D ** -0.5,
        "w_ff1": n(ks[21], (L, D, D_FF)) * D ** -0.5,
        "w_ff2": n(ks[22], (L, D_FF, D)) * D_FF ** -0.5,
    }

def first_block(x, c, w_ada, b_ada, norm1_w, norm2_w, w_in, conv_w, conv_b, dt_bias, a_log, d_skip,
              ssd_norm_w, w_ssd_out, q_norm_w, k_norm_w, w_attn_out, w_pool_mix, pool_scale,
              w_pool_out, w_out, w_ff1, w_ff2):
    cond = jax.nn.silu(c)
    slopes = jnp.asarray(_alibi_slopes(ATTN_HEADS)).reshape(len(DILATED_GROUPS), ATTN_HEADS_PER_GROUP)
    for l in range(DEPTH):
        mod = (cond @ w_ada[l] + b_ada[l])[:, None, :]
        sh1, sc1, g1, sh2, sc2, g2 = jnp.split(mod, 6, axis=-1)
        h = _rms(x, norm1_w[l]) * (1 + sc1) + sh1
        x = x + g1 * _hybrid_mixer(h, w_in[l], conv_w[l], conv_b[l], dt_bias[l], a_log[l], d_skip[l],
                                   ssd_norm_w[l], w_ssd_out[l], q_norm_w[l], k_norm_w[l], w_attn_out[l],
                                   w_pool_mix[l], pool_scale[l], w_pool_out[l], w_out[l], slopes)
        h = _rms(x, norm2_w[l]) * (1 + sc2) + sh2
        x = x + g2 * (jnp.square(jax.nn.relu(h @ w_ff1[l])) @ w_ff2[l])
    return x


DEPTH_2 = 2

HEAD_DIM = 64
A_Q_HEADS = 8
A_KV_HEADS = 2
A_GROUP = A_Q_HEADS // A_KV_HEADS
WINDOW = 128
N_BUCKETS = 32
MAX_DISTANCE = 128
B_HEADS = 8
B_DK = 64
B_DV = 64
B_CONV = 4
CHUNK = 64
A_Q_W = A_Q_HEADS * HEAD_DIM
A_KV_W = A_KV_HEADS * HEAD_DIM
B_QK_W = B_HEADS * B_DK
B_V_W = B_HEADS * B_DV
B_QKV_W = 2 * B_QK_W + B_V_W
AB_SIZES = (A_Q_W, A_KV_W, A_KV_W, B_QKV_W, B_V_W, B_HEADS, B_HEADS)
AB_IN = sum(AB_SIZES)
AB_OUT = A_Q_W + B_V_W
LRU_WIDTH = D_MODEL
LRU_BLOCKS = 8
LRU_BW = LRU_WIDTH // LRU_BLOCKS
LRU_CONV = 4
LRU_C = 8.0
SC_WIDTH = D_MODEL // 2
SC_CONV = 3
CD_SIZES = (LRU_WIDTH, LRU_WIDTH, SC_WIDTH, SC_WIDTH, SC_WIDTH)
CD_IN = sum(CD_SIZES)
CD_OUT = LRU_WIDTH + SC_WIDTH
D_FF_2 = 2816
N_EXPERTS = 8
TOP_K = 2
D_FF_EXPERT = 3584
N_EVEN = (DEPTH_2 + 1) // 2
N_ODD = DEPTH_2 // 2


def split_cols(t, sizes):
    return jnp.split(t, [int(s) for s in np.cumsum(sizes)[:-1]], axis=-1)

def rmsnorm(x, w):
    xf = x.astype(jnp.float32)
    y = xf * lax.rsqrt(jnp.mean(xf * xf, axis=-1, keepdims=True) + EPS)
    return (y * w.astype(jnp.float32)).astype(x.dtype)

def l2norm(x):
    xf = x.astype(jnp.float32)
    return xf * lax.rsqrt(jnp.sum(xf * xf, axis=-1, keepdims=True) + EPS)

def causal_dwconv(x, w, b=None):
    K = w.shape[0]
    T = x.shape[1]
    xp = jnp.pad(x, ((0, 0), (K - 1, 0), (0, 0)))
    y = xp[:, 0:T] * w[0]
    for k in range(1, K):
        y = y + xp[:, k:k + T] * w[k]
    if b is not None:
        y = y + b
    return y

def t5_causal_bucket(dist):
    max_exact = N_BUCKETS // 2
    d = np.maximum(dist, 0)
    large = max_exact + (np.log(np.maximum(d, 1) / max_exact) / math.log(MAX_DISTANCE / max_exact)
                         * (N_BUCKETS - max_exact)).astype(np.int32)
    large = np.minimum(large, N_BUCKETS - 1)
    return np.where(d < max_exact, d, large).astype(np.int32)

def swa_sink_attention(q, k, v, sinks, rel_bias):
    Bsz, T = q.shape[0], q.shape[1]
    nb = T // WINDOW
    qb = q.reshape(Bsz, nb, WINDOW, A_KV_HEADS, A_GROUP, HEAD_DIM)

    def band(t):
        tb = t.reshape(Bsz, nb, WINDOW, A_KV_HEADS, HEAD_DIM)
        prev = jnp.pad(tb[:, :-1], ((0, 0), (1, 0), (0, 0), (0, 0), (0, 0)))
        return jnp.concatenate([prev, tb], axis=2)

    kb, vb = band(k), band(v)
    logits = jnp.einsum('bnqkgd,bnskd->bnkgqs', qb, kb,
                        preferred_element_type=jnp.float32) * (HEAD_DIM ** -0.5)
    qi = np.arange(WINDOW)[:, None]
    s = np.arange(2 * WINDOW)[None, :]
    dist = qi + WINDOW - s
    in_window = (dist >= 0) & (dist < WINDOW)
    bias = rel_bias[t5_causal_bucket(dist)].astype(jnp.float32)
    bias = jnp.transpose(bias, (2, 0, 1)).reshape(A_KV_HEADS, A_GROUP, WINDOW, 2 * WINDOW)
    key_valid = (np.arange(nb)[:, None] * WINDOW - WINDOW + s) >= 0
    mask = in_window[None] & key_valid[:, None, :]
    logits = jnp.where(mask[None, :, None, None], logits + bias, -jnp.inf)
    sink = sinks.astype(jnp.float32).reshape(A_KV_HEADS, A_GROUP)[None, None, :, :, None, None]
    m = jnp.maximum(jnp.max(logits, axis=-1, keepdims=True), sink)
    p = jnp.exp(logits - m)
    p = p / (jnp.sum(p, axis=-1, keepdims=True) + jnp.exp(sink - m))
    out = jnp.einsum('bnkgqs,bnskd->bnqkgd', p.astype(v.dtype), vb)
    return out.reshape(Bsz, T, A_Q_W)

def gated_delta_rule(q, k, v, g, beta):
    Bsz, T, H, dk = q.shape
    dv = v.shape[-1]
    n = T // CHUNK

    def chunks(t):
        t = t.astype(jnp.float32).reshape((Bsz, n, CHUNK, H) + t.shape[3:])
        return jnp.moveaxis(t, 3, 1)

    q, k, v, g, beta = chunks(q), chunks(k), chunks(v), chunks(g), chunks(beta)
    q = q * (dk ** -0.5)
    g = jnp.cumsum(g, axis=-1)
    causal = np.tril(np.ones((CHUNK, CHUNK), dtype=bool))
    strict = np.tril(np.ones((CHUNK, CHUNK), dtype=bool), -1)
    decay = jnp.exp(jnp.where(causal, g[..., :, None] - g[..., None, :], -jnp.inf))
    kk = jnp.einsum('bhncd,bhnsd->bhncs', k, k)
    L = jnp.where(strict, beta[..., None] * kk * decay, 0.0)
    eye = jnp.eye(CHUNK, dtype=jnp.float32)
    Tm = lax.linalg.triangular_solve(eye + L, jnp.broadcast_to(eye, L.shape),
                                     left_side=True, lower=True, unit_diagonal=True)
    u = Tm @ (v * beta[..., None])
    w = Tm @ (k * (beta * jnp.exp(g))[..., None])
    qk = jnp.where(causal, jnp.einsum('bhncd,bhnsd->bhncs', q, k) * decay, 0.0)
    g_last = g[..., -1:]
    k_dec = k * jnp.exp(g_last - g)[..., None]
    q_dec = q * jnp.exp(g)[..., None]

    def step(S, xs):
        q_i, k_i, u_i, w_i, qk_i, gl_i = xs
        v_new = u_i - jnp.einsum('bhcd,bhde->bhce', w_i, S)
        o = jnp.einsum('bhcd,bhde->bhce', q_i, S) + jnp.einsum('bhcs,bhse->bhce', qk_i, v_new)
        S = S * jnp.exp(gl_i)[..., None] + jnp.einsum('bhcd,bhce->bhde', k_i, v_new)
        return S, o

    xs = tuple(jnp.moveaxis(t, 2, 0) for t in (q_dec, k_dec, u, w, qk, g_last))
    S0 = jnp.zeros((Bsz, H, dk, dv), jnp.float32)
    _, o = lax.scan(step, S0, xs)
    return jnp.transpose(o, (1, 0, 3, 2, 4)).reshape(Bsz, T, H, dv)

def mixer_ab(h, w_in, sinks, conv_w, a_log, dt_bias, norm_w, w_out, rel_bias):
    Bsz, T, _ = h.shape
    qa, ka, va, qkv_b, gate_b, beta_b, a_b = split_cols(h @ w_in, AB_SIZES)
    attn = swa_sink_attention(qa.reshape(Bsz, T, A_Q_HEADS, HEAD_DIM),
                              ka.reshape(Bsz, T, A_KV_HEADS, HEAD_DIM),
                              va.reshape(Bsz, T, A_KV_HEADS, HEAD_DIM), sinks, rel_bias)
    qkv_b = jax.nn.silu(causal_dwconv(qkv_b, conv_w))
    qb, kb, vb = split_cols(qkv_b, (B_QK_W, B_QK_W, B_V_W))
    qb = l2norm(qb.reshape(Bsz, T, B_HEADS, B_DK))
    kb = l2norm(kb.reshape(Bsz, T, B_HEADS, B_DK))
    vb = vb.reshape(Bsz, T, B_HEADS, B_DV)
    beta = jax.nn.sigmoid(beta_b.astype(jnp.float32))
    g = -jnp.exp(a_log.astype(jnp.float32)) * jax.nn.softplus(a_b.astype(jnp.float32) + dt_bias.astype(jnp.float32))
    o = gated_delta_rule(qb, kb, vb, g, beta)
    o = rmsnorm(o, norm_w) * jax.nn.silu(gate_b.astype(jnp.float32).reshape(Bsz, T, B_HEADS, B_DV))
    o = o.reshape(Bsz, T, B_V_W).astype(h.dtype)
    return jnp.concatenate([attn, o], axis=-1) @ w_out

def lru_combine(left, right):
    a1, b1 = left
    a2, b2 = right
    return a1 * a2, a2 * b1 + b2

def mixer_cd(h, w_in, conv_w, conv_b, gate_a_w, gate_a_b, gate_x_w, gate_x_b, lam, sconv_w, w_out):
    Bsz, T, _ = h.shape
    xc, yc, bd, cd, hd = split_cols(h @ w_in, CD_SIZES)
    xc = causal_dwconv(xc, conv_w, conv_b)
    xblk = xc.reshape(Bsz, T, LRU_BLOCKS, LRU_BW)
    r = jax.nn.sigmoid((jnp.einsum('btni,nij->btnj', xblk, gate_a_w).reshape(Bsz, T, LRU_WIDTH)
                        + gate_a_b).astype(jnp.float32))
    i = jax.nn.sigmoid((jnp.einsum('btni,nij->btnj', xblk, gate_x_w).reshape(Bsz, T, LRU_WIDTH)
                        + gate_x_b).astype(jnp.float32))
    log_a = -LRU_C * r * jax.nn.softplus(-lam.astype(jnp.float32))
    a = jnp.exp(log_a)
    b = jnp.sqrt(-jnp.expm1(2.0 * log_a)) * (i * xc.astype(jnp.float32))
    _, hs = lax.associative_scan(lru_combine, (a, b), axis=1)
    yc_out = hs.astype(h.dtype) * jax.nn.gelu(yc)
    yd_out = bd * causal_dwconv(cd * hd, sconv_w)
    return jnp.concatenate([yc_out, yd_out], axis=-1) @ w_out

def swiglu(h, wg, wu, wd):
    return (jax.nn.silu(h @ wg) * (h @ wu)) @ wd

def moe_swiglu(h, router_w, router_b, wg, wu, wd):
    logits = (h @ router_w).astype(jnp.float32) + router_b.astype(jnp.float32)
    top_val, top_idx = lax.top_k(logits, TOP_K)
    top_w = jax.nn.softmax(top_val, axis=-1)
    gates = jnp.sum(jax.nn.one_hot(top_idx, N_EXPERTS, dtype=jnp.float32) * top_w[..., None], axis=-2)
    gates = gates.astype(h.dtype)
    out = jnp.zeros_like(h)
    for e in range(N_EXPERTS):
        out = out + gates[..., e:e + 1] * swiglu(h, wg[e], wu[e], wd[e])
    return out

def second_inputs(seed: int = 0) -> dict:
    key = jax.random.key(seed)
    ks = jax.random.split(key, 33)
    D = D_MODEL

    def nrm(k, shape, scale):
        return jax.random.normal(k, shape, jnp.float32) * scale

    def gain(k, shape):
        return 1.0 + nrm(k, shape, 0.02)

    dt = jnp.exp(jax.random.uniform(ks[12], (N_EVEN, B_HEADS), jnp.float32, math.log(1e-3), math.log(1e-1)))
    u = jax.random.uniform(ks[25], (N_ODD, LRU_WIDTH), jnp.float32, 0.9, 0.999)
    p = u ** (1.0 / LRU_C)
    return {
        'x': nrm(ks[0], (BATCH, SEQ, D), 1.0),
        'c': nrm(ks[1], (BATCH, D), 1.0),
        'rel_bias': nrm(ks[2], (N_BUCKETS, A_Q_HEADS), 0.5),
        'ada_w': nrm(ks[3], (DEPTH_2, D, 6 * D), 0.5 * D ** -0.5),
        'ada_b': nrm(ks[4], (DEPTH_2, 6 * D), 0.02),
        'norm_mix_w': gain(ks[5], (DEPTH_2, D)),
        'norm_ffn_w': gain(ks[6], (DEPTH_2, D)),
        'final_norm_w': gain(ks[7], (D,)),
        'ab_w_in': nrm(ks[8], (N_EVEN, D, AB_IN), D ** -0.5),
        'attn_sinks': nrm(ks[9], (N_EVEN, A_Q_HEADS), 0.5),
        'dn_conv_w': nrm(ks[10], (N_EVEN, B_CONV, B_QKV_W), B_CONV ** -0.5),
        'dn_a_log': jnp.log(jax.random.uniform(ks[11], (N_EVEN, B_HEADS), jnp.float32, 1.0, 16.0)),
        'dn_dt_bias': dt + jnp.log(-jnp.expm1(-dt)),
        'dn_norm_w': gain(ks[13], (N_EVEN, B_DV)),
        'ab_w_out': nrm(ks[14], (N_EVEN, AB_OUT, D), AB_OUT ** -0.5),
        'ffn_w_gate': nrm(ks[15], (N_EVEN, D, D_FF_2), D ** -0.5),
        'ffn_w_up': nrm(ks[16], (N_EVEN, D, D_FF_2), D ** -0.5),
        'ffn_w_down': nrm(ks[17], (N_EVEN, D_FF_2, D), D_FF_2 ** -0.5),
        'cd_w_in': nrm(ks[18], (N_ODD, D, CD_IN), D ** -0.5),
        'lru_conv_w': nrm(ks[19], (N_ODD, LRU_CONV, LRU_WIDTH), LRU_CONV ** -0.5),
        'lru_conv_b': nrm(ks[20], (N_ODD, LRU_WIDTH), 0.01),
        'lru_gate_a_w': nrm(ks[21], (N_ODD, LRU_BLOCKS, LRU_BW, LRU_BW), LRU_BW ** -0.5),
        'lru_gate_a_b': nrm(ks[22], (N_ODD, LRU_WIDTH), 0.01),
        'lru_gate_x_w': nrm(ks[23], (N_ODD, LRU_BLOCKS, LRU_BW, LRU_BW), LRU_BW ** -0.5),
        'lru_gate_x_b': nrm(ks[24], (N_ODD, LRU_WIDTH), 0.01),
        'lru_lambda': jnp.log(p) - jnp.log1p(-p),
        'sconv_w': nrm(ks[26], (N_ODD, SC_CONV, SC_WIDTH), SC_CONV ** -0.5),
        'cd_w_out': nrm(ks[27], (N_ODD, CD_OUT, D), CD_OUT ** -0.5),
        'moe_router_w': nrm(ks[28], (N_ODD, D, N_EXPERTS), D ** -0.5),
        'moe_router_b': nrm(ks[29], (N_ODD, N_EXPERTS), 0.01),
        'moe_w_gate': nrm(ks[30], (N_ODD, N_EXPERTS, D, D_FF_EXPERT), D ** -0.5),
        'moe_w_up': nrm(ks[31], (N_ODD, N_EXPERTS, D, D_FF_EXPERT), D ** -0.5),
        'moe_w_down': nrm(ks[32], (N_ODD, N_EXPERTS, D_FF_EXPERT, D), D_FF_EXPERT ** -0.5),
    }

def second_block(x, c, rel_bias, ada_w, ada_b, norm_mix_w, norm_ffn_w, final_norm_w,
              ab_w_in, attn_sinks, dn_conv_w, dn_a_log, dn_dt_bias, dn_norm_w, ab_w_out,
              ffn_w_gate, ffn_w_up, ffn_w_down,
              cd_w_in, lru_conv_w, lru_conv_b, lru_gate_a_w, lru_gate_a_b, lru_gate_x_w, lru_gate_x_b,
              lru_lambda, sconv_w, cd_w_out, moe_router_w, moe_router_b, moe_w_gate, moe_w_up, moe_w_down):
    cond = jax.nn.silu(c)
    for l in range(DEPTH_2):
        sh1, sc1, g1, sh2, sc2, g2 = jnp.split(cond @ ada_w[l] + ada_b[l], 6, axis=-1)
        hn = rmsnorm(x, norm_mix_w[l]) * (1.0 + sc1[:, None]) + sh1[:, None]
        if l % 2 == 0:
            e = l // 2
            mix = mixer_ab(hn, ab_w_in[e], attn_sinks[e], dn_conv_w[e], dn_a_log[e], dn_dt_bias[e],
                           dn_norm_w[e], ab_w_out[e], rel_bias)
        else:
            o = l // 2
            mix = mixer_cd(hn, cd_w_in[o], lru_conv_w[o], lru_conv_b[o], lru_gate_a_w[o], lru_gate_a_b[o],
                           lru_gate_x_w[o], lru_gate_x_b[o], lru_lambda[o], sconv_w[o], cd_w_out[o])
        x = x + g1[:, None] * mix
        hn = rmsnorm(x, norm_ffn_w[l]) * (1.0 + sc2[:, None]) + sh2[:, None]
        if l % 2 == 0:
            e = l // 2
            ffn = swiglu(hn, ffn_w_gate[e], ffn_w_up[e], ffn_w_down[e])
        else:
            o = l // 2
            ffn = moe_swiglu(hn, moe_router_w[o], moe_router_b[o], moe_w_gate[o], moe_w_up[o], moe_w_down[o])
        x = x + g2[:, None] * ffn
    return rmsnorm(x, final_norm_w)


def setup_inputs(seed=0):
    out = dict(first_inputs(seed))
    for name, value in second_inputs(seed + 1).items():
        if name != "x":
            out[name + "_2"] = value
    return out


def reference(
    x, c, w_ada, b_ada, norm1_w, norm2_w, w_in, conv_w, conv_b, dt_bias, a_log, d_skip,
    ssd_norm_w, w_ssd_out, q_norm_w, k_norm_w, w_attn_out, w_pool_mix, pool_scale, w_pool_out,
    w_out, w_ff1, w_ff2, c_2, rel_bias_2, ada_w_2, ada_b_2, norm_mix_w_2, norm_ffn_w_2,
    final_norm_w_2, ab_w_in_2, attn_sinks_2, dn_conv_w_2, dn_a_log_2, dn_dt_bias_2, dn_norm_w_2,
    ab_w_out_2, ffn_w_gate_2, ffn_w_up_2, ffn_w_down_2, cd_w_in_2, lru_conv_w_2, lru_conv_b_2,
    lru_gate_a_w_2, lru_gate_a_b_2, lru_gate_x_w_2, lru_gate_x_b_2, lru_lambda_2, sconv_w_2,
    cd_w_out_2, moe_router_w_2, moe_router_b_2, moe_w_gate_2, moe_w_up_2, moe_w_down_2,
):
    x = first_block(
        x, c, w_ada, b_ada, norm1_w, norm2_w, w_in, conv_w, conv_b, dt_bias, a_log, d_skip,
        ssd_norm_w, w_ssd_out, q_norm_w, k_norm_w, w_attn_out, w_pool_mix, pool_scale,
        w_pool_out, w_out, w_ff1, w_ff2,
    )
    return second_block(
        x, c_2, rel_bias_2, ada_w_2, ada_b_2, norm_mix_w_2, norm_ffn_w_2, final_norm_w_2,
        ab_w_in_2, attn_sinks_2, dn_conv_w_2, dn_a_log_2, dn_dt_bias_2, dn_norm_w_2, ab_w_out_2,
        ffn_w_gate_2, ffn_w_up_2, ffn_w_down_2, cd_w_in_2, lru_conv_w_2, lru_conv_b_2,
        lru_gate_a_w_2, lru_gate_a_b_2, lru_gate_x_w_2, lru_gate_x_b_2, lru_lambda_2, sconv_w_2,
        cd_w_out_2, moe_router_w_2, moe_router_b_2, moe_w_gate_2, moe_w_up_2, moe_w_down_2,
    )


_drawn_inputs = setup_inputs


def setup_inputs(seed=0):
    import zlib

    import numpy as np

    out = dict(_drawn_inputs(seed))
    spreads = {}
    factors = {'conv_b': 8.0,
     'd_skip': 6.009,
     'ssd_norm_w': 3.493,
     'q_norm_w': 7.292,
     'k_norm_w': 6.938,
     'pool_scale': 3.257,
     'rel_bias_2': 3.86,
     'norm_mix_w_2': 5.2,
     'norm_ffn_w_2': 6.277,
     'final_norm_w_2': 25.036,
     'attn_sinks_2': 48.611,
     'dn_norm_w_2': 8.0,
     'lru_conv_b_2': 39.894,
     'lru_gate_a_b_2': 200.0,
     'lru_gate_x_b_2': 64.0,
     'moe_router_b_2': 28.536}
    for name, (base, spread) in spreads.items():
        noise = np.random.default_rng([zlib.crc32(name.encode()), seed]).standard_normal(out[name].shape)
        drawn = base * np.exp(spread * noise) if base else spread * noise
        out[name] = jnp.asarray(drawn.astype(out[name].dtype))
    for name, factor in factors.items():
        out[name] = (out[name] * factor).astype(out[name].dtype)
    return out
```

```python
import math
from contextlib import ExitStack

import numpy as np

import concourse.bass as bass
from concourse import mybir

P = 128
F32 = mybir.dt.float32
ACT = mybir.ActivationFunctionType
ALU = mybir.AluOpType
AX = mybir.AxisListType

D = 1024
S = 256
KT = D // P
TT = S // P
NEG = -1.0e30
EPS = 1e-6

HEADS = 12
DILATIONS = (1, 4, 16)
SPANS = (128, 128, 128)
POOL_WINDOWS = (2, 4, 8, 16)
LEVELS = (1, 2, 4, 8, 16, 32)
F_EXPERT = 3584
EXPERTS = 8
ROUNDS = TT * EXPERTS


def alibi_slopes(n):
    def pow2(k):
        start = 2.0 ** (-8.0 / k)
        return [start ** (i + 1) for i in range(k)]
    if math.log2(n).is_integer():
        s = pow2(n)
    else:
        c = 2 ** math.floor(math.log2(n))
        s = pow2(c) + pow2(2 * c)[0::2][: n - c]
    return np.sort(np.asarray(s, np.float32))[::-1].copy()


def constant_columns():
    k = np.arange(P)[:, None]
    m = np.arange(P)[None, :]
    block = (k // 64) == (m // 64)
    parts = {
        "ident": (k == m),
        "ones": np.ones((P, P)),
        "until": (k <= m),
        "after": (k > m),
        "until64": (k <= m) & block,
        "after64": (k > m) & block,
        "block64": block,
        "causal_neg": np.where(k <= m, 0.0, NEG),
        "causal64_neg": np.where((k <= m) & block, 0.0, NEG),
        "eps": np.full((P, 1), EPS),
        "eight_down": np.tile(8.0 - np.arange(8), (P, 1)),
        "slot_number": np.tile(np.arange(P) * 1.0, (P, 1)),
    }
    for w in LEVELS:
        parts[f"level{w}"] = ((k // (2 * w)) == (m // (2 * w))) & (m % (2 * w) >= w) & (k % (2 * w) < w)
    for g, w in enumerate(POOL_WINDOWS):
        lag = m - k
        parts[f"pool_first{g}"] = ((lag >= 0) & (lag < w)) / np.minimum(m + 1.0, w) - (lag == 0)
        parts[f"pool_same{g}"] = ((lag >= 0) & (lag < w)) / float(w) - (lag == 0)
        parts[f"pool_prev{g}"] = ((lag + P >= 0) & (lag + P < w)) / float(w)
    for t in range(TT):
        for g, (dil, span) in enumerate(zip(DILATIONS, SPANS)):
            s = np.arange((t + 1) * P)[None, :]
            dist = (t * P + k) - s
            seen = (dist >= 0) & (dist % dil == 0) & (dist // dil <= span)
            parts[f"dist{t}{g}"] = np.where(seen, dist, -NEG)
    dist = 255 - np.arange(383)
    large = 16 + (np.log(np.maximum(dist, 1) / 16) / math.log(128 / 16) * 16).astype(np.int32)
    bucket = np.where(dist < 16, np.maximum(dist, 0), np.minimum(large, 31))
    seen = (dist >= 0) & (dist < 128)
    line = np.zeros((P, 383))
    line[:32] = (bucket[None, :] == np.arange(32)[:, None]) & seen[None, :]
    line[32] = ~seen
    parts["bucket_line"] = line
    at, cols, n = {}, [], 0
    for name, a in parts.items():
        a = np.asarray(a, np.float32)
        at[name] = (n, a.shape[1])
        n += a.shape[1]
        cols.append(a)
    return np.ascontiguousarray(np.concatenate(cols, 1)), at


def row_plan():
    tiles = [
        [("norm1_w", 8), ("norm2_w", 8), ("conv_w", 48), ("conv_b", 12), ("ssd_norm_w", 8),
         ("q_norm_w", 1), ("k_norm_w", 1), ("pool_scale", 8)],
        [("norm_mix_w_2", 16), ("norm_ffn_w_2", 16), ("dn_conv_w_2", 48), ("lru_conv_w_2", 32)],
        [("lru_conv_b_2", 8), ("lru_gate_a_b_2", 8), ("lru_gate_x_b_2", 8), ("lru_lambda_2", 8),
         ("sconv_w_2", 12), ("dn_norm_w_2", 1), ("c", 8), ("c_2", 8)],
    ]
    at = {}
    for i, t in enumerate(tiles):
        r = 0
        for name, n in t:
            at[name] = (i, r, n)
            r += n
        assert r <= P
    return at, [sum(n for _, n in t) for t in tiles]


RING = 3
SLOT = 4096


class Plan:

    def __init__(self):
        self.chunks = []
        self.stage = {}
        self.steps = 0

    def add(self, name, chunks):
        self.stage[name] = (len(self.chunks), self.steps)
        for pieces, kt, n, steps in chunks:
            self.steps += steps
            self.chunks.append((pieces, kt, n, self.steps))


def rows_of(w, r0, kt, c0, n):
    return w[r0:r0 + kt * P, c0:c0 + n].rearrange("(k p) n -> p k n", p=P)


def make_plan(w):
    plan = Plan()

    def wide(name, a, c0, n, per):
        out = []
        for c in range(0, n, 512):
            m = min(512, n - c)
            out.append(([(0, rows_of(a, 0, KT, c0 + c, m))], KT, m, per(m)))
        plan.add(name, out)

    def down(name, a, rows):
        out = []
        for r in range(0, rows, 512):
            kt = min(4, (rows - r) // P)
            out.append(([(0, rows_of(a, r, kt, 0, D))], kt, D, 1))
        plan.add(name, out)

    tok = lambda m: TT
    feat = lambda m: (m // P + 1) // 2
    w_in = w["w_in"][0]
    wide("q", w_in, 2576, 1536, feat)
    wide("k", w_in, 4112, 1536, feat)
    wide("v", w_in, 5648, 1536, tok)
    wide("gate_attn", w_in, 8208 + 1024, 1024, tok)
    down("attn_out", w["w_attn_out"][0], 512)
    wide("u", w_in, 7184, 1024, tok)
    plan.add("pool_mix", [([(0, w["w_pool_mix"][0].rearrange("g (k p) o -> p (g k) o", p=P))], 8, 256, 4)])
    wide("gate_pool", w_in, 8208 + 2048, 1024, tok)
    down("pool_out", w["w_pool_out"][0], 1024)
    wide("xbc", w_in, 1024, 1536, feat)
    wide("dt", w_in, 2560, 16, tok)
    wide("z", w_in, 0, 1024, tok)
    wide("gate_ssd", w_in, 8208, 1024, tok)
    down("ssd_out", w["w_ssd_out"][0], 1024)
    down("mix_out", w["w_out"][0], 1024)
    wide("ff1", w["w_ff1"][0], 0, 4096, feat)
    down("ff2", w["w_ff2"][0], 4096)

    ab = w["ab_w_in_2"][0]
    wide("qa", ab, 0, 512, feat)
    wide("kva", ab, 512, 256, lambda m: 3)
    wide("qkv_b", ab, 768, 1536, feat)
    wide("gate_b", ab, 2304, 512, tok)
    wide("ba", ab, 2816, 16, tok)
    down("ab_out", w["ab_w_out_2"][0], 1024)
    gate, up = w["ffn_w_gate_2"][0], w["ffn_w_up_2"][0]
    both = []
    for c in range(0, 2816, 512):
        m = min(512, 2816 - c)
        both += [([(0, rows_of(a, 0, KT, c, m))], KT, m, feat(m)) for a in (gate, up)]
    plan.add("ffn", both)
    down("ffn_down", w["ffn_w_down_2"][0], 2816)
    wide("cd_in", w["cd_w_in_2"][0], 0, 3584, feat)
    plan.add("lru_gates", [([(0, w["lru_gate_a_w_2"][0].rearrange("n i j -> i n j")),
                             (8 * P, w["lru_gate_x_w_2"][0].rearrange("n i j -> i n j"))], 16, P, 8)])
    down("cd_out", w["cd_w_out_2"][0], 1536)
    return plan


def alloc_views(arena):
    def at(off, *shape):
        n = int(np.prod(shape))
        v = arena[:, off:off + n]
        if len(shape) == 2:
            v = v.rearrange("p (a b) -> p a b", b=shape[1])
        if len(shape) == 3:
            v = v.rearrange("p (a b c) -> p a b c", b=shape[1], c=shape[2])
        return v
    return at


class Lane:

    def __init__(self, eng, step):
        self.eng, self.step, self.count, self.last = eng, step, {}, None

    def __call__(self, ins, sem=None):
        sem = sem or self.step
        ins.then_inc(sem, 1)
        self.count[sem.name] = self.count.get(sem.name, 0) + 1
        self.last = (sem, self.count[sem.name])

    def settle(self):
        self.eng.wait_ge(*self.last)


QT, KTT, VT = 4096, 7168, 10240
QSQ, QRS = 13312, 14336
AS_, AP_, APT, AOT = 13312, 14848, 16384, 17920
PU, PP, PM = 4096, 6144, 8192
SRAW, SX, SZ, SXC, SXX, SXD, SB, SST, SCB = 4096, 7204, 10276, 12324, 14372, 16420, 17444, 17700, 18724
SE = SRAW
FH, FT = 2048, 10240
EG, EH, ES, ET, ESEL, EGATED, ETURN, EY, MO = 2048, 3072, 4096, 5120, 8704, 8960, 9216, 9472, 12288
DOUT, DQKV, DGS = 0, 2048, 5120
WQ, WK, WV, WRAW, T5_OFF, WS, WPT = 6144, 7168, 7680, 7936, 11044, 13092, 14116
DVB, DKBG, DKDEC, DEGB, DQK, DLT, DT, DTT = 6144, 7168, 8192, 9216, 11264, 13312, 15360, 17408
DLM, DU = DQKV + 1024, DQKV + 2048
DUU, DWT, DQD, DST, DVN, DO = DLT, DLT + 1024, DQKV, DT + 1024, DT + 1280, DLM
LOUT, LRAW, LX, LY, LB, LR, LI, LA = 0, 3072, 5144, 7192, 9240, 12312, 14360, 16408
LH = LB
ARENA = 19456
SG, SBETA, SGC, SEG = 224, 240, 256, 272

UNITS = 6
SLAB = 3072


def build(nc, w, consts_dram, const_at, out, scratch, upto=99):
    with ExitStack() as ctx:
        def sb(name, *shape):
            return ctx.enter_context(nc.sbuf_tensor(name, [P, *shape], F32))

        sems = {}

        def sem(name):
            if name not in sems:
                sems[name] = ctx.enter_context(nc.semaphore(name))
            return sems[name]

        n_const = sum(n for _, n in const_at.values())
        consts = sb("consts", n_const)
        ring = sb("ring", RING, SLOT)
        x = sb("x", TT, D)
        hT = sb("hT", KT, S)
        slab = sb("slab", 2, SLAB)
        ada = sb("ada", SLAB)
        gain = sb("gain", D)
        shift = sb("shift", 2 * KT)
        row_at, row_n = row_plan()
        cols = sb("cols", len(row_n), P)
        spread = sb("spread", 128)
        router = sb("router", KT, EXPERTS)
        small = sb("small", 640)
        rounds = ctx.enter_context(nc.sbuf_tensor("rounds", [P, 2], mybir.dt.int32))
        routes = sb("routes", 2, TT, ROUNDS + 1)
        arena_t = sb("arena", ARENA)
        ps = ctx.enter_context(nc.psum_tensor("ps", [P, 8, 512], F32))
        A = alloc_views(arena_t)

        def con(name):
            o, n = const_at[name]
            return consts[:, o:o + n]

        def col(name, i=0, n=1):
            t, r, m = row_at[name]
            assert i + n <= m
            return cols[:, t, r + i:r + i + n]

        ident, ones = con("ident"), con("ones")
        plan = make_plan(w)
        slopes = alibi_slopes(HEADS)

        SPREAD = {"dt_bias": (0, 16), "a_log": (16, 16), "d_skip": (32, 16), "attn_sinks_2": (48, 8),
                  "dn_a_log_2": (56, 8), "dn_dt_bias_2": (64, 8), "moe_router_b_2": (72, 8)}

        def spr(name):
            o, n = SPREAD[name]
            return spread[:, o:o + n]

        lin_done = sem("lin_done")
        w_landed = [sem(f"w_landed{s}") for s in range(RING)]
        stage_end = sem("stage_end")
        params_in = sem("params_in")
        rows_in = sem("rows_in")
        x_in = sem("x_in")
        out_written = sem("out_written")

        def lin0(name):
            return plan.stage[name][1]

        block = ctx.enter_context(nc.Block())
        N_BAR = 3

        def barrier_of(eng):
            n = [0]

            def barrier():
                n[0] += 1
                eng.drain().then_inc(stage_end, 1)
                eng.wait_ge(stage_end, N_BAR * n[0])
            return barrier

        GU = F_EXPERT // 512
        E_CHUNKS = 3 * GU
        def e_slot(c):
            return (len(plan.chunks) + c) % RING

        moe_gate, moe_up, moe_down = w["moe_w_gate_2"][0], w["moe_w_up_2"][0], w["moe_w_down_2"][0]

        @block.sync
        def _(sp):
            for name, (t, r, n) in row_at.items():
                if name == "dn_norm_w_2":
                    for h in range(2):
                        sp.dma_start(A(0, 3, P)[r:r + 1, t, 64 * h:64 * h + 64], w[name]).then_inc(rows_in, 16)
                    continue
                src = w[name].flatten().rearrange("(r p) -> r p", p=P)
                sp.dma_start(A(0, 3, P)[r:r + n, t, :], src).then_inc(rows_in, 16)
            sp.dma_start(consts[:], consts_dram).then_inc(params_in, 16)
            for t in range(TT):
                sp.dma_start(x[:, t, :], w["x"][0, t * P:(t + 1) * P, :]).then_inc(x_in, 16)
            for name in SPREAD:
                sp.dma_start(spr(name), w[name].broadcast_to([P, SPREAD[name][1]])).then_inc(params_in, 16)
            sp.dma_start(router[:], w["moe_router_w_2"][0].rearrange("(k p) e -> p k e", p=P)).then_inc(params_in, 16)
            sp.dma_start(A(500, 8)[0:32, :], w["rel_bias_2"]).then_inc(rows_in, 16)
            for i, (pieces, kt, n, _) in enumerate(plan.chunks[:None if upto > 11 else [0, 0, 9, 9, 19, 29, 47, 54, 54, 56, 74, 85][upto]]):
                if i >= RING:
                    sp.wait_ge(lin_done, plan.chunks[i - RING][3])
                for off, src in pieces:
                    m = src.shape[1] * src.shape[2]
                    dst = ring[:, i % RING, off:off + m].rearrange("p (k n) -> p k n", n=src.shape[2])
                    sp.dma_start(dst, src).then_inc(w_landed[i % RING], 16)

            down_rows = moe_down.rearrange("e f d -> (e f) d")

            def expert_chunk(e, c):
                if c < 2 * GU:
                    a = (moe_gate, moe_up)[c % 2]
                    src = a[e, :, (c // 2) * 512:(c // 2 + 1) * 512].rearrange("(k p) n -> p k n", p=P)
                else:
                    src = down_rows[bass.ds(e * F_EXPERT + (c - 2 * GU) * 512, 512), :].rearrange("(k p) n -> p k n", p=P)
                dst = ring[:, e_slot(c), :].rearrange("p (k n) -> p k n", n=src.shape[2])
                sp.dma_start(dst, src).then_inc(w_landed[e_slot(c)], 16)

            if upto < 12:
                return
            def expert_weights(first, e):
                for c in range(E_CHUNKS):
                    sp.wait_ge(lin_done, e * E_CHUNKS + (plan.steps + first * E_CHUNKS + c - RING + 1))
                    expert_chunk(e, c)

            with sp.Fori(0, EXPERTS) as e:
                expert_weights(0, e)
            sp.wait_ge(sem("routing"), 3)
            more = sp.value_load(rounds[0:1, 1:2], min_val=0, max_val=EXPERTS)
            with sp.If(more > 0):
                with sp.Fori(0, EXPERTS) as e:
                    expert_weights(EXPERTS, e)
            sp.end_ifs()
            sp.wait_ge(sem("final_scaled"), TT)
            for t in range(TT):
                sp.dma_start(out[0, t * P:(t + 1) * P, :], A(0, TT, D)[:, t, :]).then_inc(out_written, 16)
            sp.wait_ge(out_written, 16 * TT)

        landed_at = []
        uses = [0] * RING
        for i, (pieces, *_) in enumerate(plan.chunks):
            uses[i % RING] += len(pieces)
            landed_at.append(16 * uses[i % RING])
        N_ROWS = 16 * (len(row_at) + 2)
        N_PARAMS = 16 * (2 + len(SPREAD))

        ada_w = [w["w_ada"][0], w["ada_w_2"][0], w["ada_w_2"][1]]
        ada_b = [w["b_ada"][0], w["ada_b_2"][0], w["ada_b_2"][1]]

        @block.gpsimd
        def _(pool):
            pool.wait_ge(params_in, N_PARAMS)
            pool.wait_ge(sem("bias_line"), 8)
            pool.dma_start(scratch[:, :, 0:383], A(8192, 8, 383)).then_inc(sem("line_out"), 16)
            for u in range(UNITS if upto > 11 else [1, 1, 2, 2, 2, 2, 3, 4, 4, 4, 5, 6][upto]):
                pool.wait_ge(sem("ada_clear"), u + 1)
                src = ada_b[u // 2][(u % 2) * SLAB:(u % 2 + 1) * SLAB]
                pool.dma_start(ada[0:1, :], src.rearrange("(a n) -> a n", a=1)).then_inc(sem("ada_bias"), 16)
                for k in range(KT):
                    i = u * KT + k
                    if i >= 2:
                        pool.wait_ge(sem("slab_used"), i - 1)
                    pool.dma_start(slab[:, i % 2, :], ada_w[u // 2][k * P:(k + 1) * P, (u % 2) * SLAB:(u % 2 + 1) * SLAB]
                                   ).then_inc(sem(f"slab_in{i % 2}"), 16)
                if u == 2 and upto > 6:
                    pool.wait_ge(sem("line_out"), 16)
                    pool.wait_ge(sem("bias_wanted"), 1)
                    skew = bass.AP(tensor=scratch.tensor, offset=127, ap=[[8 * 384 - 1, P], [384, 8], [1, 256]])
                    pool.dma_start(A(T5_OFF, 8, 256), skew).then_inc(sem("bias_in"), 16)

        @block.tensor
        def _(pe):
            barrier = barrier_of(pe)

            def weights(name, c):
                i = plan.stage[name][0] + c
                pieces, kt, n, _ = plan.chunks[i]
                pe.wait_ge(w_landed[i % RING], landed_at[i])
                return ring[:, i % RING, 0:kt * n].rearrange("p (k n) -> p k n", n=n)

            def token_product(name, evacuated, lhs=hT, g0=0):
                g = g0
                n_chunks = {"v": 3, "gate_attn": 2, "u": 2, "gate_pool": 2, "dt": 1, "z": 2, "gate_ssd": 2,
                            "gate_b": 1, "ba": 1}[name]
                for c in range(n_chunks):
                    wt = weights(name, c)
                    n = wt.shape[2]
                    for t in range(TT):
                        if g >= 4:
                            pe.wait_ge(evacuated, g - 3)
                        for k in range(KT):
                            mm = pe.matmul(ps[:, g % 4, 0:n], lhs[:, k, t * P:(t + 1) * P], wt[:, k, :],
                                           start=(k == 0), stop=(k == KT - 1))
                        mm.then_inc(lin_done, 1)
                        g += 1

            def feature_pair(wt, j, bank, rhs=hT, last=True):
                tiles = min(2, wt.shape[2] // P - 2 * j)
                for i in range(tiles):
                    for k in range(KT):
                        mm = pe.matmul(ps[:, bank, i * S:(i + 1) * S], wt[:, k, (2 * j + i) * P:(2 * j + i + 1) * P],
                                       rhs[:, k, :], start=(k == 0), stop=(k == KT - 1))
                mm.then_inc(lin_done, 1)

            def down_product(name, n_chunks, lhs):
                total = sum(plan.chunks[plan.stage[name][0] + c][1] for c in range(n_chunks))
                k0 = 0
                for c in range(n_chunks):
                    wt = weights(name, c)
                    for t in range(TT):
                        for h in range(2):
                            for k in range(wt.shape[1]):
                                mm = pe.matmul(ps[:, 4 + 2 * t + h, :], lhs(k0 + k, t), wt[:, k, h * 512:(h + 1) * 512],
                                               start=(k0 + k == 0), stop=(k0 + k == total - 1))
                    mm.then_inc(lin_done, 1)
                    k0 += wt.shape[1]

            def modulation(u):
                pe.wait_ge(sem("ada_ready"), u + 1)
                for j in range(2 * KT):
                    pe.matmul(ps[:, 4, j:j + 1], ada[:, j * P:(j + 1) * P], ones[:, 0:1], start=True, stop=True)
                for h in range(2):
                    mm = pe.matmul(ps[:, 5 + h, :], ones, ada[:, 2 * D + h * 512:2 * D + (h + 1) * 512],
                                   start=True, stop=True)
                mm.then_inc(sem("mod_summed"), 1)

            def turn_all(src, sem_in, n_in, sem_out):
                pe.wait_ge(sem_in, n_in)
                for k in range(KT):
                    for t in range(TT):
                        mm = pe.transpose(ps[:, 4 + k // 2, (k % 2) * S + t * P:(k % 2) * S + (t + 1) * P],
                                          src[:, t, k * P:(k + 1) * P], ident)
                mm.then_inc(sem_out, 1)

            pe.wait_ge(rows_in, N_ROWS)
            pe.wait_ge(params_in, N_PARAMS)
            for i, n in enumerate(row_n):
                mm = pe.transpose(ps[:, 0, i * P:i * P + n], A(0, 3, P)[0:n, i, :], ident[0:n, 0:n])
            mm.then_inc(sem("line_mm"), 1)
            pe.wait_ge(sem("line_lhs"), 1)
            for h in range(8):
                if h >= 2:
                    pe.wait_ge(sem("bias_line"), h - 1)
                pe.matmul(ps[:, 2 + h % 2, 0:383], A(1024, 8, P)[0:33, h, :], con("bucket_line")[0:33, :],
                          start=True, stop=True).then_inc(sem("line_mm"), 1)
            modulation(0)
            barrier()
            if upto < 1:
                return
            turn_all(A(0, TT, D), sem("x_scaled"), TT, sem("h_turned"))
            barrier()

            if upto < 2:
                return
            g = 0
            for name in ("q", "k"):
                for c in range(3):
                    wt = weights(name, c)
                    for j in range(2):
                        if g >= 4:
                            pe.wait_ge(sem("qk_raw"), g - 3)
                        feature_pair(wt, j, g % 4)
                        if g >= 1:
                            pe.wait_ge(sem("qk_raw"), g)
                            if g >= 3:
                                pe.wait_ge(sem("qk_rstd"), g - 2)
                            pe.matmul(ps[:, 4 + (g - 1) % 2, :], ones, A(QSQ, 2, 512)[:, (g - 1) % 2, :],
                                      start=True, stop=True).then_inc(sem("qk_ss"), 1)
                        g += 1
            pe.wait_ge(sem("qk_raw"), g)
            pe.wait_ge(sem("qk_rstd"), g - 2)
            pe.matmul(ps[:, 4 + (g - 1) % 2, :], ones, A(QSQ, 2, 512)[:, (g - 1) % 2, :],
                      start=True, stop=True).then_inc(sem("qk_ss"), 1)
            token_product("v", sem("v_out"))
            barrier()

            if upto < 3:
                return
            qT, kT, v = A(QT, HEADS, S), A(KTT, HEADS, S), A(VT, TT, HEADS * P)

            def attn_scores(i):
                j, t = i // 2, i % 2
                n = (t + 1) * P
                if i >= 2:
                    pe.wait_ge(sem("at_masked"), i - 1)
                for g in range(3):
                    h = 4 * g + j
                    if t == 0:
                        o = ps[:, 2 * (i % 2), g * P:(g + 1) * P]
                    else:
                        o = ps[:, 2 * (i % 2) + g // 2, (g % 2) * S:(g % 2 + 1) * S]
                    mm = pe.matmul(o, qT[:, h, t * P:(t + 1) * P], kT[:, h, 0:n], start=True, stop=True)
                mm.then_inc(sem("at_scores"), 1)

            def attn_apply(i):
                j, t = i // 2, i % 2
                n = 3 * (t + 1)
                pe.wait_ge(sem("at_probs"), i + 1)
                if i >= 1:
                    pe.wait_ge(sem("at_turned"), i)
                for b in range(n):
                    mm = pe.transpose(ps[:, 4 + b // 4, (b % 4) * P:(b % 4 + 1) * P],
                                      A(AP_, 2, 768)[:, i % 2, b * P:(b + 1) * P], ident)
                mm.then_inc(sem("at_pT"), 1)
                pe.wait_ge(sem("at_turned"), i + 1)
                if i >= 2:
                    pe.wait_ge(sem("at_out"), i - 1)
                b = 0
                for g in range(3):
                    for s in range(t + 1):
                        mm = pe.matmul(ps[:, 6 + i % 2, 0:P], v[:, s, (4 * g + j) * P:(4 * g + j + 1) * P],
                                       A(APT, 2, 768)[:, i % 2, b * P:(b + 1) * P], start=(b == 0), stop=(b == n - 1))
                        b += 1
                mm.then_inc(sem("at_pv"), 1)

            attn_scores(0)
            for i in range(8):
                if i < 7:
                    attn_scores(i + 1)
                attn_apply(i)
            barrier()

            if upto < 4:
                return
            oT = A(AOT, 4, S)
            token_product("gate_attn", sem("ga_out"))
            down_product("attn_out", 1, lambda k, t: oT[:, k, t * P:(t + 1) * P])
            barrier()

            token_product("u", sem("u_out"))
            pe.wait_ge(sem("u_out"), 4)
            u = A(PU, TT, D)
            for c in range(KT):
                g, bank, o = c // 2, 4 + c // 2, (c % 2) * S
                pe.matmul(ps[:, bank, o:o + P], u[:, 0, c * P:(c + 1) * P], con(f"pool_first{g}"), start=True, stop=True)
                pe.matmul(ps[:, bank, o + P:o + S], u[:, 0, c * P:(c + 1) * P], con(f"pool_prev{g}"),
                          start=True, stop=False)
                mm = pe.matmul(ps[:, bank, o + P:o + S], u[:, 1, c * P:(c + 1) * P], con(f"pool_same{g}"),
                               start=False, stop=True)
                if c % 2:
                    mm.then_inc(sem("pooled"), 1)
            wt = weights("pool_mix", 0)
            pT = A(PP, KT, S)
            for g in range(4):
                pe.wait_ge(sem("pooled_out"), g + 1)
                for o in range(2):
                    for k in range(2):
                        mm = pe.matmul(ps[:, g, o * S:(o + 1) * S], wt[:, 2 * g + k, o * P:(o + 1) * P],
                                       pT[:, 2 * g + k, :], start=(k == 0), stop=(k == 1))
                mm.then_inc(lin_done, 1)
            pe.wait_ge(sem("pool_mixed"), 4)
            token_product("gate_pool", sem("gp_out"))
            mT = A(PM, KT, S)
            down_product("pool_out", 2, lambda k, t: mT[:, k, t * P:(t + 1) * P])
            barrier()

            if upto < 5:
                return
            for g in range(6):
                if g % 2 == 0:
                    wt = weights("xbc", g // 2)
                if g >= 4:
                    pe.wait_ge(sem("xbc_out"), g - 3)
                feature_pair(wt, g % 2, g % 4)
            pe.wait_ge(sem("xbc_out"), 6)
            token_product("dt", None)
            pe.wait_ge(sem("dt_out"), 2)
            token_product("z", sem("z_out"))
            pe.wait_ge(sem("dtA"), 1)
            dtA = small[:, 32:64].rearrange("p (t h) -> p t h", t=2)
            pe.matmul(ps[:, 4, 0:32], con("until"), small[:, 32:64], start=True, stop=True)
            pe.matmul(ps[:, 4, 32:48], con("after"), dtA[:, 0, :], start=True, stop=True).then_inc(sem("acum_mm"), 1)
            barrier()
            xbcT = A(SX, 12, S)
            for t in range(TT):
                for c in range(KT):
                    mm = pe.transpose(ps[:, 4 + 2 * t + c // 4, (c % 4) * P:(c % 4 + 1) * P],
                                      xbcT[:, c, t * P:(t + 1) * P], ident)
            mm.then_inc(sem("xs_turned"), 1)
            for g in range(2):
                pe.transpose(ps[:, 0, g * P:(g + 1) * P], xbcT[:, 8 + g, 0:P], ident)
            for t in range(TT):
                for g in range(2):
                    mm = pe.matmul(ps[:, 1, (2 * t + g) * P:(2 * t + g + 1) * P], xbcT[:, 8 + g, t * P:(t + 1) * P],
                                   xbcT[:, 10 + g, t * P:(t + 1) * P], start=True, stop=True)
            mm.then_inc(sem("cb_mm"), 1)
            pe.wait_ge(sem("ssd_inputs"), 1)
            for g in range(2):
                mm = pe.matmul(ps[:, g, :], A(SB, 2, P)[:, g, :], A(SXD, D)[:, g * 512:(g + 1) * 512],
                               start=True, stop=True)
            mm.then_inc(sem("state_mm"), 1)
            pe.wait_ge(sem("state_out"), 1)
            for g in range(2):
                mm = pe.matmul(ps[:, g, :], xbcT[:, 10 + g, P:S], A(SST, 2, 512)[:, g, :], start=True, stop=True)
            mm.then_inc(sem("yoff_mm"), 1)

            def ssd_spread(b):
                t, hb = b // 4, b % 4
                if b >= 2:
                    pe.wait_ge(sem("seg_out"), b - 1)
                for j in range(4):
                    h = 4 * hb + j
                    mm = pe.matmul(ps[:, 2 + b % 2, j * P:(j + 1) * P], dtA[:, t, h:h + 1].broadcast_to([P, P]),
                                   con("until"), start=True, stop=True)
                mm.then_inc(sem("seg_mm"), 1)

            ssd_spread(0)
            for b in range(8):
                if b < 7:
                    ssd_spread(b + 1)
                pe.wait_ge(sem("decay_cb"), b + 1)
                t, hb = b // 4, b % 4
                for j in range(4):
                    h = 4 * hb + j
                    mm = pe.matmul(ps[:, 4 + 2 * t + h // 8, (h % 8) * 64:(h % 8 + 1) * 64],
                                   A(SE, 2, 512)[:, b % 2, j * P:(j + 1) * P],
                                   A(SXX, TT, D)[:, t, h * 64:(h + 1) * 64], start=True, stop=True)
                mm.then_inc(sem("ydiag_mm"), 1)
            barrier()
            turn_all(A(SRAW, TT, D), sem("y_normed"), 1, sem("y_turned"))
            pe.wait_ge(sem("yT_out"), 1)
            token_product("gate_ssd", sem("gs_out"))
            yT = A(SX, KT, S)
            down_product("ssd_out", 2, lambda k, t: yT[:, k, t * P:(t + 1) * P])
            barrier()

            if upto < 6:
                return
            turn_all(A(0, TT, D), sem("mix_done"), 1, sem("mix_turned"))
            pe.wait_ge(sem("mixT_out"), 1)
            mixT = A(2048, KT, S)
            down_product("mix_out", 2, lambda k, t: mixT[:, k, t * P:(t + 1) * P])
            barrier()
            modulation(1)
            barrier()
            turn_all(A(0, TT, D), sem("x_scaled"), 2 * TT, sem("h_turned"))
            barrier()
            for g in range(16):
                if g % 2 == 0:
                    wt = weights("ff1", g // 2)
                if g >= 4:
                    pe.wait_ge(sem("ff_relu"), g - 3)
                feature_pair(wt, g % 2, g % 4)
            pe.wait_ge(sem("ff_hidden"), 16)
            hid = A(FH, 32, S)
            down_product("ff2", 8, lambda k, t: hid[:, k, t * P:(t + 1) * P])
            barrier()
            modulation(2)
            barrier()
            if upto < 7:
                return

            turn_all(A(0, TT, D), sem("x_scaled"), 3 * TT, sem("h_turned"))
            barrier()
            wt = weights("qa", 0)
            for j in range(2):
                feature_pair(wt, j, j)
            wt = weights("kva", 0)
            for k in range(KT):
                mm = pe.matmul(ps[:, 2, 0:S], wt[:, k, 0:P], hT[:, k, :], start=(k == 0), stop=(k == KT - 1))
            mm.then_inc(lin_done, 1)
            for t in range(TT):
                for k in range(KT):
                    mm = pe.matmul(ps[:, 3, t * P:(t + 1) * P], hT[:, k, t * P:(t + 1) * P], wt[:, k, P:2 * P],
                                   start=(k == 0), stop=(k == KT - 1))
                mm.then_inc(lin_done, 1)
            for g in range(6):
                if g % 2 == 0:
                    wt = weights("qkv_b", g // 2)
                pe.wait_ge(sem("ab_out1"), g + 1)
                feature_pair(wt, g % 2, g % 4)
            wt = weights("gate_b", 0)
            for t in range(TT):
                for k in range(KT):
                    mm = pe.matmul(ps[:, 4 + t, :], hT[:, k, t * P:(t + 1) * P], wt[:, k, :],
                                   start=(k == 0), stop=(k == KT - 1))
                mm.then_inc(lin_done, 1)
            wt = weights("ba", 0)
            for t in range(TT):
                for k in range(KT):
                    mm = pe.matmul(ps[:, 6, 16 * t:16 * t + 16], hT[:, k, t * P:(t + 1) * P], wt[:, k, :],
                                   start=(k == 0), stop=(k == KT - 1))
                mm.then_inc(lin_done, 1)
            barrier()
            if upto < 8:
                return
            qaT, kdup, va = A(WQ, 4, S), A(WK, 2, S), A(WV, TT, P)
            for i in range(4):
                t, par = i // 2, i % 2
                n = (t + 1) * P
                lo = 64 * par
                if i >= 1:
                    pe.wait_ge(sem("wa_biased"), i)
                for a in range(4):
                    h = 2 * a + par
                    o = ps[:, 0, a * P:(a + 1) * P] if t == 0 else ps[:, a // 2, (a % 2) * S:(a % 2 + 1) * S]
                    mm = pe.matmul(o, qaT[lo:lo + 64, a, t * P:(t + 1) * P], kdup[lo:lo + 64, h // 4, 0:n],
                                   start=True, stop=True)
                mm.then_inc(sem("wa_scores"), 1)
                pe.wait_ge(sem("wa_probs"), i + 1)
                for b in range(4 * (t + 1)):
                    mm = pe.transpose(ps[:, 2 + b // 4, (b % 4) * P:(b % 4 + 1) * P],
                                      A(WS, 4 * S)[:, b * P:(b + 1) * P], ident)
                mm.then_inc(sem("wa_pT"), 1)
                pe.wait_ge(sem("wa_turned"), i + 1)
                for a in range(4):
                    h = 2 * a + par
                    for s in range(t + 1):
                        b = a * (t + 1) + s
                        mm = pe.matmul(ps[lo:lo + 64, 4, a * P:(a + 1) * P], va[:, s, (h // 4) * 64:(h // 4 + 1) * 64],
                                       A(WPT, 4 * S)[:, b * P:(b + 1) * P], start=(s == 0), stop=(s == t))
                mm.then_inc(sem("wa_pv"), 1)
                pe.wait_ge(sem("wa_out"), i + 1)
            for g in range(4):
                pe.wait_ge(sem("l2_sq"), g + 1)
                if g >= 2:
                    pe.wait_ge(sem("l2_rstd"), g - 1)
                pe.matmul(ps[:, 5 + g % 2, :], con("block64"), A(WS, 2, 512)[:, g % 2, :],
                          start=True, stop=True).then_inc(sem("l2_ss"), 1)
            barrier()
            if upto < 9:
                return
            qkvT = A(DQKV, 12, S)
            for t in range(TT):
                for c in range(8):
                    mm = pe.transpose(ps[:, 2 * t + c // 4, (c % 4) * P:(c % 4 + 1) * P],
                                      qkvT[:, 4 + c, t * P:(t + 1) * P], ident)
            mm.then_inc(sem("kv_turned"), 1)
            g16 = small[:, SG:SG + 16]
            pe.wait_ge(sem("dn_g"), 1)
            pe.matmul(ps[:, 4, 0:16], con("until64"), g16, start=True, stop=True)
            pe.matmul(ps[:, 4, 16:32], con("after64"), g16, start=True, stop=True).then_inc(sem("dn_gc"), 1)
            barrier()
            beta16 = small[:, SBETA:SBETA + 16]
            for b in range(4):
                t, par = b // 2, b % 2
                lo = 64 * par
                o = 4 * (b % 2)
                if b >= 2:
                    pe.wait_ge(sem("dn_lt"), b - 1)
                for a in range(4):
                    h = 2 * a + par
                    sl = slice(a * P, (a + 1) * P)
                    c = t * 8 + h
                    q_, k_ = qkvT[lo:lo + 64, a, t * P:(t + 1) * P], qkvT[lo:lo + 64, 4 + a, t * P:(t + 1) * P]
                    pe.matmul(ps[:, o, sl], g16[:, c:c + 1].broadcast_to([P, P]), con("until64"), start=True, stop=True)
                    pe.matmul(ps[:, o + 1, sl], beta16[:, c:c + 1].broadcast_to([P, P]), ident, start=True, stop=True)
                    pe.matmul(ps[:, o + 2, sl], k_, k_, start=True, stop=True)
                    mm = pe.matmul(ps[:, o + 3, sl], k_, q_, start=True, stop=True)
                mm.then_inc(sem("dn_mm"), 1)
            barrier()
            T, TTr = A(DT, 4, 512), A(DTT, 4, 512)
            for l in range(len(LEVELS)):
                for b in range(4):
                    n = 4 * l + b
                    pe.wait_ge(sem("dn_lm"), n + 1)
                    if n >= 4:
                        pe.wait_ge(sem("dn_T"), n - 3)
                    for a in range(4):
                        sl = slice(a * P, (a + 1) * P)
                        mm = pe.matmul(ps[:, b, sl], A(DLM, 2, 512)[:, b % 2, sl], T[:, b, sl], start=True, stop=True)
                    mm.then_inc(sem("dn_u"), 1)
                    pe.wait_ge(sem("dn_uout"), n + 1)
                    if n >= 2:
                        pe.wait_ge(sem("dn_T"), n - 1)
                    for a in range(4):
                        sl = slice(a * P, (a + 1) * P)
                        pe.matmul(ps[:, 4 + 2 * (b % 2), sl], TTr[:, b, sl], A(DU, 2, 512)[:, b % 2, sl],
                                  start=True, stop=True)
                        mm = pe.matmul(ps[:, 5 + 2 * (b % 2), sl], A(DU, 2, 512)[:, b % 2, sl], TTr[:, b, sl],
                                       start=True, stop=True)
                    mm.then_inc(sem("dn_tu"), 1)
            barrier()
            vb, kbg, kdec = A(DVB, TT, 512), A(DKBG, TT, 512), A(DKDEC, TT, 512)
            for t in range(TT):
                for a in range(4):
                    for par in range(2):
                        h = 2 * a + par
                        inv = TTr[:, 2 * t + par, a * P:(a + 1) * P]
                        pe.matmul(ps[:, t, h * 64:(h + 1) * 64], inv, vb[:, t, h * 64:(h + 1) * 64],
                                  start=True, stop=True)
                        mm = pe.matmul(ps[64 * par:64 * par + 64, 2 + t, a * P:(a + 1) * P],
                                       kbg[:, t, h * 64:(h + 1) * 64], inv, start=True, stop=True)
            mm.then_inc(sem("dn_uw"), 1)
            barrier()
            St, vn, wTt, qd = A(DST, 4, 64), A(DVN, 8, 64), A(DWT, TT, 512), A(DQD, 4, S)
            qk = A(DQK, 4, 512)
            for ci in range(4):
                t, pb = ci // 2, 64 * (ci % 2)
                pe.wait_ge(sem("dn_S"), ci + 1)
                if ci >= 1:
                    pe.wait_ge(sem("dn_o"), ci)
                for par in range(2):
                    lo = 64 * par
                    for a in range(4):
                        pe.matmul(ps[pb:pb + 64, par, a * 64:(a + 1) * 64],
                                  wTt[lo:lo + 64, t, a * P + pb:a * P + pb + 64], St[lo:lo + 64, a, :],
                                  start=True, stop=True)
                        mm = pe.matmul(ps[pb:pb + 64, par, 256 + a * 64:256 + (a + 1) * 64],
                                       qd[lo:lo + 64, a, t * P + pb:t * P + pb + 64], St[lo:lo + 64, a, :],
                                       start=True, stop=True)
                mm.then_inc(sem("dn_ws"), 1)
                pe.wait_ge(sem("dn_vn"), ci + 1)
                for a in range(4):
                    for par in range(2):
                        h = 2 * a + par
                        pe.matmul(ps[pb:pb + 64, 2, h * 64:(h + 1) * 64],
                                  qk[pb:pb + 64, 2 * t + par, a * P + pb:a * P + pb + 64], vn[pb:pb + 64, h, :],
                                  start=True, stop=True)
                        mm = pe.matmul(ps[64 * par:64 * par + 64, 3, a * 64:(a + 1) * 64],
                                       kdec[pb:pb + 64, t, h * 64:(h + 1) * 64], vn[pb:pb + 64, h, :],
                                       start=True, stop=True)
                mm.then_inc(sem("dn_su"), 1)
            pe.wait_ge(sem("dn_gated"), 1)
            o_ = A(DO, TT, 512)
            for t in range(TT):
                for c in range(4):
                    mm = pe.transpose(ps[:, 4 + c // 2, (c % 2) * S + t * P:(c % 2) * S + (t + 1) * P],
                                      o_[:, t, c * P:(c + 1) * P], ident)
            mm.then_inc(sem("ob_turned"), 1)
            pe.wait_ge(sem("ob_out"), 1)
            abT = A(DOUT, 8, S)
            down_product("ab_out", 2, lambda k, t: abT[:, k, t * P:(t + 1) * P])
            barrier()
            modulation(3)
            barrier()
            if upto < 10:
                return
            turn_all(A(0, TT, D), sem("x_scaled"), 4 * TT, sem("h_turned"))
            barrier()
            g = 0
            for c in range(6):
                pairs = 2 if c < 5 else 1
                for kind in range(2):
                    wt = weights("ffn", 2 * c + kind)
                    for j in range(pairs):
                        if c >= 1:
                            pe.wait_ge(sem("sw_silu") if kind == 0 else sem("sw_hidden"), 2 * (c - 1) + j + 1)
                        feature_pair(wt, j, 2 * kind + j)
            pe.wait_ge(sem("sw_hidden"), 11)
            hid = A(FH, 22, S)
            down_product("ffn_down", 6, lambda k, t: hid[:, k, t * P:(t + 1) * P])
            barrier()
            modulation(4)
            barrier()

            if upto < 11:
                return
            turn_all(A(0, TT, D), sem("x_scaled"), 5 * TT, sem("h_turned"))
            barrier()
            for g in range(14):
                if g % 2 == 0:
                    wt = weights("cd_in", g // 2)
                if g >= 4:
                    pe.wait_ge(sem("cd_out1"), g - 3)
                feature_pair(wt, g % 2, g % 4)
            wt = weights("lru_gates", 0)
            pe.wait_ge(sem("lru_step"), 1)
            xcc = A(LX, KT, S)
            for g in range(8):
                bank = 4 + g % 4
                if g >= 4:
                    pe.wait_ge(sem("lru_gate"), 2 * (g - 3))
                for i in range(2):
                    n = 2 * (g % 4) + i
                    mm = pe.matmul(ps[:, bank, i * S:(i + 1) * S], wt[:, 8 * (g // 4) + n, :], xcc[:, n, :],
                                   start=True, stop=True)
                mm.then_inc(lin_done, 1)
            barrier()
            pe.wait_ge(sem("cd_ready"), 1)
            cdT = A(LOUT, 12, S)
            down_product("cd_out", 3, lambda k, t: cdT[:, k, t * P:(t + 1) * P])
            barrier()
            modulation(5)
            barrier()

            if upto < 12:
                return
            turn_all(A(0, TT, D), sem("x_scaled"), 6 * TT, sem("h_turned"))
            barrier()
            for t in range(TT):
                for k in range(KT):
                    mm = pe.matmul(ps[:, 0, t * 8:(t + 1) * 8], hT[:, k, t * P:(t + 1) * P], router[:, k, :],
                                   start=(k == 0), stop=(k == KT - 1))
            mm.then_inc(sem("routed"), 1)
            pe.wait_ge(sem("routing"), 2)
            mask = A(MO, TT, EXPERTS)
            pe.matmul(ps[:, 1, 0:8], con("until"), mask[:, 0, :], start=True, stop=True)
            pe.matmul(ps[:, 1, 8:16], ones, mask[:, 0, :], start=True, stop=False)
            pe.matmul(ps[:, 1, 8:16], con("until"), mask[:, 1, :], start=False, stop=True)
            pe.matmul(ps[:, 1, 16:24], ones, mask[:, 0, :], start=True, stop=False)
            pe.matmul(ps[:, 1, 16:24], ones, mask[:, 1, :], start=False, stop=True).then_inc(sem("routed"), 1)

            xn, gathered = A(0, TT, D), A(EG, KT, P)
            hidden, hiddenT = A(EH, 2, 512), A(ET, 28, P)
            select, gated, turned = A(ESEL, TT, P), A(EGATED, TT, P), A(ETURN, TT, P)

            def gather(done):
                for k in range(KT):
                    for t in range(TT):
                        mm = pe.matmul(ps[:, k // 4, (k % 4) * P:(k % 4 + 1) * P], xn[:, t, k * P:(k + 1) * P],
                                       select[:, t, :], start=(t == 0), stop=(t == TT - 1))
                mm.then_inc(done, 1)

            def scatter(t):
                for h in range(2):
                    pe.matmul(ps[:, 6 + h, :], turned[:, t, :], A(EY, D)[:, h * 512:(h + 1) * 512],
                              start=True, stop=True).then_inc(sem("scattered"), 1)

            def turn_hidden(i, f):
                pe.wait_ge(sem("moe_hidden"), i * GU + (f + 1))
                if f < 2:
                    pe.wait_ge(sem("moe_added"), i * 4 + (4 + f))
                else:
                    pe.wait_ge(sem("hidden_copied"), i * GU + (f - 1))
                for j in range(4):
                    mm = pe.transpose(ps[:, 6 + f % 2, j * P:(j + 1) * P], hidden[:, f % 2, j * P:(j + 1) * P], ident)
                mm.then_inc(sem("hidden_turned"), 1)

            pe.wait_ge(sem("routing"), 3)
            n_rounds = pe.value_load(rounds[0:1, 0:1], min_val=EXPERTS, max_val=ROUNDS)
            pe.wait_ge(sem("selected"), 1)
            gather(sem("gathered"))
            with pe.Fori(0, n_rounds) as i:
                def chunk(c, n):
                    slot = e_slot(c)
                    pe.wait_ge(w_landed[slot], i * (16 * GU) + (16 * uses[slot] + 16 * (c // RING + 1)))
                    return ring[:, slot, :].rearrange("p (k n) -> p k n", n=n)

                pe.wait_ge(sem("gathered_ready"), i * 2 + 2)
                for f in range(GU):
                    for kind in range(2):
                        if f >= 2:
                            pe.wait_ge(sem("moe_hidden") if kind else sem("moe_silu"), i * GU + (f - 1))
                        wt = chunk(2 * f + kind, 512)
                        for k in range(KT):
                            mm = pe.matmul(ps[:, 2 * kind + f % 2, :], gathered[:, k, :], wt[:, k, :],
                                           start=(k == 0), stop=(k == KT - 1))
                        mm.then_inc(lin_done, 1)
                        if f == 0:
                            if kind == 0:
                                pe.wait_ge(sem("expert_out"), i * 2 + 2)
                            else:
                                pe.wait_ge(sem("moe_added"), i * 4 + 3)
                            scatter(kind)
                    if f:
                        turn_hidden(i, f - 1)
                for f in range(GU):
                    wt = chunk(2 * GU + f, D)
                    pe.wait_ge(sem("hidden_copied"), i * GU + (f + 1))
                    for h in range(2):
                        for k in range(4):
                            mm = pe.matmul(ps[:, 4 + h, :], hiddenT[:, 4 * f + k, :], wt[:, k, h * 512:(h + 1) * 512],
                                           start=(f + k == 0), stop=(4 * f + k == 27))
                    mm.then_inc(lin_done, 1)
                    if f == 0:
                        turn_hidden(i, GU - 1)
                    if f == 1:
                        pe.wait_ge(sem("selected"), i + 2)
                        for t in range(TT):
                            pe.transpose(ps[:, 2, t * P:(t + 1) * P], gated[:, t, :], ident)
                        gather(sem("gathered"))
            pe.wait_ge(sem("expert_out"), n_rounds * 2 + 2)
            scatter(0)
            pe.wait_ge(sem("moe_added"), n_rounds * 4 + 3)
            scatter(1)
            barrier()

        @block.scalar
        def _(act):
            barrier = barrier_of(act)
            L = Lane(act, sem("act_step"))
            eps = con("eps")

            def f(o, i, fn, s=None, **kw):
                L(nc.scalar.activation(o, i, fn, **kw), s)

            def copy(o, i, s=None):
                L(nc.scalar.copy(o, i), s)

            def rstd(dst, src, scale, s=None):
                f(dst, src, ACT.Ln, bias=eps, scale=scale)
                L.settle()
                f(dst, dst, ACT.Exp, s, scale=-0.5)

            norm = [0]

            def norm_stats(scratch_):
                n = norm[0]
                norm[0] += 1
                for t in range(TT):
                    f(scratch_[:, t, :], x[:, t, :], ACT.Square, accum_out=small[:, 600 + t:601 + t])
                L.settle()
                rstd(small[:, 602:604], small[:, 600:602], 1.0 / D, sem("norm_rstd"))

            act.wait_ge(sem("line_mm"), 1)
            for i, n in enumerate(row_n):
                copy(cols[:, i, 0:n], ps[:, 0, i * P:i * P + n], sem("cols_out"))
            L.settle()
            for i, name in enumerate(("c", "c_2")):
                f(small[:, 608 + 8 * i:616 + 8 * i], col(name, 0, 8), ACT.Silu, sem("c_silu"))
            for h in range(8):
                act.wait_ge(sem("line_mm"), h + 2)
                copy(A(8192, 8, 383)[:, h, :], ps[:, 2 + h % 2, 0:383], sem("bias_line"))
            act.wait_ge(params_in, N_PARAMS)
            f(small[:, 0:16], spr("a_log"), ACT.Exp, sem("a_exp"))
            f(small[:, 16:24], spr("dn_a_log_2"), ACT.Exp, sem("a_exp"))
            act.wait_ge(x_in, 16 * TT)
            norm_stats(A(4096, TT, D))
            barrier()
            if upto < 1:
                return
            barrier()

            if upto < 2:
                return
            for g in range(12):
                act.wait_ge(lin_done, lin0("q") + g + 1)
                dst = A(QT if g < 6 else KTT, HEADS, S)[:, 2 * (g % 6):2 * (g % 6) + 2, :].rearrange("p a b -> p (a b)")
                copy(dst, ps[:, g % 4, :])
                if g >= 2:
                    act.wait_ge(sem("qk_ss"), g - 1)
                f(A(QSQ, 2, 512)[:, g % 2, :], ps[:, g % 4, :], ACT.Square, sem("qk_raw"))
                if g >= 1:
                    act.wait_ge(sem("qk_ss"), g)
                    if g >= 3:
                        act.wait_ge(sem("qk_normed"), g - 2)
                    rstd(A(QRS, 2, 512)[:, (g - 1) % 2, :], ps[:, 4 + (g - 1) % 2, :], 1.0 / P, sem("qk_rstd"))
            act.wait_ge(sem("qk_ss"), 12)
            act.wait_ge(sem("qk_normed"), 10)
            rstd(A(QRS, 2, 512)[:, 1, :], ps[:, 5, :], 1.0 / P, sem("qk_rstd"))
            v = A(VT, TT, HEADS * P)
            for g in range(6):
                act.wait_ge(lin_done, lin0("v") + g + 1)
                copy(v[:, g % 2, (g // 2) * 512:(g // 2 + 1) * 512], ps[:, g % 4, :], sem("v_out"))
            barrier()

            if upto < 3:
                return
            for i in range(8):
                t = i % 2
                n = 3 * (t + 1) * P
                act.wait_ge(sem("at_max"), i + 1)
                f(A(AP_, 2, 768)[:, i % 2, 0:n], A(AS_, 2, 768)[:, i % 2, 0:n], ACT.Exp, sem("at_exp"),
                  bias=small[:, 64 + i:65 + i], accum_out=small[:, 72 + i:73 + i])
                act.wait_ge(sem("at_pT"), i + 1)
                b = n // P
                copy(A(APT, 2, 768)[:, i % 2, 0:min(b, 4) * P], ps[:, 4, 0:min(b, 4) * P],
                     None if b > 4 else sem("at_turned"))
                if b > 4:
                    copy(A(APT, 2, 768)[:, i % 2, 4 * P:b * P], ps[:, 5, 0:(b - 4) * P], sem("at_turned"))
            barrier()

            if upto < 4:
                return
            gate = A(2048, TT, D)

            def gates(name, s):
                for g in range(4):
                    act.wait_ge(lin_done, lin0(name) + g + 1)
                    f(gate[:, g % 2, (g // 2) * 512:(g // 2 + 1) * 512], ps[:, g % 4, :], ACT.Sigmoid, s)

            gates("gate_attn", sem("ga_out"))
            barrier()
            u = A(PU, TT, D)
            for g in range(4):
                act.wait_ge(lin_done, lin0("u") + g + 1)
                copy(u[:, g % 2, (g // 2) * 512:(g // 2 + 1) * 512], ps[:, g % 4, :], sem("u_out"))
            gates("gate_pool", sem("gp_out"))
            barrier()

            if upto < 5:
                return
            raw = A(SRAW, 12, 259)
            for g in range(6):
                act.wait_ge(lin_done, lin0("xbc") + g + 1)
                copy(raw[:, 2 * g:2 * g + 2, 3:259], ps[:, g % 4, :].rearrange("p (a b) -> p a b", a=2), sem("xbc_out"))
            act.wait_ge(sem("softplus_in"), 1)
            f(small[:, 128:160], small[:, 96:128], ACT.Exp, sem("softplus_fn"), scale=-1.0)
            act.wait_ge(sem("softplus_in"), 2)
            f(small[:, 192:224], small[:, 160:192], ACT.Ln, sem("softplus_fn"))
            for g in range(4):
                act.wait_ge(lin_done, lin0("z") + g + 1)
                f(A(SZ, TT, D)[:, g % 2, (g // 2) * 512:(g // 2 + 1) * 512], ps[:, g % 4, :], ACT.Silu, sem("z_out"))
            xbcT = A(SX, 12, S)
            for c in range(12):
                act.wait_ge(sem("conv"), c + 1)
                f(xbcT[:, c, :], xbcT[:, c, :], ACT.Silu, bias=col("conv_b", c))
            act.wait_ge(sem("acum_mm"), 1)
            copy(small[:, 224:256], ps[:, 4, 0:32])
            f(small[:, 256:288], ps[:, 4, 0:32], ACT.Exp)
            f(small[:, 288:304], ps[:, 4, 32:48], ACT.Exp)
            barrier()
            act.wait_ge(sem("cb_mm"), 1)
            copy(A(SB, 256), ps[:, 0, 0:256])
            copy(A(SCB, 512), ps[:, 1, :], sem("bcb_out"))
            act.wait_ge(sem("state_mm"), 1)
            for g in range(2):
                copy(A(SST, 2, 512)[:, g, :], ps[:, g, :], None if g == 0 else sem("state_out"))
            for b in range(8):
                act.wait_ge(sem("seg_masked"), b + 1)
                e = A(SE, 2, 512)[:, b % 2, :]
                f(e, e, ACT.Exp, sem("seg_exp"))
            barrier()
            y = A(SRAW, TT, D)
            act.wait_ge(sem("y_gated"), 1)
            for t in range(TT):
                for g in range(2):
                    f(A(SXX, TT, D)[:, t, g * 512:(g + 1) * 512], y[:, t, g * 512:(g + 1) * 512], ACT.Square,
                      accum_out=small[:, 304 + 2 * t + g:305 + 2 * t + g])
            L.settle()
            rstd(small[:, 308:312], small[:, 304:308], 1.0 / 512, sem("y_rstd"))
            gates("gate_ssd", sem("gs_out"))
            barrier()

            if upto < 6:
                return
            barrier()
            norm_stats(A(4096, TT, D))
            barrier()
            barrier()
            hid = A(FH, 32, S)
            for g in range(16):
                act.wait_ge(lin_done, lin0("ff1") + g + 1)
                f(hid[:, 2 * g:2 * g + 2, :].rearrange("p a b -> p (a b)"), ps[:, g % 4, :], ACT.Relu, sem("ff_relu"))
            barrier()
            norm_stats(A(4096, TT, D))
            barrier()
            if upto < 7:
                return

            barrier()
            for j in range(2):
                act.wait_ge(lin_done, lin0("qa") + j + 1)
                copy(A(WQ, 2, 512)[:, j, :], ps[:, j, :], sem("ab_out1"))
            act.wait_ge(lin_done, lin0("kva") + 1)
            kdup = A(WK, 2, S)
            for kv in range(2):
                for half in range(2):
                    copy(kdup[64 * half:64 * half + 64, kv, :], ps[64 * kv:64 * kv + 64, 2, 0:S],
                         sem("ab_out1") if (kv, half) == (1, 1) else None)
            act.wait_ge(lin_done, lin0("kva") + 3)
            copy(A(WV, TT * P), ps[:, 3, 0:S], sem("ab_out1"))
            raw = A(WRAW, 12, 259)
            for g in range(6):
                act.wait_ge(lin_done, lin0("qkv_b") + g + 1)
                copy(raw[:, 2 * g:2 * g + 2, 3:259], ps[:, g % 4, :].rearrange("p (a b) -> p a b", a=2), sem("ab_out1"))
            for t in range(TT):
                act.wait_ge(lin_done, lin0("gate_b") + t + 1)
                f(A(DGS, TT, 512)[:, t, :], ps[:, 4 + t, :], ACT.Silu)
            qkvT = A(DQKV, 12, S)
            for c in range(12):
                act.wait_ge(sem("dn_conv"), c + 1)
                f(qkvT[:, c, :], qkvT[:, c, :], ACT.Silu, sem("dn_silu"))
            act.wait_ge(sem("beta_raw"), 1)
            f(small[:, SBETA:SBETA + 16], small[:, 464:480], ACT.Sigmoid)
            act.wait_ge(sem("softplus_in"), 3)
            f(small[:, 128:144], small[:, 96:112], ACT.Exp, sem("softplus_fn"), scale=-1.0)
            act.wait_ge(sem("softplus_in"), 4)
            f(small[:, 192:208], small[:, 160:176], ACT.Ln, sem("softplus_fn"))
            barrier()
            if upto < 8:
                return
            for i in range(4):
                t = i // 2
                n = 4 * (t + 1) * P
                act.wait_ge(sem("wa_shift"), i + 1)
                f(A(WS, 4 * S)[:, 0:n], A(WS, 4 * S)[:, 0:n], ACT.Exp)
                f(small[:, 96:100], small[:, 100:104], ACT.Exp, sem("wa_exp"))
                act.wait_ge(sem("wa_pT"), i + 1)
                for b in range(t + 1):
                    copy(A(WPT, 4 * S)[:, b * 512:(b + 1) * 512], ps[:, 2 + b, :],
                         sem("wa_turned") if b == t else None)
            for g in range(4):
                if g >= 2:
                    act.wait_ge(sem("l2_ss"), g - 1)
                elif g == 0:
                    act.wait_ge(sem("wa_out"), 4)
                f(A(WS, 2, 512)[:, g % 2, :], qkvT[:, 2 * g:2 * g + 2, :].rearrange("p a b -> p (a b)"), ACT.Square,
                  sem("l2_sq"))
                act.wait_ge(sem("l2_ss"), g + 1)
                if g >= 1:
                    act.wait_ge(sem("l2_normed"), g)
                rstd(A(WPT, 2, 512)[:, g % 2, :], ps[:, 5 + g % 2, :], 1.0, sem("l2_rstd"))
            barrier()
            if upto < 9:
                return
            act.wait_ge(sem("dn_gc"), 1)
            copy(small[:, SGC:SGC + 16], ps[:, 4, 0:16])
            f(small[:, SEG:SEG + 32], ps[:, 4, 0:32], ACT.Exp, sem("dn_eg"))
            barrier()
            for b in range(4):
                o = 4 * (b % 2)
                act.wait_ge(sem("dn_seg"), b + 1)
                f(A(DEGB, 4, 512)[:, b, :], ps[:, o, :], ACT.Exp, sem("dn_egb"))
                f(A(DT, 2, 512)[:, b % 2, :], A(DT, 2, 512)[:, b % 2, :], ACT.Exp, sem("dn_dec"))
            barrier()
            for n in range(4 * len(LEVELS)):
                b = n % 4
                act.wait_ge(sem("dn_u"), n + 1)
                if n >= 2:
                    act.wait_ge(sem("dn_tu"), n - 1)
                copy(A(DU, 2, 512)[:, b % 2, :], ps[:, b, :], sem("dn_uout"))
            barrier()
            act.wait_ge(sem("dn_uw"), 1)
            for t in range(TT):
                copy(A(DUU, TT, 512)[:, t, :], ps[:, t, :])
                copy(A(DWT, TT, 512)[:, t, :], ps[:, 2 + t, :])
            barrier()
            for ci in range(4):
                t, pb = ci // 2, 64 * (ci % 2)
                act.wait_ge(sem("dn_vn"), ci + 1)
                for par in range(2):
                    dst = A(DO, TT, 512)[pb:pb + 64, t, :].rearrange("p (a b e) -> p a b e", b=2, e=64)[:, :, par, :]
                    src = ps[pb:pb + 64, par, 256:512].rearrange("p (a e) -> p a e", e=64)
                    copy(dst, src, sem("dn_o1") if par else None)
            act.wait_ge(sem("dn_oss"), 1)
            rstd(small[:, 448:464], small[:, 432:448], 1.0 / 64, sem("dn_orstd"))
            barrier()
            norm_stats(A(4096, TT, D))
            barrier()
            if upto < 10:
                return
            barrier()
            for c in range(6):
                for j in range(2 if c < 5 else 1):
                    act.wait_ge(lin_done, lin0("ffn") + 4 * c + j + 1)
                    g = 2 * c + j
                    if g >= 4:
                        act.wait_ge(sem("sw_hidden"), g - 3)
                    f(A(FT, 4, 512)[:, g % 4, :], ps[:, j, :], ACT.Silu, sem("sw_silu"))
            barrier()
            norm_stats(A(4096, TT, D))
            barrier()

            if upto < 11:
                return
            barrier()
            raw = A(LRAW, 8, 259)
            for g in range(14):
                act.wait_ge(lin_done, lin0("cd_in") + g + 1)
                pair = ps[:, g % 4, :].rearrange("p (a b) -> p a b", a=2)
                if g < 4:
                    copy(raw[:, 2 * g:2 * g + 2, 3:259], pair, sem("cd_out1"))
                elif g < 8:
                    f(A(LY, KT, S)[:, 2 * g - 8:2 * g - 6, :], pair, ACT.Gelu_apprx_tanh, sem("cd_out1"))
                else:
                    copy(A(LB, 12, S)[:, 2 * g - 16:2 * g - 14, :], pair, sem("cd_out1"))
            act.wait_ge(sem("softplus_in"), 5)
            f(small[:, 128:136], small[:, 96:104], ACT.Exp, sem("softplus_fn"), scale=-1.0)
            act.wait_ge(sem("softplus_in"), 6)
            f(small[:, 192:200], small[:, 160:168], ACT.Ln, sem("softplus_fn"))
            for g in range(8):
                act.wait_ge(lin_done, lin0("lru_gates") + g + 1)
                for i in range(2):
                    n = 2 * (g % 4) + i
                    b = col("lru_gate_a_b_2" if g < 4 else "lru_gate_x_b_2", n)
                    f(A(LR if g < 4 else LI, KT, S)[:, n, :], ps[:, 4 + g % 4, i * S:(i + 1) * S], ACT.Sigmoid,
                      sem("lru_gate"), bias=b)
            act.wait_ge(sem("lru_step"), 2)
            f(A(LA, KT * S), A(LR, KT * S), ACT.Exp, sem("lru_a"))
            f(A(LH, KT * S), A(LR, KT * S), ACT.Tanh, sem("lru_a"))
            act.wait_ge(sem("lru_step"), 3)
            f(A(LR, KT * S), A(LR, KT * S), ACT.Sqrt, sem("lru_a"))
            barrier()
            barrier()
            norm_stats(A(4096, TT, D))
            barrier()
            if upto < 12:
                return
            barrier()
            act.wait_ge(sem("routing"), 1)
            for t in range(TT):
                f(small[:, 500 + t:501 + t], small[:, 502 + t:503 + t], ACT.Exp, sem("gate_exp"))
            gathered, hiddenT = A(EG, KT, P), A(ET, 28, P)

            def modulate():
                for k in range(KT // 2):
                    ins = nc.scalar.activation(gathered[:, k, :], ps[:, 0, k * P:(k + 1) * P], ACT.Identity,
                                               bias=shift[:, KT + k:KT + k + 1], scale=shift[:, k:k + 1])
                ins.then_inc(sem("gathered_ready"), 1)

            act.wait_ge(sem("routing"), 3)
            n_rounds = act.value_load(rounds[0:1, 0:1], min_val=EXPERTS, max_val=ROUNDS)
            act.wait_ge(sem("gathered"), 1)
            modulate()
            with act.Fori(0, n_rounds) as i:
                def copy_hidden(c):
                    act.wait_ge(sem("hidden_turned"), i * GU + (c + 1))
                    nc.scalar.copy(A(ET, 7, 512)[:, c, :], ps[:, 6 + c % 2, :]).then_inc(sem("hidden_copied"), 1)

                for c in range(GU):
                    act.wait_ge(lin_done, i * E_CHUNKS + (plan.steps + 2 * c + 1))
                    if c >= 2:
                        act.wait_ge(sem("moe_hidden"), i * GU + (c - 1))
                    nc.scalar.activation(A(ES, 2, 512)[:, c % 2, :], ps[:, c % 2, :], ACT.Silu
                                         ).then_inc(sem("moe_silu"), 1)
                    if c:
                        copy_hidden(c - 1)
                copy_hidden(GU - 1)
                act.wait_ge(sem("gathered"), i + 2)
                nc.scalar.copy(A(ETURN, TT * P), ps[:, 2, 0:TT * P])
                modulate()
                act.wait_ge(lin_done, i * E_CHUNKS + (plan.steps + E_CHUNKS))
                nc.scalar.copy(A(EY, D)[:, 0:512], ps[:, 4, :]).then_inc(sem("expert_out"), 1)
            barrier()
            act.wait_ge(sem("x_final"), 1)
            norm_stats(A(4096, TT, D))
            act.wait_ge(sem("x_final"), 2)
            act.dma_start(A(2048, D), w["final_norm_w_2"].rearrange("(a n) -> a n", a=1).broadcast_to([P, D])
                          ).then_inc(sem("final_w_in"), 16)

        @block.vector
        def _(dve):
            barrier = barrier_of(dve)
            L = Lane(dve, sem("dve_step"))
            V = nc.vector

            def tt(o, a, b, op, s=None):
                L(V.tensor_tensor(o, a, b, op), s)

            def ts(o, a, c1, op, c2=None, op2=None, s=None):
                if op2 is None:
                    L(V.tensor_scalar(o, a, c1, None, op), s)
                else:
                    L(V.tensor_scalar(o, a, c1, c2, op, op2), s)

            def stt(o, a, c, b, op, op2, s=None):
                L(V.scalar_tensor_tensor(out=o, in0=a, scalar=c, in1=b, op0=op, op1=op2), s)

            def copy(o, i, s=None):
                L(V.tensor_copy(o, i), s)

            def modulation_slabs(u):
                if u:
                    dve.wait_ge(sem("mod_summed"), u)
                L(V.memset(ada[:], 0.0), sem("ada_clear"))
                dve.wait_ge(sem("ada_bias"), 16 * (u + 1))
                for k in range(KT):
                    i = u * KT + k
                    dve.wait_ge(sem(f"slab_in{i % 2}"), 16 * (i // 2 + 1))
                    L.settle()
                    c = small[:, 608 + 8 * (u >= 2) + k:609 + 8 * (u >= 2) + k]
                    stt(ada[:], slab[:, i % 2, :], c, ada[:], ALU.mult, ALU.add, sem("slab_used"))
                L.settle()
                L(V.memset(small[:, 639:640], 0.0), sem("ada_ready"))

            def modulation_take(u, norm_w):
                dve.wait_ge(sem("mod_summed"), u + 1)
                stt(shift[:, 0:KT], ps[:, 4, KT:2 * KT], 1.0, norm_w, ALU.add, ALU.mult)
                copy(shift[:, KT:2 * KT], ps[:, 4, 0:KT])
                for h in range(2):
                    copy(gain[:, h * 512:(h + 1) * 512], ps[:, 5 + h, :])

            def norm_apply(u):
                dve.wait_ge(sem("norm_rstd"), u + 1)
                for t in range(TT):
                    ts(A(0, TT, D)[:, t, :], x[:, t, :], small[:, 602 + t:603 + t], ALU.mult, s=sem("x_scaled"))

            def turned_h(u):
                dve.wait_ge(sem("h_turned"), u + 1)
                for k in range(KT):
                    ts(hT[:, k, :], ps[:, 4 + k // 2, (k % 2) * S:(k % 2 + 1) * S], shift[:, k:k + 1], ALU.mult,
                       shift[:, KT + k:KT + k + 1], ALU.add)

            def residual(tmp):
                for t in range(TT):
                    for h in range(2):
                        sl = slice(h * 512, (h + 1) * 512)
                        tt(tmp[:, t, sl], gain[:, sl], ps[:, 4 + 2 * t + h, :], ALU.mult)
                L.settle()
                for t in range(TT):
                    tt(x[:, t, :], x[:, t, :], tmp[:, t, :], ALU.add)
                L.settle()

            def branch(name, s, n, first, tmp):
                mix, gate = A(0, TT, D), A(2048, TT, D)
                dve.wait_ge(s, 4)
                dve.wait_ge(lin_done, lin0(name) + n)
                for t in range(TT):
                    for h in range(2):
                        sl = slice(h * 512, (h + 1) * 512)
                        tt((mix if first else tmp)[:, t, sl], gate[:, t, sl], ps[:, 4 + 2 * t + h, :], ALU.mult)
                if not first:
                    L.settle()
                    for t in range(TT):
                        tt(mix[:, t, :], mix[:, t, :], tmp[:, t, :], ALU.add)

            soft = [0]

            def softplus(src, n, dst):
                k = soft[0] = soft[0] + 1
                ax, e, u, lnu = (small[:, o:o + n] for o in (96, 128, 160, 192))
                L.settle()
                ts(ax, src, -1.0, ALU.mult)
                L.settle()
                tt(ax, ax, src, ALU.max, sem("softplus_in"))
                dve.wait_ge(sem("softplus_fn"), 2 * k - 1)
                ts(u, e, 1.0, ALU.add, s=sem("softplus_in"))
                L.settle()
                d, z = small[:, 320:320 + n], small[:, 352:352 + n]
                ts(d, u, -1.0, ALU.add)
                L.settle()
                ts(z, d, 0.0, ALU.is_equal)
                L.settle()
                tt(d, d, z, ALU.add)
                L.settle()
                L(V.reciprocal(d, d))
                tt(z, z, e, ALU.mult)
                L.settle()
                tt(d, d, e, ALU.mult)
                L.settle()
                dve.wait_ge(sem("softplus_fn"), 2 * k)
                tt(d, d, lnu, ALU.mult)
                L.settle()
                tt(d, d, z, ALU.add)
                ts(ax, src, 0.0, ALU.max)
                L.settle()
                tt(dst, d, ax, ALU.add)
                L.settle()

            def conv(raw, dst, taps, wname, stride, tiles, s=None, bias=None):
                L.settle()
                for c in range(tiles):
                    for j in range(taps):
                        wc = col(wname, j * stride + c)
                        src = raw[:, c, j:j + S]
                        last = j == taps - 1
                        if j == 0:
                            if bias:
                                ts(dst[:, c, :], src, wc, ALU.mult, col(bias, c), ALU.add)
                            else:
                                ts(dst[:, c, :], src, wc, ALU.mult)
                        else:
                            L.settle()
                            stt(dst[:, c, :], src, wc, dst[:, c, :], ALU.mult, ALU.add, s if last else None)

            L(V.memset(A(500, 8)[32:33, :], NEG))
            dve.wait_ge(rows_in, N_ROWS)
            dve.wait_ge(params_in, N_PARAMS)
            L.settle()
            tt(A(1024, 8, P)[0:33, :, :], ones[0:33, :].unsqueeze(1).broadcast_to([33, 8, P]),
               A(500, 8)[0:33, :].unsqueeze(2).broadcast_to([33, 8, P]), ALU.mult, sem("line_lhs"))
            dve.wait_ge(sem("c_silu"), 2)
            dve.wait_ge(sem("cols_out"), 3)
            dve.wait_ge(sem("a_exp"), 2)
            modulation_slabs(0)
            modulation_take(0, col("norm1_w", 0, 8))
            ts(small[:, 0:24], small[:, 0:24], -1.0, ALU.mult)
            ts(small[:, 24:25], col("q_norm_w"), float(P) ** -0.5, ALU.mult)
            dve.wait_ge(sem("bias_line"), 8)
            dve.wait_ge(sem("line_out"), 16)
            dve.wait_ge(x_in, 16 * TT)
            barrier()
            if upto < 1:
                return
            norm_apply(0)
            turned_h(0)
            barrier()

            if upto < 2:
                return
            for g in range(12):
                dve.wait_ge(sem("qk_rstd"), g + 1)
                dst = A(QT if g < 6 else KTT, HEADS, S)[:, 2 * (g % 6):2 * (g % 6) + 2, :].rearrange("p a b -> p (a b)")
                stt(dst, dst, small[:, 24:25] if g < 6 else col("k_norm_w"), A(QRS, 2, 512)[:, g % 2, :],
                    ALU.mult, ALU.mult, sem("qk_normed"))
            modulation_slabs(1)
            barrier()

            if upto < 3:
                return
            for i in range(9):
                if i < 8:
                    j, t = i // 2, i % 2
                    n = (t + 1) * P
                    dve.wait_ge(sem("at_scores"), i + 1)
                    if i >= 2:
                        dve.wait_ge(sem("at_exp"), i - 1)
                    for g in range(3):
                        o = (ps[:, 2 * (i % 2), g * P:(g + 1) * P] if t == 0
                             else ps[:, 2 * (i % 2) + g // 2, (g % 2) * S:(g % 2 + 1) * S])
                        stt(A(AS_, 2, 768)[:, i % 2, g * n:(g + 1) * n], con(f"dist{t}{g}"),
                            -float(slopes[4 * g + j]), o, ALU.mult, ALU.add, sem("at_masked") if g == 2 else None)
                    L.settle()
                    L(V.tensor_reduce(small[:, 64 + i:65 + i], A(AS_, 2, 768)[:, i % 2, 0:3 * n], AX.X, ALU.max,
                                      negate=True), sem("at_max"))
                    dve.wait_ge(sem("at_exp"), i + 1)
                    L(V.reciprocal(small[:, 80 + i:81 + i], small[:, 72 + i:73 + i]))
                    L.settle()
                    p_ = A(AP_, 2, 768)[:, i % 2, 0:3 * n]
                    ts(p_, p_, small[:, 80 + i:81 + i], ALU.mult, s=sem("at_probs"))
                if i >= 1:
                    j, t = (i - 1) // 2, (i - 1) % 2
                    dve.wait_ge(sem("at_pv"), i)
                    copy(A(AOT, 4, S)[:, j, t * P:(t + 1) * P], ps[:, 6 + (i - 1) % 2, 0:P], sem("at_out"))
            barrier()

            if upto < 4:
                return
            branch("attn_out", sem("ga_out"), 1, True, None)
            barrier()
            for g in range(4):
                dve.wait_ge(sem("pooled"), g + 1)
                copy(A(PP, KT, S)[:, 2 * g:2 * g + 2, :].rearrange("p a b -> p (a b)"), ps[:, 4 + g, :], sem("pooled_out"))
            for g in range(4):
                dve.wait_ge(lin_done, lin0("pool_mix") + g + 1)
                for o in range(2):
                    ts(A(PM, KT, S)[:, 2 * g + o, :], ps[:, g, o * S:(o + 1) * S], col("pool_scale", 2 * g + o), ALU.mult,
                       s=sem("pool_mixed") if o else None)
            branch("pool_out", sem("gp_out"), 2, False, A(PP, TT, D))
            barrier()

            if upto < 5:
                return
            raw = A(SRAW, 12, 259)
            L(V.memset(raw[:, :, 0:3], 0.0))
            dve.wait_ge(lin_done, lin0("dt") + 2)
            bias = spr("dt_bias")
            xdt = small[:, 400:432]
            for t in range(TT):
                tt(xdt[:, 16 * t:16 * t + 16], ps[:, t, 0:16], bias, ALU.add, sem("dt_out"))
            dt = small[:, 464:496]
            softplus(xdt, 32, dt)
            tt(small[:, 32:64].rearrange("p (t h) -> p t h", t=2), dt.rearrange("p (t h) -> p t h", t=2),
               small[:, 0:16].unsqueeze(1).broadcast_to([P, 2, 16]), ALU.mult, sem("dtA"))
            dve.wait_ge(sem("xbc_out"), 6)
            conv(raw, A(SX, 12, S), 4, "conv_w", 12, 12, sem("conv"))
            barrier()

            def heads(a, n=16, e=64):
                return a.rearrange("p (h e) -> p h e", e=e)

            def per_head(c, n=16, e=64):
                return c.unsqueeze(2).broadcast_to([P, n, e])

            dve.wait_ge(sem("xs_turned"), 1)
            xc, X = A(SXC, TT, D), A(SXX, TT, D)
            for t in range(TT):
                for h in range(2):
                    copy(xc[:, t, h * 512:(h + 1) * 512], ps[:, 4 + 2 * t + h, :])
            L.settle()
            for t in range(TT):
                tt(heads(X[:, t, :]), heads(xc[:, t, :]), per_head(dt[:, 16 * t:16 * t + 16]), ALU.mult)
            L.settle()
            tt(heads(A(SXD, D)), heads(X[:, 0, :]), per_head(small[:, 288:304]), ALU.mult)
            dve.wait_ge(sem("bcb_out"), 1)
            L.settle()
            L(V.memset(small[:, 638:639], 0.0), sem("ssd_inputs"))

            def seg(b):
                t, hb = b // 4, b % 4
                e = A(SE + 512 * (b % 2), 4, P)
                dve.wait_ge(sem("seg_mm"), b + 1)
                if b >= 2:
                    dve.wait_ge(sem("ydiag_mm"), b - 1)
                ac = small[:, 224 + 16 * t + 4 * hb:228 + 16 * t + 4 * hb]
                tt(e, ps[:, 2 + b % 2, :].rearrange("p (j l) -> p j l", j=4), per_head(ac, 4, P), ALU.subtract,
                   sem("seg_out"))
                L.settle()
                tt(e, e, con("causal_neg").unsqueeze(1).broadcast_to([P, 4, P]), ALU.add, sem("seg_masked"))

            def times_cb(b):
                t, hb = b // 4, b % 4
                e = A(SE + 512 * (b % 2), 4, P)
                dve.wait_ge(sem("seg_exp"), b + 1)
                cb = A(SCB, 4, P)[:, 2 * t + hb // 2, :]
                tt(e, e, cb.unsqueeze(1).broadcast_to([P, 4, P]), ALU.mult, sem("decay_cb"))

            seg(0)
            for b in range(8):
                if b < 7:
                    seg(b + 1)
                times_cb(b)
            barrier()
            y = A(SRAW, TT, D)
            for t in range(TT):
                tt(heads(y[:, t, :]), heads(xc[:, t, :]), per_head(spr("d_skip")), ALU.mult)
            L.settle()
            for t in range(TT):
                for h in range(2):
                    sl = slice(h * 512, (h + 1) * 512)
                    tt(y[:, t, sl], y[:, t, sl], ps[:, 4 + 2 * t + h, :], ALU.add)
            for g in range(2):
                tt(heads(A(SXD, D)[:, g * 512:(g + 1) * 512]), heads(ps[:, g, :]),
                   per_head(small[:, 272 + 8 * g:280 + 8 * g], 8), ALU.mult)
            L.settle()
            tt(y[:, 1, :], y[:, 1, :], A(SXD, D), ALU.add)
            L.settle()
            for t in range(TT):
                tt(y[:, t, :], y[:, t, :], A(SZ, TT, D)[:, t, :], ALU.mult, sem("y_gated") if t else None)
            dve.wait_ge(sem("y_rstd"), 1)
            for t in range(TT):
                for g in range(2):
                    sl = slice(g * 512, (g + 1) * 512)
                    ts(y[:, t, sl], y[:, t, sl], small[:, 308 + 2 * t + g:309 + 2 * t + g], ALU.mult,
                       s=sem("y_normed") if t and g else None)
            dve.wait_ge(sem("y_turned"), 1)
            for k in range(KT):
                ts(A(SX, KT, S)[:, k, :], ps[:, 4 + k // 2, (k % 2) * S:(k % 2 + 1) * S], col("ssd_norm_w", k), ALU.mult,
                   s=sem("yT_out") if k == KT - 1 else None)
            branch("ssd_out", sem("gs_out"), 2, False, A(SXC, TT, D))
            L.settle()
            L(V.memset(small[:, 638:639], 0.0), sem("mix_done"))
            barrier()

            if upto < 6:
                return
            dve.wait_ge(sem("mix_turned"), 1)
            for k in range(4):
                copy(A(2048, 4, 512)[:, k, :], ps[:, 4 + k, :], sem("mixT_out") if k == 3 else None)
            dve.wait_ge(lin_done, lin0("mix_out") + 2)
            residual(A(4096, TT, D))
            barrier()
            modulation_take(1, col("norm2_w", 0, 8))
            barrier()
            norm_apply(1)
            turned_h(1)
            barrier()
            modulation_slabs(2)
            hid = A(FH, 32, S)
            for g in range(16):
                dve.wait_ge(sem("ff_relu"), g + 1)
                h_ = hid[:, 2 * g:2 * g + 2, :].rearrange("p a b -> p (a b)")
                tt(h_, h_, h_, ALU.mult, sem("ff_hidden"))
            dve.wait_ge(lin_done, lin0("ff2") + 8)
            residual(A(0, TT, D))
            barrier()
            modulation_take(2, col("norm_mix_w_2", 0, 8))
            barrier()
            if upto < 7:
                return

            norm_apply(2)
            turned_h(2)
            barrier()
            L(V.memset(A(WRAW, 12, 259)[:, :, 0:3], 0.0), sem("bias_wanted"))
            dve.wait_ge(sem("ab_out1"), 10)
            conv(A(WRAW, 12, 259), A(DQKV, 12, S), 4, "dn_conv_w_2", 12, 12, sem("dn_conv"))
            dve.wait_ge(lin_done, lin0("ba") + 2)
            ba = ps[:, 6, 0:32].rearrange("p (t j) -> p t j", t=2)
            tt(small[:, 400:416].rearrange("p (t j) -> p t j", t=2), ba[:, :, 8:16],
               spr("dn_dt_bias_2").unsqueeze(1).broadcast_to([P, 2, 8]), ALU.add)
            copy(small[:, 464:480].rearrange("p (t j) -> p t j", t=2), ba[:, :, 0:8], sem("beta_raw"))
            softplus(small[:, 400:416], 16, small[:, 416:432])
            tt(small[:, SG:SG + 16].rearrange("p (t j) -> p t j", t=2),
               small[:, 416:432].rearrange("p (t j) -> p t j", t=2),
               small[:, 16:24].unsqueeze(1).broadcast_to([P, 2, 8]), ALU.mult, sem("dn_g"))
            modulation_slabs(3)
            barrier()
            if upto < 8:
                return
            dve.wait_ge(sem("bias_in"), 16)
            for i in range(4):
                t, par = i // 2, i % 2
                n = (t + 1) * P
                dve.wait_ge(sem("wa_scores"), i + 1)
                s_ = A(WS, 4, n)
                bias = A(T5_OFF, 4, 2, S)[:, :, par, S - n:S]
                for a2 in range(t + 1):
                    m = 4 // (t + 1)
                    src = ps[:, a2, :].rearrange("p (a n) -> p a n", n=n)
                    stt(s_[:, a2 * m:(a2 + 1) * m, :], src, 0.125, bias[:, a2 * m:(a2 + 1) * m, :], ALU.mult, ALU.add,
                        sem("wa_biased") if a2 == t else None)
                L.settle()
                mx, sk = small[:, 104:108], spr("attn_sinks_2").rearrange("p (a b) -> p a b", b=2)[:, :, par]
                L(V.tensor_reduce(mx, s_, AX.X, ALU.max))
                L.settle()
                tt(mx, mx, sk, ALU.max)
                L.settle()
                tt(s_, s_, mx.unsqueeze(2).broadcast_to([P, 4, n]), ALU.subtract)
                tt(small[:, 100:104], sk, mx, ALU.subtract, sem("wa_shift"))
                dve.wait_ge(sem("wa_exp"), i + 1)
                den = small[:, 108:112]
                L(V.tensor_reduce(den, s_, AX.X, ALU.add))
                L.settle()
                tt(den, den, small[:, 96:100], ALU.add)
                L.settle()
                L(V.reciprocal(den, den))
                L.settle()
                tt(s_, s_, den.unsqueeze(2).broadcast_to([P, 4, n]), ALU.mult, sem("wa_probs"))
                dve.wait_ge(sem("wa_pv"), i + 1)
                lo = 64 * par
                copy(A(DOUT, 8, S)[lo:lo + 64, 0:4, t * P:(t + 1) * P],
                     ps[lo:lo + 64, 4, :].rearrange("p (a n) -> p a n", n=P), sem("wa_out"))
            qkvT = A(DQKV, 12, S)
            for g in range(4):
                dve.wait_ge(sem("l2_rstd"), g + 1)
                dst = qkvT[:, 2 * g:2 * g + 2, :].rearrange("p a b -> p (a b)")
                stt(dst, dst, 0.125 if g < 2 else 1.0, A(WPT, 2, 512)[:, g % 2, :], ALU.mult, ALU.mult, sem("l2_normed"))
            barrier()
            if upto < 9:
                return
            dve.wait_ge(sem("kv_turned"), 1)
            dve.wait_ge(sem("dn_eg"), 1)
            beta, eg, egs = small[:, SBETA:SBETA + 16], small[:, SEG:SEG + 16], small[:, SEG + 16:SEG + 32]
            bg = small[:, 104:120]
            tt(bg, beta, eg, ALU.mult)
            L.settle()
            vb, kbg, kdec = A(DVB, TT, 512), A(DKBG, TT, 512), A(DKDEC, TT, 512)
            for t in range(TT):
                sl = slice(8 * t, 8 * t + 8)
                k_, v_ = heads(ps[:, 2 * t, :]), heads(ps[:, 2 * t + 1, :])
                tt(heads(vb[:, t, :]), v_, per_head(beta[:, sl], 8), ALU.mult)
                tt(heads(kbg[:, t, :]), k_, per_head(bg[:, sl], 8), ALU.mult)
                tt(heads(kdec[:, t, :]), k_, per_head(egs[:, sl], 8), ALU.mult)
            barrier()
            for b in range(4):
                t, par = b // 2, b % 2
                o = 4 * (b % 2)
                quad = lambda a: a.rearrange("p (j l) -> p j l", j=4)
                gc = small[:, SGC + 8 * t:SGC + 8 * t + 8].rearrange("p (a b) -> p a b", b=2)[:, :, par]
                d = A(DT + 512 * (b % 2), 4, P)
                dve.wait_ge(sem("dn_mm"), b + 1)
                tt(d, quad(ps[:, o, :]), gc.unsqueeze(2).broadcast_to([P, 4, P]), ALU.subtract)
                L.settle()
                tt(d, d, con("causal64_neg").unsqueeze(1).broadcast_to([P, 4, P]), ALU.add, sem("dn_seg"))
                dve.wait_ge(sem("dn_dec"), b + 1)
                lt = A(DLT + 512 * b, 4, P)
                tt(lt, quad(ps[:, o + 2, :]), d, ALU.mult)
                tt(A(DQK + 512 * b, 4, P), quad(ps[:, o + 3, :]), d, ALU.mult)
                L.settle()
                tt(lt, lt, quad(ps[:, o + 1, :]), ALU.mult, sem("dn_lt"))
            dve.wait_ge(sem("dn_egb"), 4)
            L.settle()
            for b in range(4):
                t, par = b // 2, b % 2
                lo = 64 * par
                q_ = qkvT[lo:lo + 64, 0:4, t * P:(t + 1) * P]
                tt(q_, q_, A(DEGB + 512 * b, 4, P)[lo:lo + 64], ALU.mult)
            L.settle()
            T, TTr = A(DT, 4, 512), A(DTT, 4, 512)
            for b in range(4):
                for m in (DT, DTT):
                    copy(A(m + 512 * b, 4, P), ident.unsqueeze(1).broadcast_to([P, 4, P]))
            barrier()
            N = 4 * len(LEVELS)

            def masked(n):
                b = n % 4
                if n >= 2:
                    dve.wait_ge(sem("dn_u"), n - 1)
                tt(A(DLM + 512 * (b % 2), 4, P), A(DLT + 512 * b, 4, P),
                   con(f"level{LEVELS[n // 4]}").unsqueeze(1).broadcast_to([P, 4, P]), ALU.mult, sem("dn_lm"))

            masked(0)
            masked(1)
            for n in range(N):
                b = n % 4
                dve.wait_ge(sem("dn_tu"), n + 1)
                tt(T[:, b, :], T[:, b, :], ps[:, 4 + 2 * (b % 2), :], ALU.subtract)
                tt(TTr[:, b, :], TTr[:, b, :], ps[:, 5 + 2 * (b % 2), :], ALU.subtract, sem("dn_T"))
                if n + 2 < N:
                    masked(n + 2)
            barrier()
            barrier()
            St, vn, uu = A(DST, 4, 64), A(DVN, 8, 64), A(DUU, TT, 512)
            o_ = A(DO, TT, 512)
            L(V.memset(A(DST, 256), 0.0))
            L.settle()
            L(V.memset(small[:, 638:639], 0.0), sem("dn_S"))
            for ci in range(4):
                t, pb = ci // 2, 64 * (ci % 2)
                dve.wait_ge(sem("dn_ws"), ci + 1)
                for par in range(2):
                    v4 = vn[pb:pb + 64].rearrange("p (a b) e -> p a b e", b=2)[:, :, par, :]
                    u4 = uu[pb:pb + 64, t, :].rearrange("p (a b e) -> p a b e", b=2, e=64)[:, :, par, :]
                    tt(v4, u4, ps[pb:pb + 64, par, 0:256].rearrange("p (a e) -> p a e", e=64), ALU.subtract,
                       sem("dn_vn") if par else None)
                for par in range(2):
                    lo = 64 * par
                    eg_ = A(DEGB + 512 * (2 * t + par), 4, P)[lo:lo + 64, :, pb + 63:pb + 64]
                    tt(St[lo:lo + 64], St[lo:lo + 64], eg_.broadcast_to([64, 4, 64]), ALU.mult)
                dve.wait_ge(sem("dn_su"), ci + 1)
                L.settle()
                tt(A(DST, 256), A(DST, 256), ps[:, 3, 0:256], ALU.add, sem("dn_S"))
                dve.wait_ge(sem("dn_o1"), ci + 1)
                tt(o_[pb:pb + 64, t, :], o_[pb:pb + 64, t, :], ps[pb:pb + 64, 2, :], ALU.add, sem("dn_o"))
            L.settle()
            sq = A(DLT, TT * 512)
            of = A(DO, TT * 512)
            tt(sq, of, of, ALU.mult)
            L.settle()
            L(V.tensor_reduce(small[:, 432:448], heads(sq), AX.X, ALU.add), sem("dn_oss"))
            dve.wait_ge(sem("dn_orstd"), 1)
            tt(heads(of), heads(of), per_head(small[:, 448:464]), ALU.mult)
            L.settle()
            tt(of, of, A(DGS, TT * 512), ALU.mult, sem("dn_gated"))
            dve.wait_ge(sem("ob_turned"), 1)
            for c in range(2):
                ts(A(DOUT, 4, 512)[:, 2 + c, :], ps[:, 4 + c, :], col("dn_norm_w_2"), ALU.mult,
                   s=sem("ob_out") if c else None)
            dve.wait_ge(lin_done, lin0("ab_out") + 2)
            residual(A(DLT, TT, D))
            barrier()
            modulation_take(3, col("norm_ffn_w_2", 0, 8))
            barrier()
            if upto < 10:
                return
            norm_apply(3)
            turned_h(3)
            barrier()
            hid = A(FH, 22, S)
            for c in range(6):
                for j in range(2 if c < 5 else 1):
                    g = 2 * c + j
                    dve.wait_ge(sem("sw_silu"), g + 1)
                    dve.wait_ge(lin_done, lin0("ffn") + (4 * c + 2 + j + 1 if c < 5 else 4 * c + 2))
                    tt(hid[:, 2 * g:2 * g + 2, :].rearrange("p a b -> p (a b)"), A(FT, 4, 512)[:, g % 4, :],
                       ps[:, 2 + j, :], ALU.mult, sem("sw_hidden"))
            modulation_slabs(4)
            dve.wait_ge(lin_done, lin0("ffn_down") + 6)
            residual(A(0, TT, D))
            barrier()
            modulation_take(4, col("norm_mix_w_2", 8, 8))
            barrier()

            if upto < 11:
                return
            norm_apply(4)
            turned_h(4)
            barrier()
            raw = A(LRAW, 8, 259)
            L(V.memset(raw[:, :, 0:3], 0.0))
            dve.wait_ge(sem("cd_out1"), 4)
            conv(raw, A(LX, KT, S), 4, "lru_conv_w_2", 8, 8, None, bias="lru_conv_b_2")
            L.settle()
            L(V.memset(small[:, 638:639], 0.0), sem("lru_step"))
            ts(small[:, 400:408], col("lru_lambda_2", 0, 8), -1.0, ALU.mult)
            softplus(small[:, 400:408], 8, small[:, 408:416])
            ts(small[:, 408:416], small[:, 408:416], -8.0, ALU.mult)
            dve.wait_ge(sem("cd_out1"), 14)
            B3 = A(LB, 12, S)
            pad = A(LRAW, 4, 258)
            L.settle()
            L(V.memset(pad[:, :, 0:2], 0.0))
            tt(pad[:, :, 2:258], B3[:, 4:8, :], B3[:, 8:12, :], ALU.mult)
            L.settle()
            yd = A(LOUT, 12, S)[:, 8:12, :]
            conv(pad, yd, 3, "sconv_w_2", 4, 4)
            L.settle()
            tt(yd, yd, B3[:, 0:4, :], ALU.mult)
            dve.wait_ge(sem("lru_gate"), 8)
            R, I_, Aa, H = (A(o, KT, S) for o in (LR, LI, LA, LH))
            for n in range(KT):
                ts(R[:, n, :], R[:, n, :], small[:, 408 + n:409 + n], ALU.mult, s=sem("lru_step") if n == KT - 1 else None)
            dve.wait_ge(sem("lru_gate"), 16)
            If, Af, Hf, Rf = (A(o, KT * S) for o in (LI, LA, LH, LR))
            tt(If, If, A(LX, KT * S), ALU.mult)
            dve.wait_ge(sem("lru_a"), 2)
            tt(Rf, Af, Af, ALU.mult)
            L.settle()
            stt(Rf, Rf, 1.0, Hf, ALU.add, ALU.mult)
            L.settle()
            ts(Rf, Rf, -1.0, ALU.mult, 0.0, ALU.max, s=sem("lru_step"))
            dve.wait_ge(sem("lru_a"), 3)
            tt(If, If, Rf, ALU.mult)
            L.settle()
            for n in range(KT):
                L(V.tensor_tensor_scan(H[:, n, :], Aa[:, n, :], I_[:, n, :], 0.0, ALU.mult, ALU.add))
            L.settle()
            tt(A(LOUT, KT * S), Hf, A(LY, KT * S), ALU.mult, sem("cd_ready"))
            modulation_slabs(5)
            barrier()
            dve.wait_ge(lin_done, lin0("cd_out") + 3)
            residual(A(LX, TT, D))
            barrier()
            modulation_take(5, col("norm_ffn_w_2", 8, 8))
            barrier()
            if upto < 12:
                return
            norm_apply(5)
            turned_h(5)
            barrier()
            dve.wait_ge(sem("routed"), 1)
            lg = small[:, 504:520].rearrange("p (t e) -> p t e", t=2)
            eq = small[:, 520:536].rearrange("p (t e) -> p t e", t=2)
            rank = con("eight_down").unsqueeze(1).broadcast_to([P, 2, 8])
            pick = [small[:, 536 + 16 * i:552 + 16 * i].rearrange("p (t e) -> p t e", t=2) for i in range(2)]
            top, best = [small[:, 568 + 2 * i:570 + 2 * i] for i in range(2)], small[:, 572:574]
            tt(lg, ps[:, 0, 0:16].rearrange("p (t e) -> p t e", t=2),
               spr("moe_router_b_2").unsqueeze(1).broadcast_to([P, 2, 8]), ALU.add)
            L.settle()
            for i in range(2):
                L(V.tensor_reduce(top[i], lg, AX.X, ALU.max))
                L.settle()
                tt(eq, lg, top[i].unsqueeze(2).broadcast_to([P, 2, 8]), ALU.is_equal)
                L.settle()
                tt(eq, eq, rank, ALU.mult)
                L.settle()
                L(V.tensor_reduce(best, eq, AX.X, ALU.max))
                L.settle()
                tt(pick[i], eq, best.unsqueeze(2).broadcast_to([P, 2, 8]), ALU.is_equal)
                L.settle()
                if i == 0:
                    stt(lg, pick[0], 2.0 * NEG, lg, ALU.mult, ALU.add)
                    L.settle()
            tt(small[:, 502:504], top[1], top[0], ALU.subtract, sem("routing"))
            dve.wait_ge(sem("gate_exp"), 2)
            ex, w1 = small[:, 500:502], small[:, 574:576]
            ts(w1, ex, 1.0, ALU.add)
            L.settle()
            L(V.reciprocal(w1, w1))
            L.settle()
            tt(ex, ex, w1, ALU.mult)
            L.settle()
            mask = A(MO, TT, EXPERTS)
            tt(mask, pick[0], pick[1], ALU.add, sem("routing"))
            L.settle()
            tt(pick[0], pick[0], w1.unsqueeze(2).broadcast_to([P, 2, 8]), ALU.mult)
            tt(pick[1], pick[1], ex.unsqueeze(2).broadcast_to([P, 2, 8]), ALU.mult)
            L.settle()
            slot_of, gate_of = routes[:, 0], routes[:, 1]
            for r in range(TT):
                tt(gate_of[:, :, r * EXPERTS:(r + 1) * EXPERTS], pick[0], pick[1], ALU.add)
            L(V.memset(gate_of[:, :, ROUNDS:], 0.0))
            L(V.memset(slot_of[:, :, ROUNDS:], -1.0))
            dve.wait_ge(sem("routed"), 2)
            ranks = ps[:, 1, 0:16].rearrange("p (t e) -> p t e", t=2)
            tt(lg, ranks, mask, ALU.mult)
            L(V.tensor_reduce(best[:, 0:1], ps[:, 1, 16:24], AX.X, ALU.max))
            L.settle()
            for r in range(TT):
                ts(slot_of[:, :, r * EXPERTS:(r + 1) * EXPERTS], lg, -1.0 - P * r, ALU.add)
            ts(best[:, 1:2], best[:, 0:1], P + 0.5, ALU.is_gt, 1.0 * EXPERTS, ALU.mult)
            L.settle()
            ts(best[:, 0:1], best[:, 1:2], 1.0 * EXPERTS, ALU.add)
            L.settle()
            copy(rounds[:], best, sem("routing"))
            acc = A(MO, TT, D)
            L.settle()
            select, gated = A(ESEL, TT, P), A(EGATED, TT, P)

            def build_selection(i):
                for t in range(TT):
                    ins = V.tensor_scalar(select[:, t, :], con("slot_number"), slot_of[:, t, bass.ds(i, 1)], None,
                                          ALU.is_equal)
                return ins

            build_selection(0).then_inc(sem("selected"), 1)
            L(V.memset(A(EY, D), 0.0), sem("expert_out"))
            L(V.memset(A(ETURN, TT * P), 0.0), sem("expert_out"))
            L(V.memset(acc, 0.0), sem("moe_added"))
            gathered = A(EG, KT, P)

            def modulate():
                for k in range(KT // 2, KT):
                    ins = V.tensor_scalar(gathered[:, k, :], ps[:, 1, (k - 4) * P:(k - 3) * P], shift[:, k:k + 1],
                                          shift[:, KT + k:KT + k + 1], ALU.mult, ALU.add)
                ins.then_inc(sem("gathered_ready"), 1)

            def add_output(i, t):
                for h in range(2):
                    dve.wait_ge(sem("scattered"), i * 4 + (2 * t + h + 1))
                    sl = slice(h * 512, (h + 1) * 512)
                    V.tensor_tensor(acc[:, t, sl], acc[:, t, sl], ps[:, 6 + h, :], ALU.add
                                    ).then_inc(sem("moe_added"), 1)

            n_rounds = dve.value_load(rounds[0:1, 0:1], min_val=EXPERTS, max_val=ROUNDS)
            dve.wait_ge(sem("gathered"), 1)
            modulate()
            with dve.Fori(0, n_rounds) as i:
                build_selection(i + 1)
                for t in range(TT):
                    ins = V.tensor_scalar(gated[:, t, :], con("slot_number"), slot_of[:, t, bass.ds(i, 1)],
                                          gate_of[:, t, bass.ds(i, 1)], ALU.is_equal, ALU.mult)
                ins.then_inc(sem("selected"), 1)
                dve.wait_ge(sem("moe_added"), i * 4 + 1)
                add_output(i, 0)
                for f in range(GU):
                    dve.wait_ge(sem("moe_silu"), i * GU + (f + 1))
                    dve.wait_ge(lin_done, i * E_CHUNKS + (plan.steps + 2 * f + 2))
                    if f >= 2:
                        dve.wait_ge(sem("hidden_turned"), i * GU + (f - 1))
                    V.tensor_tensor(A(EH, 2, 512)[:, f % 2, :], A(ES, 2, 512)[:, f % 2, :], ps[:, 2 + f % 2, :], ALU.mult
                                    ).then_inc(sem("moe_hidden"), 1)
                    if f == 0:
                        add_output(i, 1)
                dve.wait_ge(sem("gathered"), i + 2)
                modulate()
                dve.wait_ge(lin_done, i * E_CHUNKS + (plan.steps + E_CHUNKS))
                V.tensor_copy(A(EY, D)[:, 512:1024], ps[:, 5, :]).then_inc(sem("expert_out"), 1)
            dve.wait_ge(sem("moe_added"), n_rounds * 4 + 1)
            add_output(n_rounds, 0)
            add_output(n_rounds, 1)
            barrier()
            tt(acc[:, 0, :], acc[:, 0, :], gain[:], ALU.mult)
            tt(acc[:, 1, :], acc[:, 1, :], gain[:], ALU.mult)
            L.settle()
            tt(x[:], x[:], acc, ALU.add, sem("x_final"))
            L(V.memset(small[:, 638:639], 0.0), sem("x_final"))
            dve.wait_ge(sem("final_w_in"), 16)
            dve.wait_ge(sem("norm_rstd"), 7)
            for t in range(TT):
                stt(A(0, TT, D)[:, t, :], x[:, t, :], small[:, 602 + t:603 + t], A(2048, D), ALU.mult, ALU.mult,
                    sem("final_scaled"))


_INS = [
    "x", "c", "w_ada", "b_ada", "norm1_w", "norm2_w", "w_in", "conv_w", "conv_b", "dt_bias", "a_log", "d_skip",
    "ssd_norm_w", "w_ssd_out", "q_norm_w", "k_norm_w", "w_attn_out", "w_pool_mix", "pool_scale", "w_pool_out",
    "w_out", "w_ff1", "w_ff2", "c_2", "rel_bias_2", "ada_w_2", "ada_b_2", "norm_mix_w_2", "norm_ffn_w_2",
    "final_norm_w_2", "ab_w_in_2", "attn_sinks_2", "dn_conv_w_2", "dn_a_log_2", "dn_dt_bias_2", "dn_norm_w_2",
    "ab_w_out_2", "ffn_w_gate_2", "ffn_w_up_2", "ffn_w_down_2", "cd_w_in_2", "lru_conv_w_2", "lru_conv_b_2",
    "lru_gate_a_w_2", "lru_gate_a_b_2", "lru_gate_x_w_2", "lru_gate_x_b_2", "lru_lambda_2", "sconv_w_2",
    "cd_w_out_2", "moe_router_w_2", "moe_router_b_2", "moe_w_gate_2", "moe_w_up_2", "moe_w_down_2",
]


def program(nc, shapes, **kw):
    w = {n: nc.dram_tensor(f"in_{n}", shapes[n], F32, kind="ExternalInput").ap() for n in _INS}
    consts, at = constant_columns()
    consts_dram = nc.dram_tensor("in_consts", consts.shape, F32, kind="ExternalInput").ap()
    out = nc.dram_tensor("out_0", (1, S, D), F32, kind="ExternalOutput").ap()
    scratch = nc.dram_tensor("bias_lines", (P, 8, 384), F32, kind="Internal").ap()
    build(nc, w, consts_dram, at, out, scratch, **kw)
    return consts


def kernel(**inputs):
    import concourse.bacc as _bacc
    from concourse.bass_utils import run_bass_kernel_spmd as _run

    nc = _bacc.Bacc("TRN2", target_bir_lowering=False, num_devices=1)
    arrays = {f"in_{n}": np.ascontiguousarray(inputs[n]) for n in _INS}
    arrays["in_consts"] = program(nc, {n: inputs[n].shape for n in _INS})
    r = _run(nc, [arrays], core_ids=[0])
    return r.results[0]["out_0"]
```

```python
import math
from contextlib import ExitStack

import numpy as np

import concourse.bass as bass
from concourse import mybir

P = 128
F32 = mybir.dt.float32
F32R = mybir.dt.float32r
ACT = mybir.ActivationFunctionType
ALU = mybir.AluOpType
AX = mybir.AxisListType

D = 1024
S = 256
KT = D // P
TT = S // P
NEG = -1.0e30
EPS = 1e-6

HEADS = 12
DILATIONS = (1, 4, 16)
SPANS = (128, 128, 128)
POOL_WINDOWS = (2, 4, 8, 16)
LEVELS = (1, 2, 4, 8, 16, 32)
F_EXPERT = 3584
EXPERTS = 8
ROUNDS = TT * EXPERTS


def alibi_slopes(n):
    def pow2(k):
        start = 2.0 ** (-8.0 / k)
        return [start ** (i + 1) for i in range(k)]
    if math.log2(n).is_integer():
        s = pow2(n)
    else:
        c = 2 ** math.floor(math.log2(n))
        s = pow2(c) + pow2(2 * c)[0::2][: n - c]
    return np.sort(np.asarray(s, np.float32))[::-1].copy()


def constant_columns():
    k = np.arange(P)[:, None]
    m = np.arange(P)[None, :]
    block = (k // 64) == (m // 64)
    parts = {
        "ident": (k == m),
        "ones": np.ones((P, P)),
        "until": (k <= m),
        "after": (k > m),
        "until64": (k <= m) & block,
        "after64": (k > m) & block,
        "block64": block,
        "causal_neg": np.where(k <= m, 0.0, NEG),
        "causal64_neg": np.where((k <= m) & block, 0.0, NEG),
        "eps": np.full((P, 1), EPS),
        "eight_down": np.tile(8.0 - np.arange(8), (P, 1)),
        "slot_number": np.tile(np.arange(P) * 1.0, (P, 1)),
    }
    for w in LEVELS:
        parts[f"level{w}"] = ((k // (2 * w)) == (m // (2 * w))) & (m % (2 * w) >= w) & (k % (2 * w) < w)
    for g, w in enumerate(POOL_WINDOWS):
        lag = m - k
        parts[f"pool_first{g}"] = ((lag >= 0) & (lag < w)) / np.minimum(m + 1.0, w) - (lag == 0)
        parts[f"pool_same{g}"] = ((lag >= 0) & (lag < w)) / float(w) - (lag == 0)
        parts[f"pool_prev{g}"] = ((lag + P >= 0) & (lag + P < w)) / float(w)
    for t in range(TT):
        for g, (dil, span) in enumerate(zip(DILATIONS, SPANS)):
            s = np.arange((t + 1) * P)[None, :]
            dist = (t * P + k) - s
            seen = (dist >= 0) & (dist % dil == 0) & (dist // dil <= span)
            parts[f"dist{t}{g}"] = np.where(seen, dist, -NEG)
    dist = 255 - np.arange(383)
    large = 16 + (np.log(np.maximum(dist, 1) / 16) / math.log(128 / 16) * 16).astype(np.int32)
    bucket = np.where(dist < 16, np.maximum(dist, 0), np.minimum(large, 31))
    seen = (dist >= 0) & (dist < 128)
    line = np.zeros((P, 383))
    line[:32] = (bucket[None, :] == np.arange(32)[:, None]) & seen[None, :]
    line[32] = ~seen
    parts["bucket_line"] = line
    at, cols, n = {}, [], 0
    for name, a in parts.items():
        a = np.asarray(a, np.float32)
        at[name] = (n, a.shape[1])
        n += a.shape[1]
        cols.append(a)
    return np.ascontiguousarray(np.concatenate(cols, 1)), at


def row_plan():
    tiles = [
        [("norm1_w", 8), ("norm2_w", 8), ("conv_w", 48), ("conv_b", 12), ("ssd_norm_w", 8),
         ("q_norm_w", 1), ("k_norm_w", 1), ("pool_scale", 8)],
        [("norm_mix_w_2", 16), ("norm_ffn_w_2", 16), ("dn_conv_w_2", 48), ("lru_conv_w_2", 32)],
        [("lru_conv_b_2", 8), ("lru_gate_a_b_2", 8), ("lru_gate_x_b_2", 8), ("lru_lambda_2", 8),
         ("sconv_w_2", 12), ("dn_norm_w_2", 1)],
    ]
    at = {}
    for i, t in enumerate(tiles):
        r = 0
        for name, n in t:
            at[name] = (i, r, n)
            r += n
        assert r <= P
    return at, [sum(n for _, n in t) for t in tiles]


RING = 3
SLOT = 4096


class Plan:

    def __init__(self):
        self.chunks = []
        self.stage = {}
        self.steps = 0

    def add(self, name, chunks):
        self.stage[name] = (len(self.chunks), self.steps)
        for pieces, kt, n, steps in chunks:
            self.steps += steps
            self.chunks.append((pieces, kt, n, self.steps))


def rows_of(w, r0, kt, c0, n):
    return w[r0:r0 + kt * P, c0:c0 + n].rearrange("(k p) n -> p k n", p=P)


def make_plan(w):
    plan = Plan()

    def wide(name, a, c0, n, per):
        out = []
        for c in range(0, n, 512):
            m = min(512, n - c)
            out.append(([(0, rows_of(a, 0, KT, c0 + c, m))], KT, m, per(m)))
        plan.add(name, out)

    def down(name, a, rows, steps=1):
        out = []
        for r in range(0, rows, 512):
            kt = min(4, (rows - r) // P)
            out.append(([(0, rows_of(a, r, kt, 0, D))], kt, D, steps))
        plan.add(name, out)

    tok = lambda m: TT
    feat = lambda m: (m // P + 1) // 2
    w_in = w["w_in"][0]
    wide("q", w_in, 2576, 1536, feat)
    wide("k", w_in, 4112, 1536, feat)
    wide("v", w_in, 5648, 1536, tok)
    wide("gate_attn", w_in, 8208 + 1024, 1024, tok)
    down("attn_out", w["w_attn_out"][0], 512)
    wide("u", w_in, 7184, 1024, tok)
    plan.add("pool_mix", [([(0, w["w_pool_mix"][0].rearrange("g (k p) o -> p (g k) o", p=P))], 8, 256, 4)])
    wide("gate_pool", w_in, 8208 + 2048, 1024, tok)
    down("pool_out", w["w_pool_out"][0], 1024)
    wide("xbc", w_in, 1024, 1536, feat)
    wide("dt", w_in, 2560, 16, tok)
    wide("z", w_in, 0, 1024, tok)
    wide("gate_ssd", w_in, 8208, 1024, tok)
    down("ssd_out", w["w_ssd_out"][0], 1024)
    down("mix_out", w["w_out"][0], 1024)
    wide("ff1", w["w_ff1"][0], 0, 4096, feat)
    down("ff2", w["w_ff2"][0], 4096)

    ab = w["ab_w_in_2"][0]
    wide("qa", ab, 0, 512, feat)
    wide("kva", ab, 512, 256, lambda m: 3)
    wide("qkv_b", ab, 768, 1536, feat)
    wide("gate_b", ab, 2304, 512, tok)
    wide("ba", ab, 2816, 16, tok)
    down("ab_out", w["ab_w_out_2"][0], 1024)
    gate, up = w["ffn_w_gate_2"][0], w["ffn_w_up_2"][0]
    both = []
    for c in range(0, 2816, 512):
        m = min(512, 2816 - c)
        both += [([(0, rows_of(a, 0, KT, c, m))], KT, m, feat(m)) for a in (gate, up)]
    plan.add("ffn", both)
    down("ffn_down", w["ffn_w_down_2"][0], 2816)
    wide("cd_in", w["cd_w_in_2"][0], 0, 3584, feat)
    plan.add("lru_gates", [([(0, w["lru_gate_a_w_2"][0].rearrange("n i j -> i n j")),
                             (8 * P, w["lru_gate_x_w_2"][0].rearrange("n i j -> i n j"))], 16, P, 8)])
    down("cd_out", w["cd_w_out_2"][0], 1536, 2)
    return plan


def alloc_views(arena):
    def at(off, *shape):
        n = int(np.prod(shape))
        v = arena[:, off:off + n]
        if len(shape) == 2:
            v = v.rearrange("p (a b) -> p a b", b=shape[1])
        if len(shape) == 3:
            v = v.rearrange("p (a b c) -> p a b c", b=shape[1], c=shape[2])
        return v
    return at


class Lane:

    def __init__(self, eng, step):
        self.eng, self.step, self.count, self.last = eng, step, {}, None

    def __call__(self, ins, sem=None):
        sem = sem or self.step
        ins.then_inc(sem, 1)
        self.count[sem.name] = self.count.get(sem.name, 0) + 1
        self.last = (sem, self.count[sem.name])

    def settle(self):
        self.eng.wait_ge(*self.last)


QT, KTT, VT = 4096, 7168, 10240
QSQ, QRS = 13312, 14336
AS_, AP_, APT, AOT = 13312, 14848, 16384, 17920
PU, PP, PM = 4096, 6144, 8192
SRAW, SX, SZ, SXC, SXX, SXD, SB, SST, SCB = 4096, 7204, 10276, 12324, 14372, 16420, 17444, 17700, 18724
SE = SRAW
FH, FT = 2048, 10240
XN, EG, EH, ES, ESEL, EGATED, ETURN, EY, MO = 10240, 12288, 13312, 14336, 15360, 15616, 15872, 16128, 17152
DOUT, DQKV, DGS = 0, 2048, 5120
WQ, WK, WV, WRAW, T5_OFF, WS, WPT = 6144, 7168, 7680, 7936, 11044, 13092, 14116
DVB, DKBG, DKDEC, DEGB, DQK, DLT, DT, DTT = 6144, 7168, 8192, 9216, 11264, 13312, 15360, 17408
DLM, DU = DQKV + 1024, DQKV + 2048
DUU, DWT, DQD, DST, DVN, DO = DLT, DLT + 1024, DQKV, DT + 1024, DT + 1280, DLM
LOUT, LRAW, LX, LY, LB, LR, LI, LA = 0, 3072, 5144, 7192, 9240, 12312, 14360, 16408
LH = LB
ARENA = 19456
SG, SBETA, SGC, SEG = 224, 240, 256, 272

UNITS = 6
SLAB = 3072


def build(nc, w, consts_dram, const_at, out, scratch):
    with ExitStack() as ctx:
        def sb(name, *shape):
            return ctx.enter_context(nc.sbuf_tensor(name, [P, *shape], F32))

        sems = {}

        def sem(name):
            if name not in sems:
                sems[name] = ctx.enter_context(nc.semaphore(name))
            return sems[name]

        n_const = sum(n for _, n in const_at.values())
        consts = sb("consts", n_const)
        ring = sb("ring", RING, SLOT)
        x = sb("x", TT, D)
        hT = sb("hT", KT, S)
        gain = sb("gain", D)
        shift = sb("shift", 2, 2 * KT)
        row_at, row_n = row_plan()
        cols = sb("cols", len(row_n), P)
        spread = sb("spread", 128)
        router = sb("router", KT, EXPERTS)
        small = sb("small", 640)
        rounds = ctx.enter_context(nc.sbuf_tensor("rounds", [P, 2], mybir.dt.int32))
        routes = sb("routes", 2, TT, ROUNDS + 1)
        with ExitStack() as early:
            slab, ada, arena_t = (early.enter_context(nc.sbuf_tensor(name, [P, *shape], F32))
                                  for name, shape in (("slab", (2, SLAB)), ("ada", (SLAB,)), ("arena", (ARENA,))))

        def split_sb(name, *shape):
            return ctx.enter_context(nc.sbuf_tensor(name, [P, *shape], F32R))

        HALF = SLOT // 2
        w_high, w_low = split_sb("w_high", 3, HALF), split_sb("w_low", 2, HALF)
        tokens_hl = split_sb("tokens_hl", 2, KT, P)
        hidden_hl = split_sb("hidden_hl", 2, F_EXPERT // P, P)
        assert 5 * HALF + 2 * (KT + F_EXPERT // P) * P <= 3 * SLAB + XN
        ps = ctx.enter_context(nc.psum_tensor("ps", [P, 8, 512], F32))
        A = alloc_views(arena_t)

        def con(name):
            o, n = const_at[name]
            return consts[:, o:o + n]

        def col(name, i=0, n=1):
            t, r, m = row_at[name]
            assert i + n <= m
            return cols[:, t, r + i:r + i + n]

        ident, ones = con("ident"), con("ones")
        plan = make_plan(w)
        slopes = alibi_slopes(HEADS)

        SPREAD = {"dt_bias": (0, 16), "a_log": (16, 16), "d_skip": (32, 16), "attn_sinks_2": (48, 8),
                  "dn_a_log_2": (56, 8), "dn_dt_bias_2": (64, 8), "moe_router_b_2": (72, 8)}

        def spr(name):
            o, n = SPREAD[name]
            return spread[:, o:o + n]

        lin_done = sem("lin_done")
        w_landed = [sem(f"w_landed{s}") for s in range(RING)]
        stage_end = sem("stage_end")
        params_in = sem("params_in")
        rows_in = sem("rows_in")
        x_in = sem("x_in")
        out_written = sem("out_written")

        def lin0(name):
            return plan.stage[name][1]

        block = ctx.enter_context(nc.Block())
        N_BAR = 3

        def barrier_of(eng):
            n = [0]

            def barrier():
                n[0] += 1
                eng.drain().then_inc(stage_end, 1)
                eng.wait_ge(stage_end, N_BAR * n[0])
            return barrier

        GU = F_EXPERT // 512
        E_CHUNKS = 3 * GU
        E_STEPS = 2 * E_CHUNKS

        def half_of(m):
            a = (m % 2) * HALF
            return ring[:, e_slot(m // 2), a:a + HALF], w_high[:, m % 3, :], w_low[:, m % 2, :]

        def e_slot(c):
            return (len(plan.chunks) + c) % RING

        moe_gate, moe_up, moe_down = w["moe_w_gate_2"][0], w["moe_w_up_2"][0], w["moe_w_down_2"][0]

        @block.sync
        def _(sp):
            for name, (t, r, n) in row_at.items():
                if name == "dn_norm_w_2":
                    for h in range(2):
                        sp.dma_start(A(0, 3, P)[r:r + 1, t, 64 * h:64 * h + 64], w[name]).then_inc(rows_in, 16)
                    continue
                src = w[name].flatten().rearrange("(r p) -> r p", p=P)
                sp.dma_start(A(0, 3, P)[r:r + n, t, :], src).then_inc(rows_in, 16)
            sp.dma_start(consts[:], consts_dram).then_inc(params_in, 16)
            for t in range(TT):
                sp.dma_start(x[:, t, :], w["x"][0, t * P:(t + 1) * P, :]).then_inc(x_in, 16)
            for name in SPREAD:
                sp.dma_start(spr(name), w[name].broadcast_to([P, SPREAD[name][1]])).then_inc(params_in, 16)
            sp.dma_start(router[:], w["moe_router_w_2"][0].rearrange("(k p) e -> p k e", p=P)).then_inc(params_in, 16)
            sp.dma_start(A(500, 8)[0:32, :], w["rel_bias_2"]).then_inc(rows_in, 16)
            for i, (pieces, kt, n, _) in enumerate(plan.chunks):
                if i >= RING:
                    sp.wait_ge(lin_done, plan.chunks[i - RING][3])
                else:
                    sp.wait_ge(sem("slab_used"), KT - 2 + i)
                for off, src in pieces:
                    m = src.shape[1] * src.shape[2]
                    dst = ring[:, i % RING, off:off + m].rearrange("p (k n) -> p k n", n=src.shape[2])
                    sp.dma_start(dst, src).then_inc(w_landed[i % RING], 16)

            down_rows = moe_down.rearrange("e f d -> (e f) d")

            def expert_chunk(e, c):
                if c < 2 * GU:
                    a = (moe_gate, moe_up)[c % 2]
                    src = a[e, :, (c // 2) * 512:(c // 2 + 1) * 512].rearrange("(k p) n -> p k n", p=P)
                else:
                    src = down_rows[bass.ds(e * F_EXPERT + (c - 2 * GU) * 512, 512), :].rearrange("(k p) n -> p k n", p=P)
                dst = ring[:, e_slot(c), :].rearrange("p (k n) -> p k n", n=src.shape[2])
                sp.dma_start(dst, src).then_inc(w_landed[e_slot(c)], 16)

            def expert_weights(before, e, from_chunk=0):
                for c in range(from_chunk, E_CHUNKS):
                    sp.wait_ge(sem("low_ready"), e * E_STEPS + (before * E_STEPS + 2 * (c - RING + 1)))
                    expert_chunk(e, c)

            for c in range(RING):
                sp.wait_ge(lin_done, plan.chunks[len(plan.chunks) - RING + c][3])
                expert_chunk(0, c)
            expert_weights(0, 0, RING)
            with sp.Fori(1, EXPERTS) as e:
                expert_weights(0, e)
            sp.wait_ge(sem("vector2"), 6)
            more = sp.value_load(rounds[0:1, 1:2], min_val=0, max_val=EXPERTS)
            with sp.If(more > 0):
                with sp.Fori(0, EXPERTS) as e:
                    expert_weights(EXPERTS, e)
            sp.end_ifs()
            sp.wait_ge(sem("final_scaled"), TT)
            for t in range(TT):
                sp.dma_start(out[0, t * P:(t + 1) * P, :], A(0, TT, D)[:, t, :]).then_inc(out_written, 16)
            sp.wait_ge(out_written, 16 * TT)

        landed_at = []
        uses = [0] * RING
        for i, (pieces, *_) in enumerate(plan.chunks):
            uses[i % RING] += len(pieces)
            landed_at.append(16 * uses[i % RING])
        N_ROWS = 16 * (len(row_at) + 2)
        N_PARAMS = 16 * (2 + len(SPREAD))

        ada_w = [w["w_ada"][0], w["ada_w_2"][0], w["ada_w_2"][1]]
        ada_b = [w["b_ada"][0], w["ada_b_2"][0], w["ada_b_2"][1]]

        @block.gpsimd
        def _(pool):
            for u in range(UNITS):
                pool.wait_ge(sem("ada_clear"), u + 1)
                src = ada_b[u // 2][(u % 2) * SLAB:(u % 2 + 1) * SLAB]
                pool.dma_start(ada[0:1, :], src.rearrange("(a n) -> a n", a=1)).then_inc(sem("ada_bias"), 16)
                for k in range(KT):
                    i = u * KT + k
                    if i >= 2:
                        pool.wait_ge(sem("slab_used"), i - 1)
                    rows = ada_w[u // 2].rearrange("(p k) n -> p k n", p=P)[:, k, (u % 2) * SLAB:(u % 2 + 1) * SLAB]
                    pool.dma_start(slab[:, i % 2, :], rows).then_inc(sem(f"slab_in{i % 2}"), 16)
                if u == 3:
                    pool.wait_ge(sem("line_out"), 16)
                    pool.wait_ge(sem("bias_wanted"), 1)
                    skew = bass.AP(tensor=scratch.tensor, offset=127, ap=[[8 * 384 - 1, P], [384, 8], [1, 256]])
                    pool.dma_start(A(T5_OFF, 8, 256), skew).then_inc(sem("bias_in"), 16)

        @block.tensor
        def _(pe):
            barrier = barrier_of(pe)

            def weights(name, c):
                i = plan.stage[name][0] + c
                pieces, kt, n, _ = plan.chunks[i]
                pe.wait_ge(w_landed[i % RING], landed_at[i])
                return ring[:, i % RING, 0:kt * n].rearrange("p (k n) -> p k n", n=n)

            def token_product(name, evacuated, lhs=hT, g0=0):
                g = g0
                n_chunks = {"v": 3, "gate_attn": 2, "u": 2, "gate_pool": 2, "dt": 1, "z": 2, "gate_ssd": 2,
                            "gate_b": 1, "ba": 1}[name]
                for c in range(n_chunks):
                    wt = weights(name, c)
                    n = wt.shape[2]
                    for t in range(TT):
                        if g >= 4:
                            pe.wait_ge(evacuated, g - 3)
                        for k in range(KT):
                            mm = pe.matmul(ps[:, g % 4, 0:n], lhs[:, k, t * P:(t + 1) * P], wt[:, k, :],
                                           start=(k == 0), stop=(k == KT - 1))
                        mm.then_inc(lin_done, 1)
                        g += 1

            def feature_pair(wt, j, bank, rhs=hT, last=True):
                tiles = min(2, wt.shape[2] // P - 2 * j)
                for i in range(tiles):
                    for k in range(KT):
                        mm = pe.matmul(ps[:, bank, i * S:(i + 1) * S], wt[:, k, (2 * j + i) * P:(2 * j + i + 1) * P],
                                       rhs[:, k, :], start=(k == 0), stop=(k == KT - 1))
                mm.then_inc(lin_done, 1)

            def down_product(name, n_chunks, lhs, unit=None):
                total = sum(plan.chunks[plan.stage[name][0] + c][1] for c in range(n_chunks))
                k0 = 0
                for c in range(n_chunks):
                    wt = weights(name, c)
                    if unit and c == n_chunks - 1:
                        modulation_columns(unit)
                    for t in range(TT):
                        for h in range(2):
                            for k in range(wt.shape[1]):
                                mm = pe.matmul(ps[:, 4 + 2 * t + h, :], lhs(k0 + k, t), wt[:, k, h * 512:(h + 1) * 512],
                                               start=(k0 + k == 0), stop=(k0 + k == total - 1))
                    mm.then_inc(lin_done, 2 if name == "cd_out" else 1)
                    k0 += wt.shape[1]

            def modulation_columns(u):
                pe.wait_ge(sem("ada_ready"), u + 1)
                for j in range(2 * KT):
                    mm = pe.matmul(ps[:, 0, j:j + 1], ada[:, j * P:(j + 1) * P], ones[:, 0:1], start=True, stop=True)
                mm.then_inc(sem("mod_summed"), 1)

            def modulation_gain():
                for h in range(2):
                    mm = pe.matmul(ps[:, 2 + h, :], ones, ada[:, 2 * D + h * 512:2 * D + (h + 1) * 512],
                                   start=True, stop=True)
                mm.then_inc(sem("mod_summed"), 1)

            def turn_all(src, sem_in, n_in, sem_out):
                pe.wait_ge(sem_in, n_in)
                for k in range(KT):
                    for t in range(TT):
                        mm = pe.transpose(ps[:, 4 + k // 2, (k % 2) * S + t * P:(k % 2) * S + (t + 1) * P],
                                          src[:, t, k * P:(k + 1) * P], ident)
                mm.then_inc(sem_out, 1)

            pe.wait_ge(rows_in, N_ROWS)
            pe.wait_ge(params_in, N_PARAMS)
            for i, n in enumerate(row_n):
                mm = pe.transpose(ps[:, 0, i * P:i * P + n], A(0, 3, P)[0:n, i, :], ident[0:n, 0:n])
            mm.then_inc(sem("line_mm"), 1)
            pe.wait_ge(sem("line_lhs"), 1)
            for h in range(8):
                if h >= 2:
                    pe.wait_ge(sem("bias_line"), h - 1)
                pe.matmul(ps[:, 2 + h % 2, 0:383], A(1024, 8, P)[0:33, h, :], con("bucket_line")[0:33, :],
                          start=True, stop=True).then_inc(sem("line_mm"), 1)
            modulation_columns(0)
            barrier()
            turn_all(A(0, TT, D), sem("x_scaled"), TT, sem("h_turned"))
            modulation_gain()
            barrier()

            g = 0
            for name in ("q", "k"):
                for c in range(3):
                    wt = weights(name, c)
                    for j in range(2):
                        if g >= 4:
                            pe.wait_ge(sem("qk_raw"), g - 3)
                        feature_pair(wt, j, g % 4)
                        if g >= 1:
                            pe.wait_ge(sem("qk_raw"), g)
                            if g >= 3:
                                pe.wait_ge(sem("qk_rstd"), g - 2)
                            pe.matmul(ps[:, 4 + (g - 1) % 2, :], ones, A(QSQ, 2, 512)[:, (g - 1) % 2, :],
                                      start=True, stop=True).then_inc(sem("qk_ss"), 1)
                        g += 1
            pe.wait_ge(sem("qk_raw"), g)
            pe.wait_ge(sem("qk_rstd"), g - 2)
            pe.matmul(ps[:, 4 + (g - 1) % 2, :], ones, A(QSQ, 2, 512)[:, (g - 1) % 2, :],
                      start=True, stop=True).then_inc(sem("qk_ss"), 1)
            token_product("v", sem("v_out"))
            barrier()

            qT, kT, v = A(QT, HEADS, S), A(KTT, HEADS, S), A(VT, TT, HEADS * P)

            def attn_scores(i):
                j, t = i // 2, i % 2
                n = (t + 1) * P
                if i >= 2:
                    pe.wait_ge(sem("at_masked"), i - 1)
                for g in range(3):
                    h = 4 * g + j
                    if t == 0:
                        o = ps[:, 2 * (i % 2), g * P:(g + 1) * P]
                    else:
                        o = ps[:, 2 * (i % 2) + g // 2, (g % 2) * S:(g % 2 + 1) * S]
                    mm = pe.matmul(o, qT[:, h, t * P:(t + 1) * P], kT[:, h, 0:n], start=True, stop=True)
                mm.then_inc(sem("at_scores"), 1)

            def attn_apply(i):
                j, t = i // 2, i % 2
                n = 3 * (t + 1)
                pe.wait_ge(sem("at_probs"), i + 1)
                if i >= 1:
                    pe.wait_ge(sem("at_turned"), i)
                for b in range(n):
                    mm = pe.transpose(ps[:, 4 + b // 4, (b % 4) * P:(b % 4 + 1) * P],
                                      A(AP_, 2, 768)[:, i % 2, b * P:(b + 1) * P], ident)
                mm.then_inc(sem("at_pT"), 1)
                pe.wait_ge(sem("at_turned"), i + 1)
                if i >= 2:
                    pe.wait_ge(sem("at_out"), i - 1)
                b = 0
                for g in range(3):
                    for s in range(t + 1):
                        mm = pe.matmul(ps[:, 6 + i % 2, 0:P], v[:, s, (4 * g + j) * P:(4 * g + j + 1) * P],
                                       A(APT, 2, 768)[:, i % 2, b * P:(b + 1) * P], start=(b == 0), stop=(b == n - 1))
                        b += 1
                mm.then_inc(sem("at_pv"), 1)

            attn_scores(0)
            for i in range(8):
                if i < 7:
                    attn_scores(i + 1)
                attn_apply(i)
            barrier()

            oT = A(AOT, 4, S)
            token_product("gate_attn", sem("ga_out"))
            down_product("attn_out", 1, lambda k, t: oT[:, k, t * P:(t + 1) * P])
            barrier()

            token_product("u", sem("u_out"))
            pe.wait_ge(sem("u_out"), 4)
            u = A(PU, TT, D)
            for c in range(KT):
                g, bank, o = c // 2, 4 + c // 2, (c % 2) * S
                pe.matmul(ps[:, bank, o:o + P], u[:, 0, c * P:(c + 1) * P], con(f"pool_first{g}"), start=True, stop=True)
                pe.matmul(ps[:, bank, o + P:o + S], u[:, 0, c * P:(c + 1) * P], con(f"pool_prev{g}"),
                          start=True, stop=False)
                mm = pe.matmul(ps[:, bank, o + P:o + S], u[:, 1, c * P:(c + 1) * P], con(f"pool_same{g}"),
                               start=False, stop=True)
                if c % 2:
                    mm.then_inc(sem("pooled"), 1)
            wt = weights("pool_mix", 0)
            pT = A(PP, KT, S)
            for g in range(4):
                pe.wait_ge(sem("pooled_out"), g + 1)
                for o in range(2):
                    for k in range(2):
                        mm = pe.matmul(ps[:, g, o * S:(o + 1) * S], wt[:, 2 * g + k, o * P:(o + 1) * P],
                                       pT[:, 2 * g + k, :], start=(k == 0), stop=(k == 1))
                mm.then_inc(lin_done, 1)
            pe.wait_ge(sem("pool_mixed"), 4)
            token_product("gate_pool", sem("gp_out"))
            mT = A(PM, KT, S)
            down_product("pool_out", 2, lambda k, t: mT[:, k, t * P:(t + 1) * P])
            barrier()

            for g in range(6):
                if g % 2 == 0:
                    wt = weights("xbc", g // 2)
                if g >= 4:
                    pe.wait_ge(sem("xbc_out"), g - 3)
                feature_pair(wt, g % 2, g % 4)
            pe.wait_ge(sem("xbc_out"), 6)
            token_product("dt", None)
            pe.wait_ge(sem("dt_out"), 2)
            token_product("z", sem("z_out"))
            pe.wait_ge(sem("dtA"), 1)
            dtA = small[:, 32:64].rearrange("p (t h) -> p t h", t=2)
            pe.matmul(ps[:, 4, 0:32], con("until"), small[:, 32:64], start=True, stop=True)
            pe.matmul(ps[:, 4, 32:48], con("after"), dtA[:, 0, :], start=True, stop=True).then_inc(sem("acum_mm"), 1)
            barrier()
            xbcT = A(SX, 12, S)
            for t in range(TT):
                for c in range(KT):
                    mm = pe.transpose(ps[:, 4 + 2 * t + c // 4, (c % 4) * P:(c % 4 + 1) * P],
                                      xbcT[:, c, t * P:(t + 1) * P], ident)
            mm.then_inc(sem("xs_turned"), 1)
            for g in range(2):
                pe.transpose(ps[:, 0, g * P:(g + 1) * P], xbcT[:, 8 + g, 0:P], ident)
            for t in range(TT):
                for g in range(2):
                    mm = pe.matmul(ps[:, 1, (2 * t + g) * P:(2 * t + g + 1) * P], xbcT[:, 8 + g, t * P:(t + 1) * P],
                                   xbcT[:, 10 + g, t * P:(t + 1) * P], start=True, stop=True)
            mm.then_inc(sem("cb_mm"), 1)
            pe.wait_ge(sem("ssd_inputs"), 1)
            for g in range(2):
                mm = pe.matmul(ps[:, g, :], A(SB, 2, P)[:, g, :], A(SXD, D)[:, g * 512:(g + 1) * 512],
                               start=True, stop=True)
            mm.then_inc(sem("state_mm"), 1)
            pe.wait_ge(sem("state_out"), 1)
            for g in range(2):
                mm = pe.matmul(ps[:, g, :], xbcT[:, 10 + g, P:S], A(SST, 2, 512)[:, g, :], start=True, stop=True)
            mm.then_inc(sem("yoff_mm"), 1)

            def ssd_spread(b):
                t, hb = b // 4, b % 4
                if b >= 2:
                    pe.wait_ge(sem("seg_out"), b - 1)
                for j in range(4):
                    h = 4 * hb + j
                    mm = pe.matmul(ps[:, 2 + b % 2, j * P:(j + 1) * P], dtA[:, t, h:h + 1].broadcast_to([P, P]),
                                   con("until"), start=True, stop=True)
                mm.then_inc(sem("seg_mm"), 1)

            ssd_spread(0)
            for b in range(8):
                if b < 7:
                    ssd_spread(b + 1)
                pe.wait_ge(sem("decay_cb"), b + 1)
                t, hb = b // 4, b % 4
                for j in range(4):
                    h = 4 * hb + j
                    mm = pe.matmul(ps[:, 4 + 2 * t + h // 8, (h % 8) * 64:(h % 8 + 1) * 64],
                                   A(SE, 2, 512)[:, b % 2, j * P:(j + 1) * P],
                                   A(SXX, TT, D)[:, t, h * 64:(h + 1) * 64], start=True, stop=True)
                mm.then_inc(sem("ydiag_mm"), 1)
            barrier()
            turn_all(A(SRAW, TT, D), sem("y_normed"), 1, sem("y_turned"))
            pe.wait_ge(sem("yT_out"), 1)
            token_product("gate_ssd", sem("gs_out"))
            yT = A(SX, KT, S)
            down_product("ssd_out", 2, lambda k, t: yT[:, k, t * P:(t + 1) * P])
            barrier()

            turn_all(A(0, TT, D), sem("mix_done"), 1, sem("mix_turned"))
            pe.wait_ge(sem("mixT_out"), 1)
            mixT = A(2048, KT, S)
            down_product("mix_out", 2, lambda k, t: mixT[:, k, t * P:(t + 1) * P], 1)
            barrier()
            turn_all(A(0, TT, D), sem("x_scaled"), 2 * TT, sem("h_turned"))
            modulation_gain()
            barrier()
            for g in range(16):
                if g % 2 == 0:
                    wt = weights("ff1", g // 2)
                if g >= 4:
                    pe.wait_ge(sem("ff_relu"), g - 3)
                feature_pair(wt, g % 2, g % 4)
            pe.wait_ge(sem("ff_hidden"), 16)
            hid = A(FH, 32, S)
            down_product("ff2", 8, lambda k, t: hid[:, k, t * P:(t + 1) * P], 2)
            barrier()

            turn_all(A(0, TT, D), sem("x_scaled"), 3 * TT, sem("h_turned"))
            modulation_gain()
            barrier()
            wt = weights("qa", 0)
            for j in range(2):
                feature_pair(wt, j, j)
            wt = weights("kva", 0)
            for k in range(KT):
                mm = pe.matmul(ps[:, 2, 0:S], wt[:, k, 0:P], hT[:, k, :], start=(k == 0), stop=(k == KT - 1))
            mm.then_inc(lin_done, 1)
            for t in range(TT):
                for k in range(KT):
                    mm = pe.matmul(ps[:, 3, t * P:(t + 1) * P], hT[:, k, t * P:(t + 1) * P], wt[:, k, P:2 * P],
                                   start=(k == 0), stop=(k == KT - 1))
                mm.then_inc(lin_done, 1)
            for g in range(6):
                if g % 2 == 0:
                    wt = weights("qkv_b", g // 2)
                pe.wait_ge(sem("ab_out1"), g + 1)
                feature_pair(wt, g % 2, g % 4)
            wt = weights("gate_b", 0)
            for t in range(TT):
                for k in range(KT):
                    mm = pe.matmul(ps[:, 4 + t, :], hT[:, k, t * P:(t + 1) * P], wt[:, k, :],
                                   start=(k == 0), stop=(k == KT - 1))
                mm.then_inc(lin_done, 1)
            wt = weights("ba", 0)
            for t in range(TT):
                for k in range(KT):
                    mm = pe.matmul(ps[:, 6, 16 * t:16 * t + 16], hT[:, k, t * P:(t + 1) * P], wt[:, k, :],
                                   start=(k == 0), stop=(k == KT - 1))
                mm.then_inc(lin_done, 1)
            barrier()
            qaT, kdup, va = A(WQ, 4, S), A(WK, 2, S), A(WV, TT, P)
            for i in range(4):
                t, par = i // 2, i % 2
                n = (t + 1) * P
                lo = 64 * par
                if i >= 1:
                    pe.wait_ge(sem("wa_biased"), i)
                for a in range(4):
                    h = 2 * a + par
                    o = ps[:, 0, a * P:(a + 1) * P] if t == 0 else ps[:, a // 2, (a % 2) * S:(a % 2 + 1) * S]
                    mm = pe.matmul(o, qaT[lo:lo + 64, a, t * P:(t + 1) * P], kdup[lo:lo + 64, h // 4, 0:n],
                                   start=True, stop=True)
                mm.then_inc(sem("wa_scores"), 1)
                pe.wait_ge(sem("wa_probs"), i + 1)
                for b in range(4 * (t + 1)):
                    mm = pe.transpose(ps[:, 2 + b // 4, (b % 4) * P:(b % 4 + 1) * P],
                                      A(WS, 4 * S)[:, b * P:(b + 1) * P], ident)
                mm.then_inc(sem("wa_pT"), 1)
                pe.wait_ge(sem("wa_turned"), i + 1)
                for a in range(4):
                    h = 2 * a + par
                    for s in range(t + 1):
                        b = a * (t + 1) + s
                        mm = pe.matmul(ps[lo:lo + 64, 4, a * P:(a + 1) * P], va[:, s, (h // 4) * 64:(h // 4 + 1) * 64],
                                       A(WPT, 4 * S)[:, b * P:(b + 1) * P], start=(s == 0), stop=(s == t))
                mm.then_inc(sem("wa_pv"), 1)
                pe.wait_ge(sem("wa_out"), i + 1)
            for g in range(4):
                pe.wait_ge(sem("l2_sq"), g + 1)
                if g >= 2:
                    pe.wait_ge(sem("l2_rstd"), g - 1)
                pe.matmul(ps[:, 5 + g % 2, :], con("block64"), A(WS, 2, 512)[:, g % 2, :],
                          start=True, stop=True).then_inc(sem("l2_ss"), 1)
            barrier()
            qkvT = A(DQKV, 12, S)
            for t in range(TT):
                for c in range(8):
                    mm = pe.transpose(ps[:, 2 * t + c // 4, (c % 4) * P:(c % 4 + 1) * P],
                                      qkvT[:, 4 + c, t * P:(t + 1) * P], ident)
            mm.then_inc(sem("kv_turned"), 1)
            g16 = small[:, SG:SG + 16]
            pe.wait_ge(sem("dn_g"), 1)
            pe.matmul(ps[:, 4, 0:16], con("until64"), g16, start=True, stop=True)
            pe.matmul(ps[:, 4, 16:32], con("after64"), g16, start=True, stop=True).then_inc(sem("dn_gc"), 1)
            barrier()
            beta16 = small[:, SBETA:SBETA + 16]
            for b in range(4):
                t, par = b // 2, b % 2
                lo = 64 * par
                o = 4 * (b % 2)
                if b >= 2:
                    pe.wait_ge(sem("dn_lt"), b - 1)
                for a in range(4):
                    h = 2 * a + par
                    sl = slice(a * P, (a + 1) * P)
                    c = t * 8 + h
                    q_, k_ = qkvT[lo:lo + 64, a, t * P:(t + 1) * P], qkvT[lo:lo + 64, 4 + a, t * P:(t + 1) * P]
                    pe.matmul(ps[:, o, sl], g16[:, c:c + 1].broadcast_to([P, P]), con("until64"), start=True, stop=True)
                    pe.matmul(ps[:, o + 1, sl], beta16[:, c:c + 1].broadcast_to([P, P]), ident, start=True, stop=True)
                    pe.matmul(ps[:, o + 2, sl], k_, k_, start=True, stop=True)
                    mm = pe.matmul(ps[:, o + 3, sl], k_, q_, start=True, stop=True)
                mm.then_inc(sem("dn_mm"), 1)
            barrier()
            T, TTr = A(DT, 4, 512), A(DTT, 4, 512)
            for l in range(len(LEVELS)):
                for b in range(4):
                    n = 4 * l + b
                    pe.wait_ge(sem("dn_lm"), n + 1)
                    if n >= 4:
                        pe.wait_ge(sem("dn_T"), n - 3)
                    for a in range(4):
                        sl = slice(a * P, (a + 1) * P)
                        mm = pe.matmul(ps[:, b, sl], A(DLM, 2, 512)[:, b % 2, sl], T[:, b, sl], start=True, stop=True)
                    mm.then_inc(sem("dn_u"), 1)
                    pe.wait_ge(sem("dn_uout"), n + 1)
                    if n >= 2:
                        pe.wait_ge(sem("dn_T"), n - 1)
                    for a in range(4):
                        sl = slice(a * P, (a + 1) * P)
                        if l < len(LEVELS) - 1:
                            pe.matmul(ps[:, 4 + 2 * (b % 2), sl], TTr[:, b, sl], A(DU, 2, 512)[:, b % 2, sl],
                                      start=True, stop=True)
                        mm = pe.matmul(ps[:, 5 + 2 * (b % 2), sl], A(DU, 2, 512)[:, b % 2, sl], TTr[:, b, sl],
                                       start=True, stop=True)
                    mm.then_inc(sem("dn_tu"), 1)
            barrier()
            vb, kbg, kdec = A(DVB, TT, 512), A(DKBG, TT, 512), A(DKDEC, TT, 512)
            for t in range(TT):
                for a in range(4):
                    for par in range(2):
                        h = 2 * a + par
                        inv = TTr[:, 2 * t + par, a * P:(a + 1) * P]
                        pe.matmul(ps[:, t, h * 64:(h + 1) * 64], inv, vb[:, t, h * 64:(h + 1) * 64],
                                  start=True, stop=True)
                        mm = pe.matmul(ps[64 * par:64 * par + 64, 2 + t, a * P:(a + 1) * P],
                                       kbg[:, t, h * 64:(h + 1) * 64], inv, start=True, stop=True)
            mm.then_inc(sem("dn_uw"), 1)
            barrier()
            St, vn, wTt, qd = A(DST, 4, 64), A(DVN, 8, 64), A(DWT, TT, 512), A(DQD, 4, S)
            qk = A(DQK, 4, 512)
            for ci in range(4):
                t, pb = ci // 2, 64 * (ci % 2)
                pe.wait_ge(sem("dn_S"), ci + 1)
                if ci >= 1:
                    pe.wait_ge(sem("dn_o"), ci)
                for par in range(2):
                    lo = 64 * par
                    for a in range(4):
                        pe.matmul(ps[pb:pb + 64, par, a * 64:(a + 1) * 64],
                                  wTt[lo:lo + 64, t, a * P + pb:a * P + pb + 64], St[lo:lo + 64, a, :],
                                  start=True, stop=True)
                        mm = pe.matmul(ps[pb:pb + 64, par, 256 + a * 64:256 + (a + 1) * 64],
                                       qd[lo:lo + 64, a, t * P + pb:t * P + pb + 64], St[lo:lo + 64, a, :],
                                       start=True, stop=True)
                mm.then_inc(sem("dn_ws"), 1)
                pe.wait_ge(sem("dn_vn"), ci + 1)
                for a in range(4):
                    for par in range(2):
                        h = 2 * a + par
                        pe.matmul(ps[pb:pb + 64, 2, h * 64:(h + 1) * 64],
                                  qk[pb:pb + 64, 2 * t + par, a * P + pb:a * P + pb + 64], vn[pb:pb + 64, h, :],
                                  start=True, stop=True)
                        mm = pe.matmul(ps[64 * par:64 * par + 64, 3, a * 64:(a + 1) * 64],
                                       kdec[pb:pb + 64, t, h * 64:(h + 1) * 64], vn[pb:pb + 64, h, :],
                                       start=True, stop=True)
                mm.then_inc(sem("dn_su"), 1)
            pe.wait_ge(sem("dn_gated"), 1)
            o_ = A(DO, TT, 512)
            for t in range(TT):
                for c in range(4):
                    mm = pe.transpose(ps[:, 4 + c // 2, (c % 2) * S + t * P:(c % 2) * S + (t + 1) * P],
                                      o_[:, t, c * P:(c + 1) * P], ident)
            mm.then_inc(sem("ob_turned"), 1)
            pe.wait_ge(sem("ob_out"), 1)
            abT = A(DOUT, 8, S)
            down_product("ab_out", 2, lambda k, t: abT[:, k, t * P:(t + 1) * P], 3)
            barrier()
            turn_all(A(0, TT, D), sem("x_scaled"), 4 * TT, sem("h_turned"))
            modulation_gain()
            barrier()
            g = 0
            for c in range(6):
                pairs = 2 if c < 5 else 1
                for kind in range(2):
                    wt = weights("ffn", 2 * c + kind)
                    for j in range(pairs):
                        if c >= 1:
                            pe.wait_ge(sem("sw_silu") if kind == 0 else sem("sw_hidden"), 2 * (c - 1) + j + 1)
                        feature_pair(wt, j, 2 * kind + j)
            pe.wait_ge(sem("sw_hidden"), 11)
            hid = A(FH, 22, S)
            down_product("ffn_down", 6, lambda k, t: hid[:, k, t * P:(t + 1) * P], 4)
            barrier()

            turn_all(A(0, TT, D), sem("x_scaled"), 5 * TT, sem("h_turned"))
            modulation_gain()
            barrier()
            for g in range(14):
                if g % 2 == 0:
                    wt = weights("cd_in", g // 2)
                if g >= 4:
                    pe.wait_ge(sem("cd_out1"), g - 3)
                feature_pair(wt, g % 2, g % 4)
            wt = weights("lru_gates", 0)
            pe.wait_ge(sem("vector2"), 1)
            xcc = A(LX, KT, S)
            for g in range(8):
                bank = 4 + g % 4
                if g >= 4:
                    pe.wait_ge(sem("lru_gate"), 2 * (g - 3))
                for i in range(2):
                    n = 2 * (g % 4) + i
                    mm = pe.matmul(ps[:, bank, i * S:(i + 1) * S], wt[:, 8 * (g // 4) + n, :], xcc[:, n, :],
                                   start=True, stop=True)
                mm.then_inc(lin_done, 1)
            barrier()
            pe.wait_ge(sem("cd_ready"), 1)
            cdT = A(LOUT, 12, S)
            down_product("cd_out", 3, lambda k, t: cdT[:, k, t * P:(t + 1) * P], 5)
            barrier()

            turn_all(A(XN, TT, D), sem("x_scaled"), 6 * TT, sem("h_turned"))
            modulation_gain()
            barrier()
            for t in range(TT):
                for k in range(KT):
                    mm = pe.matmul(ps[:, 0, t * 8:(t + 1) * 8], hT[:, k, t * P:(t + 1) * P], router[:, k, :],
                                   start=(k == 0), stop=(k == KT - 1))
            mm.then_inc(sem("routed"), 1)
            pe.wait_ge(sem("vector2"), 5)
            mask = A(MO, TT, EXPERTS)
            pe.matmul(ps[:, 1, 0:8], con("until"), mask[:, 0, :], start=True, stop=True)
            pe.matmul(ps[:, 1, 8:16], ones, mask[:, 0, :], start=True, stop=False)
            pe.matmul(ps[:, 1, 8:16], con("until"), mask[:, 1, :], start=False, stop=True)
            pe.matmul(ps[:, 1, 16:24], ones, mask[:, 0, :], start=True, stop=False)
            pe.matmul(ps[:, 1, 16:24], ones, mask[:, 1, :], start=False, stop=True).then_inc(sem("routed"), 1)

            xn, hidden = A(XN, TT, D), A(EH, 2, 512)
            select, gated, turned = A(ESEL, TT, P), A(EGATED, TT, P), A(ETURN, TT, P)

            def gather(done):
                for k in range(KT):
                    for t in range(TT):
                        mm = pe.matmul(ps[:, k // 4, (k % 4) * P:(k % 4 + 1) * P], xn[:, t, k * P:(k + 1) * P],
                                       select[:, t, :], start=(t == 0), stop=(t == TT - 1))
                mm.then_inc(done, 1)

            def scatter(t):
                for h in range(2):
                    pe.matmul(ps[:, 6 + h, :], turned[:, t, :], A(EY, D)[:, h * 512:(h + 1) * 512],
                              start=True, stop=True).then_inc(sem("scattered"), 1)

            def turn_hidden(i, f):
                pe.wait_ge(sem("moe_hidden"), i * GU + (f + 1))
                if f < 2:
                    pe.wait_ge(sem("moe_added"), i * 4 + (4 + f))
                for j in range(4):
                    mm = pe.transpose(ps[:, 6 + f % 2, j * P:(j + 1) * P], hidden[:, f % 2, j * P:(j + 1) * P], ident)
                mm.then_inc(sem("hidden_turned"), 1)

            pe.wait_ge(sem("vector2"), 6)
            n_rounds = pe.value_load(rounds[0:1, 0:1], min_val=EXPERTS, max_val=ROUNDS)
            pe.wait_ge(sem("selected"), 1)
            gather(sem("gathered"))
            with pe.Fori(0, n_rounds) as i:
                def split_product(m, n, bank, acts, k0, k_tiles, col0, start, stop):
                    high, low = (a.rearrange("p (k n) -> p k n", n=n) for a in half_of(m)[1:])
                    for k in range(k_tiles):
                        for j, (x_, w_) in enumerate(((0, high), (0, low), (1, high))):
                            mm = pe.matmul(ps[:, bank, :], acts[:, x_, k0 + k, :], w_[:, k, col0:col0 + 512],
                                           start=(start and k + j == 0), stop=(stop and k == k_tiles - 1 and j == 2))
                    return mm

                pe.wait_ge(sem("gathered_ready"), i * 3 + 3)
                for f in range(GU):
                    for kind in range(2):
                        if f >= 2:
                            pe.wait_ge(sem("moe_hidden") if kind else sem("moe_silu"), i * GU + (f - 1))
                        for half in range(2):
                            m = 4 * f + 2 * kind + half
                            pe.wait_ge(sem("low_ready"), i * E_STEPS + (m + 1))
                            split_product(m, 512, 2 * kind + f % 2, tokens_hl, 4 * half, 4, 0,
                                          half == 0, half == 1).then_inc(lin_done, 1)
                        if f == 0:
                            if kind == 0:
                                pe.wait_ge(sem("expert_out"), i * 2 + 3)
                            else:
                                pe.wait_ge(sem("moe_added"), i * 4 + 3)
                            scatter(kind)
                    if f:
                        turn_hidden(i, f - 1)
                for f in range(GU):
                    for half in range(2):
                        m = 4 * GU + 2 * f + half
                        pe.wait_ge(sem("low_ready"), i * E_STEPS + (m + 1))
                        for h in range(2):
                            mm = split_product(m, D, 4 + h, hidden_hl, 4 * f + 2 * half, 2, h * 512,
                                               f + half == 0, f == GU - 1 and half == 1)
                        mm.then_inc(lin_done, 1)
                    if f == 0:
                        turn_hidden(i, GU - 1)
                    if f == 1:
                        pe.wait_ge(sem("selected"), i + 2)
                        for t in range(TT):
                            pe.transpose(ps[:, 2, t * P:(t + 1) * P], gated[:, t, :], ident)
                        gather(sem("gathered"))
            pe.wait_ge(sem("expert_out"), n_rounds * 2 + 3)
            scatter(0)
            pe.wait_ge(sem("moe_added"), n_rounds * 4 + 3)
            scatter(1)
            barrier()

        @block.scalar
        def _(act):
            barrier = barrier_of(act)
            L = Lane(act, sem("act_step"))
            eps = con("eps")

            def f(o, i, fn, s=None, **kw):
                L(nc.scalar.activation(o, i, fn, **kw), s)

            def copy(o, i, s=None):
                L(nc.scalar.copy(o, i), s)

            def rstd(dst, src, scale, s=None):
                f(dst, src, ACT.Ln, bias=eps, scale=scale)
                L.settle()
                f(dst, dst, ACT.Exp, s, scale=-0.5)

            norm = [0]

            def norm_stats(scratch_):
                n = norm[0]
                norm[0] += 1
                for t in range(TT):
                    f(scratch_[:, t, :], x[:, t, :], ACT.Square, accum_out=small[:, 600 + t:601 + t])
                L.settle()
                rstd(small[:, 602:604], small[:, 600:602], 1.0 / D, sem("norm_rstd"))

            for i, name in enumerate(("c", "c_2")):
                act.dma_start(spread[:, 96 + 8 * i:104 + 8 * i], w[name][0].rearrange("(p k) -> p k", p=P)
                              ).then_inc(sem("c_in"), 16)
            act.wait_ge(sem("c_in"), 32)
            f(small[:, 608:624], spread[:, 96:112], ACT.Silu, sem("act_params"))
            act.wait_ge(sem("line_mm"), 1)
            for i, n in enumerate(row_n):
                copy(cols[:, i, 0:n], ps[:, 0, i * P:i * P + n], sem("cols_out"))
            for h in range(8):
                act.wait_ge(sem("line_mm"), h + 2)
                copy(A(8192, 8, 383)[:, h, :], ps[:, 2 + h % 2, 0:383], sem("bias_line"))
            act.wait_ge(sem("bias_line"), 8)
            act.dma_start(scratch[:, :, 0:383], A(8192, 8, 383)).then_inc(sem("line_out"), 16)
            act.wait_ge(params_in, N_PARAMS)
            f(small[:, 0:16], spr("a_log"), ACT.Exp, sem("act_params"))
            f(small[:, 16:24], spr("dn_a_log_2"), ACT.Exp, sem("act_params"))
            act.wait_ge(x_in, 16 * TT)
            norm_stats(A(4096, TT, D))
            barrier()
            barrier()

            for g in range(12):
                act.wait_ge(lin_done, lin0("q") + g + 1)
                dst = A(QT if g < 6 else KTT, HEADS, S)[:, 2 * (g % 6):2 * (g % 6) + 2, :].rearrange("p a b -> p (a b)")
                copy(dst, ps[:, g % 4, :])
                if g >= 2:
                    act.wait_ge(sem("qk_ss"), g - 1)
                f(A(QSQ, 2, 512)[:, g % 2, :], ps[:, g % 4, :], ACT.Square, sem("qk_raw"))
                if g >= 1:
                    act.wait_ge(sem("qk_ss"), g)
                    if g >= 3:
                        act.wait_ge(sem("qk_normed"), g - 2)
                    rstd(A(QRS, 2, 512)[:, (g - 1) % 2, :], ps[:, 4 + (g - 1) % 2, :], 1.0 / P, sem("qk_rstd"))
            act.wait_ge(sem("qk_ss"), 12)
            act.wait_ge(sem("qk_normed"), 10)
            rstd(A(QRS, 2, 512)[:, 1, :], ps[:, 5, :], 1.0 / P, sem("qk_rstd"))
            v = A(VT, TT, HEADS * P)
            for g in range(6):
                act.wait_ge(lin_done, lin0("v") + g + 1)
                copy(v[:, g % 2, (g // 2) * 512:(g // 2 + 1) * 512], ps[:, g % 4, :], sem("v_out"))
            barrier()

            for i in range(8):
                t = i % 2
                n = 3 * (t + 1) * P
                act.wait_ge(sem("at_max"), i + 1)
                f(A(AP_, 2, 768)[:, i % 2, 0:n], A(AS_, 2, 768)[:, i % 2, 0:n], ACT.Exp, sem("at_exp"),
                  bias=small[:, 64 + i:65 + i], accum_out=small[:, 72 + i:73 + i])
                act.wait_ge(sem("at_pT"), i + 1)
                b = n // P
                copy(A(APT, 2, 768)[:, i % 2, 0:min(b, 4) * P], ps[:, 4, 0:min(b, 4) * P],
                     None if b > 4 else sem("at_turned"))
                if b > 4:
                    copy(A(APT, 2, 768)[:, i % 2, 4 * P:b * P], ps[:, 5, 0:(b - 4) * P], sem("at_turned"))
            barrier()

            gate = A(2048, TT, D)

            def gates(name, s):
                for g in range(4):
                    act.wait_ge(lin_done, lin0(name) + g + 1)
                    f(gate[:, g % 2, (g // 2) * 512:(g // 2 + 1) * 512], ps[:, g % 4, :], ACT.Sigmoid, s)

            gates("gate_attn", sem("ga_out"))
            barrier()
            u = A(PU, TT, D)
            for g in range(4):
                act.wait_ge(lin_done, lin0("u") + g + 1)
                copy(u[:, g % 2, (g // 2) * 512:(g // 2 + 1) * 512], ps[:, g % 4, :], sem("u_out"))
            gates("gate_pool", sem("gp_out"))
            barrier()

            raw = A(SRAW, 12, 259)
            for g in range(6):
                act.wait_ge(lin_done, lin0("xbc") + g + 1)
                copy(raw[:, 2 * g:2 * g + 2, 3:259], ps[:, g % 4, :].rearrange("p (a b) -> p a b", a=2), sem("xbc_out"))
            act.wait_ge(sem("softplus_in"), 1)
            f(small[:, 128:160], small[:, 96:128], ACT.Exp, sem("softplus_fn"), scale=-1.0)
            act.wait_ge(sem("softplus_in"), 2)
            f(small[:, 192:224], small[:, 160:192], ACT.Ln, sem("softplus_fn"))
            for g in range(4):
                act.wait_ge(lin_done, lin0("z") + g + 1)
                f(A(SZ, TT, D)[:, g % 2, (g // 2) * 512:(g // 2 + 1) * 512], ps[:, g % 4, :], ACT.Silu, sem("z_out"))
            xbcT = A(SX, 12, S)
            for c in range(12):
                act.wait_ge(sem("conv"), c + 1)
                f(xbcT[:, c, :], xbcT[:, c, :], ACT.Silu, bias=col("conv_b", c))
            act.wait_ge(sem("acum_mm"), 1)
            copy(small[:, 224:256], ps[:, 4, 0:32])
            f(small[:, 256:288], ps[:, 4, 0:32], ACT.Exp)
            f(small[:, 288:304], ps[:, 4, 32:48], ACT.Exp)
            barrier()
            act.wait_ge(sem("cb_mm"), 1)
            copy(A(SB, 256), ps[:, 0, 0:256])
            copy(A(SCB, 512), ps[:, 1, :], sem("bcb_out"))
            act.wait_ge(sem("state_mm"), 1)
            for g in range(2):
                copy(A(SST, 2, 512)[:, g, :], ps[:, g, :], None if g == 0 else sem("state_out"))
            for b in range(8):
                act.wait_ge(sem("seg_masked"), b + 1)
                e = A(SE, 2, 512)[:, b % 2, :]
                f(e, e, ACT.Exp, sem("seg_exp"))
            barrier()
            y = A(SRAW, TT, D)
            act.wait_ge(sem("y_gated"), 1)
            for t in range(TT):
                for g in range(2):
                    f(A(SXX, TT, D)[:, t, g * 512:(g + 1) * 512], y[:, t, g * 512:(g + 1) * 512], ACT.Square,
                      accum_out=small[:, 304 + 2 * t + g:305 + 2 * t + g])
            L.settle()
            rstd(small[:, 308:312], small[:, 304:308], 1.0 / 512, sem("y_rstd"))
            gates("gate_ssd", sem("gs_out"))
            barrier()

            barrier()
            norm_stats(A(4096, TT, D))
            barrier()
            hid = A(FH, 32, S)
            for g in range(16):
                act.wait_ge(lin_done, lin0("ff1") + g + 1)
                f(hid[:, 2 * g:2 * g + 2, :].rearrange("p a b -> p (a b)"), ps[:, g % 4, :], ACT.Relu, sem("ff_relu"))
            barrier()
            norm_stats(A(4096, TT, D))

            barrier()
            for j in range(2):
                act.wait_ge(lin_done, lin0("qa") + j + 1)
                copy(A(WQ, 2, 512)[:, j, :], ps[:, j, :], sem("ab_out1"))
            act.wait_ge(lin_done, lin0("kva") + 1)
            kdup = A(WK, 2, S)
            for kv in range(2):
                for half in range(2):
                    copy(kdup[64 * half:64 * half + 64, kv, :], ps[64 * kv:64 * kv + 64, 2, 0:S],
                         sem("ab_out1") if (kv, half) == (1, 1) else None)
            act.wait_ge(lin_done, lin0("kva") + 3)
            copy(A(WV, TT * P), ps[:, 3, 0:S], sem("ab_out1"))
            raw = A(WRAW, 12, 259)
            for g in range(6):
                act.wait_ge(lin_done, lin0("qkv_b") + g + 1)
                copy(raw[:, 2 * g:2 * g + 2, 3:259], ps[:, g % 4, :].rearrange("p (a b) -> p a b", a=2), sem("ab_out1"))
            for t in range(TT):
                act.wait_ge(lin_done, lin0("gate_b") + t + 1)
                f(A(DGS, TT, 512)[:, t, :], ps[:, 4 + t, :], ACT.Silu)
            qkvT = A(DQKV, 12, S)
            for c in range(12):
                act.wait_ge(sem("dn_conv"), c + 1)
                f(qkvT[:, c, :], qkvT[:, c, :], ACT.Silu, sem("dn_silu"))
            act.wait_ge(sem("beta_raw"), 1)
            f(small[:, SBETA:SBETA + 16], small[:, 464:480], ACT.Sigmoid)
            act.wait_ge(sem("softplus_in"), 3)
            f(small[:, 128:144], small[:, 96:112], ACT.Exp, sem("softplus_fn"), scale=-1.0)
            act.wait_ge(sem("softplus_in"), 4)
            f(small[:, 192:208], small[:, 160:176], ACT.Ln, sem("softplus_fn"))
            barrier()
            for i in range(4):
                t = i // 2
                n = 4 * (t + 1) * P
                act.wait_ge(sem("wa_shift"), i + 1)
                f(A(WS, 4 * S)[:, 0:n], A(WS, 4 * S)[:, 0:n], ACT.Exp)
                f(small[:, 96:100], small[:, 100:104], ACT.Exp, sem("wa_exp"))
                act.wait_ge(sem("wa_pT"), i + 1)
                for b in range(t + 1):
                    copy(A(WPT, 4 * S)[:, b * 512:(b + 1) * 512], ps[:, 2 + b, :],
                         sem("wa_turned") if b == t else None)
            for g in range(4):
                if g >= 2:
                    act.wait_ge(sem("l2_ss"), g - 1)
                elif g == 0:
                    act.wait_ge(sem("wa_out"), 4)
                f(A(WS, 2, 512)[:, g % 2, :], qkvT[:, 2 * g:2 * g + 2, :].rearrange("p a b -> p (a b)"), ACT.Square,
                  sem("l2_sq"))
                act.wait_ge(sem("l2_ss"), g + 1)
                if g >= 1:
                    act.wait_ge(sem("l2_normed"), g)
                rstd(A(WPT, 2, 512)[:, g % 2, :], ps[:, 5 + g % 2, :], 1.0, sem("l2_rstd"))
            barrier()
            act.wait_ge(sem("dn_gc"), 1)
            copy(small[:, SGC:SGC + 16], ps[:, 4, 0:16])
            f(small[:, SEG:SEG + 32], ps[:, 4, 0:32], ACT.Exp, sem("dn_eg"))
            barrier()
            for b in range(4):
                o = 4 * (b % 2)
                act.wait_ge(sem("dn_seg"), b + 1)
                f(A(DEGB, 4, 512)[:, b, :], ps[:, o, :], ACT.Exp, sem("dn_egb"))
                f(A(DT, 2, 512)[:, b % 2, :], A(DT, 2, 512)[:, b % 2, :], ACT.Exp, sem("dn_dec"))
            barrier()
            for n in range(4 * len(LEVELS)):
                b = n % 4
                act.wait_ge(sem("dn_u"), n + 1)
                if n >= 2:
                    act.wait_ge(sem("dn_tu"), n - 1)
                copy(A(DU, 2, 512)[:, b % 2, :], ps[:, b, :], sem("dn_uout"))
            barrier()
            act.wait_ge(sem("dn_uw"), 1)
            for t in range(TT):
                copy(A(DUU, TT, 512)[:, t, :], ps[:, t, :])
                copy(A(DWT, TT, 512)[:, t, :], ps[:, 2 + t, :])
            barrier()
            for ci in range(4):
                t, pb = ci // 2, 64 * (ci % 2)
                act.wait_ge(sem("dn_vn"), ci + 1)
                for par in range(2):
                    dst = A(DO, TT, 512)[pb:pb + 64, t, :].rearrange("p (a b e) -> p a b e", b=2, e=64)[:, :, par, :]
                    src = ps[pb:pb + 64, par, 256:512].rearrange("p (a e) -> p a e", e=64)
                    copy(dst, src, sem("dn_o1") if par else None)
            act.wait_ge(sem("dn_oss"), 1)
            rstd(small[:, 448:464], small[:, 432:448], 1.0 / 64, sem("dn_orstd"))
            barrier()
            norm_stats(A(4096, TT, D))
            barrier()
            for c in range(6):
                for j in range(2 if c < 5 else 1):
                    act.wait_ge(lin_done, lin0("ffn") + 4 * c + j + 1)
                    g = 2 * c + j
                    if g >= 4:
                        act.wait_ge(sem("sw_hidden"), g - 3)
                    f(A(FT, 4, 512)[:, g % 4, :], ps[:, j, :], ACT.Silu, sem("sw_silu"))
            barrier()
            norm_stats(A(4096, TT, D))

            barrier()
            raw = A(LRAW, 8, 259)
            for g in range(14):
                act.wait_ge(lin_done, lin0("cd_in") + g + 1)
                pair = ps[:, g % 4, :].rearrange("p (a b) -> p a b", a=2)
                if g < 4:
                    copy(raw[:, 2 * g:2 * g + 2, 3:259], pair, sem("cd_out1"))
                elif g < 8:
                    f(A(LY, KT, S)[:, 2 * g - 8:2 * g - 6, :], pair, ACT.Gelu_apprx_tanh, sem("cd_out1"))
                else:
                    copy(A(LB, 12, S)[:, 2 * g - 16:2 * g - 14, :], pair, sem("cd_out1"))
            act.wait_ge(sem("softplus_in"), 5)
            f(small[:, 128:136], small[:, 96:104], ACT.Exp, sem("softplus_fn"), scale=-1.0)
            act.wait_ge(sem("softplus_in"), 6)
            f(small[:, 192:200], small[:, 160:168], ACT.Ln, sem("softplus_fn"))
            for g in range(8):
                act.wait_ge(lin_done, lin0("lru_gates") + g + 1)
                for i in range(2):
                    n = 2 * (g % 4) + i
                    b = col("lru_gate_a_b_2" if g < 4 else "lru_gate_x_b_2", n)
                    f(A(LR if g < 4 else LI, KT, S)[:, n, :], ps[:, 4 + g % 4, i * S:(i + 1) * S], ACT.Sigmoid,
                      sem("lru_gate"), bias=b)
            act.wait_ge(sem("vector2"), 2)
            f(A(LA, KT * S), A(LR, KT * S), ACT.Exp, sem("scalar2"))
            f(A(LH, KT * S), A(LR, KT * S), ACT.Tanh, sem("scalar2"))
            act.wait_ge(sem("vector2"), 3)
            f(A(LR, KT * S), A(LR, KT * S), ACT.Sqrt, sem("scalar2"))
            barrier()
            barrier()
            norm_stats(A(4096, TT, D))
            barrier()
            act.wait_ge(sem("vector2"), 4)
            for t in range(TT):
                f(small[:, 500 + t:501 + t], small[:, 502 + t:503 + t], ACT.Exp, sem("scalar2"))
            def gathered_high(n):
                act.wait_ge(sem("gathered_ready"), n)
                nc.scalar.copy(tokens_hl[:, 0], A(EG, KT, P)).then_inc(sem("gathered_ready"), 1)

            def copy_output(n_done):
                act.wait_ge(lin_done, n_done)
                nc.scalar.copy(A(EY, D)[:, 0:512], ps[:, 4, :]).then_inc(sem("expert_out"), 1)

            act.wait_ge(sem("vector2"), 6)
            n_rounds = act.value_load(rounds[0:1, 0:1], min_val=EXPERTS, max_val=ROUNDS)
            gathered_high(1)
            with act.Fori(0, n_rounds) as i:
                for m in range(E_STEPS):
                    whole, high, _ = half_of(m)
                    if m % 2 == 0:
                        slot = e_slot(m // 2)
                        act.wait_ge(w_landed[slot], i * (16 * GU) + (16 * uses[slot] + 16 * (m // 2 // RING + 1)))
                    act.wait_ge(lin_done, i * E_STEPS + (plan.steps + m - 2))
                    nc.scalar.copy(high, whole).then_inc(sem("high_ready"), 1)
                    if m == 2:
                        copy_output(i * E_STEPS + plan.steps)
                    if m >= 4 and m % 4 == 0 and m <= 4 * GU:
                        c = m // 4 - 1
                        if c >= 2:
                            act.wait_ge(sem("moe_hidden"), i * GU + (c - 1))
                        nc.scalar.activation(A(ES, 2, 512)[:, c % 2, :], ps[:, c % 2, :], ACT.Silu
                                             ).then_inc(sem("moe_silu"), 1)
                    if m >= 10 and m % 4 == 2 and m < 10 + 4 * GU:
                        c = (m - 10) // 4
                        act.wait_ge(sem("hidden_turned"), i * GU + (c + 1))
                        nc.scalar.copy(hidden_hl[:, 0, 4 * c:4 * c + 4, :].rearrange("p a b -> p (a b)"), ps[:, 6 + c % 2, :]
                                       ).then_inc(sem("hidden_copied"), 1)
                    if m == 36:
                        act.wait_ge(sem("gathered"), i + 2)
                        nc.scalar.copy(A(ETURN, TT * P), ps[:, 2, 0:TT * P])
                    if m == 37:
                        gathered_high(i * 3 + 4)
            copy_output(n_rounds * E_STEPS + plan.steps)
            barrier()
            act.wait_ge(sem("x_final"), 1)
            norm_stats(A(4096, TT, D))
            act.wait_ge(sem("x_final"), 2)
            act.dma_start(A(2048, D), w["final_norm_w_2"].rearrange("(a n) -> a n", a=1).broadcast_to([P, D])
                          ).then_inc(sem("final_w_in"), 16)

        @block.vector
        def _(dve):
            barrier = barrier_of(dve)
            L = Lane(dve, sem("dve_step"))
            V = nc.vector

            def tt(o, a, b, op, s=None):
                L(V.tensor_tensor(o, a, b, op), s)

            def ts(o, a, c1, op, c2=None, op2=None, s=None):
                if op2 is None:
                    L(V.tensor_scalar(o, a, c1, None, op), s)
                else:
                    L(V.tensor_scalar(o, a, c1, c2, op, op2), s)

            def stt(o, a, c, b, op, op2, s=None):
                L(V.scalar_tensor_tensor(out=o, in0=a, scalar=c, in1=b, op0=op, op1=op2), s)

            def copy(o, i, s=None):
                L(V.tensor_copy(o, i), s)

            def modulation_slabs(u, halfway=None):
                if u:
                    dve.wait_ge(sem("mod_summed"), 2 * u)
                L(V.memset(ada[:], 0.0), sem("ada_clear"))
                dve.wait_ge(sem("ada_bias"), 16 * (u + 1))
                for k in range(KT):
                    i = u * KT + k
                    if halfway and k == KT // 2:
                        halfway()
                    dve.wait_ge(sem(f"slab_in{i % 2}"), 16 * (i // 2 + 1))
                    L.settle()
                    c = small[:, 608 + 8 * (u >= 2) + k:609 + 8 * (u >= 2) + k]
                    stt(ada[:], slab[:, i % 2, :], c, ada[:], ALU.mult, ALU.add, sem("slab_used"))
                L.settle()
                L(V.memset(small[:, 639:640], 0.0), sem("ada_ready"))

            def modulation_take(u, norm_w):
                dve.wait_ge(sem("mod_summed"), 2 * u + 1)
                stt(shift[:, u % 2, 0:KT], ps[:, 0, KT:2 * KT], 1.0, norm_w, ALU.add, ALU.mult)
                copy(shift[:, u % 2, KT:2 * KT], ps[:, 0, 0:KT])

            def norm_apply(u):
                dve.wait_ge(sem("norm_rstd"), u + 1)
                for t in range(TT):
                    ts(A(XN if u == 5 else 0, TT, D)[:, t, :], x[:, t, :], small[:, 602 + t:603 + t], ALU.mult,
                       s=sem("x_scaled"))

            def turned_h(u):
                dve.wait_ge(sem("h_turned"), u + 1)
                for k in range(KT):
                    ts(hT[:, k, :], ps[:, 4 + k // 2, (k % 2) * S:(k % 2 + 1) * S], shift[:, u % 2, k:k + 1], ALU.mult,
                       shift[:, u % 2, KT + k:KT + k + 1], ALU.add)
                dve.wait_ge(sem("mod_summed"), 2 * u + 2)
                for h in range(2):
                    copy(gain[:, h * 512:(h + 1) * 512], ps[:, 2 + h, :])

            def residual(tmp):
                for t in range(TT):
                    for h in range(2):
                        sl = slice(h * 512, (h + 1) * 512)
                        tt(tmp[:, t, sl], gain[:, sl], ps[:, 4 + 2 * t + h, :], ALU.mult)
                L.settle()
                for t in range(TT):
                    tt(x[:, t, :], x[:, t, :], tmp[:, t, :], ALU.add)
                L.settle()

            def branch(name, s, n, first, tmp):
                mix, gate = A(0, TT, D), A(2048, TT, D)
                dve.wait_ge(s, 4)
                dve.wait_ge(lin_done, lin0(name) + n)
                for t in range(TT):
                    for h in range(2):
                        sl = slice(h * 512, (h + 1) * 512)
                        tt((mix if first else tmp)[:, t, sl], gate[:, t, sl], ps[:, 4 + 2 * t + h, :], ALU.mult)
                if not first:
                    L.settle()
                    for t in range(TT):
                        tt(mix[:, t, :], mix[:, t, :], tmp[:, t, :], ALU.add)

            soft = [0]

            def softplus(src, n, dst):
                k = soft[0] = soft[0] + 1
                ax, e, u, lnu = (small[:, o:o + n] for o in (96, 128, 160, 192))
                L.settle()
                ts(ax, src, -1.0, ALU.mult)
                L.settle()
                tt(ax, ax, src, ALU.max, sem("softplus_in"))
                dve.wait_ge(sem("softplus_fn"), 2 * k - 1)
                ts(u, e, 1.0, ALU.add, s=sem("softplus_in"))
                L.settle()
                d, z = small[:, 320:320 + n], small[:, 352:352 + n]
                ts(d, u, -1.0, ALU.add)
                L.settle()
                ts(z, d, 0.0, ALU.is_equal)
                L.settle()
                tt(d, d, z, ALU.add)
                L.settle()
                L(V.reciprocal(d, d))
                tt(z, z, e, ALU.mult)
                L.settle()
                tt(d, d, e, ALU.mult)
                L.settle()
                dve.wait_ge(sem("softplus_fn"), 2 * k)
                tt(d, d, lnu, ALU.mult)
                L.settle()
                tt(d, d, z, ALU.add)
                ts(ax, src, 0.0, ALU.max)
                L.settle()
                tt(dst, d, ax, ALU.add)
                L.settle()

            def conv(raw, dst, taps, wname, stride, tiles, s=None, bias=None):
                L.settle()
                for c in range(tiles):
                    for j in range(taps):
                        wc = col(wname, j * stride + c)
                        src = raw[:, c, j:j + S]
                        last = j == taps - 1
                        if j == 0:
                            if bias:
                                ts(dst[:, c, :], src, wc, ALU.mult, col(bias, c), ALU.add)
                            else:
                                ts(dst[:, c, :], src, wc, ALU.mult)
                        else:
                            L.settle()
                            stt(dst[:, c, :], src, wc, dst[:, c, :], ALU.mult, ALU.add, s if last else None)

            def bias_rows():
                L(V.memset(A(500, 8)[32:33, :], NEG))
                dve.wait_ge(rows_in, N_ROWS)
                dve.wait_ge(params_in, N_PARAMS)
                L.settle()
                tt(A(1024, 8, P)[0:33, :, :], ones[0:33, :].unsqueeze(1).broadcast_to([33, 8, P]),
                   A(500, 8)[0:33, :].unsqueeze(2).broadcast_to([33, 8, P]), ALU.mult, sem("line_lhs"))

            dve.wait_ge(sem("act_params"), 1)
            modulation_slabs(0, bias_rows)
            dve.wait_ge(sem("cols_out"), len(row_n))
            dve.wait_ge(sem("act_params"), 3)
            modulation_take(0, col("norm1_w", 0, 8))
            ts(small[:, 0:24], small[:, 0:24], -1.0, ALU.mult)
            ts(small[:, 24:25], col("q_norm_w"), float(P) ** -0.5, ALU.mult)
            dve.wait_ge(sem("bias_line"), 8)
            dve.wait_ge(sem("line_out"), 16)
            dve.wait_ge(x_in, 16 * TT)
            barrier()
            norm_apply(0)
            turned_h(0)
            barrier()

            for g in range(12):
                dve.wait_ge(sem("qk_rstd"), g + 1)
                dst = A(QT if g < 6 else KTT, HEADS, S)[:, 2 * (g % 6):2 * (g % 6) + 2, :].rearrange("p a b -> p (a b)")
                stt(dst, dst, small[:, 24:25] if g < 6 else col("k_norm_w"), A(QRS, 2, 512)[:, g % 2, :],
                    ALU.mult, ALU.mult, sem("qk_normed"))
            barrier()

            for i in range(9):
                if i < 8:
                    j, t = i // 2, i % 2
                    n = (t + 1) * P
                    dve.wait_ge(sem("at_scores"), i + 1)
                    if i >= 2:
                        dve.wait_ge(sem("at_exp"), i - 1)
                    for g in range(3):
                        o = (ps[:, 2 * (i % 2), g * P:(g + 1) * P] if t == 0
                             else ps[:, 2 * (i % 2) + g // 2, (g % 2) * S:(g % 2 + 1) * S])
                        stt(A(AS_, 2, 768)[:, i % 2, g * n:(g + 1) * n], con(f"dist{t}{g}"),
                            -float(slopes[4 * g + j]), o, ALU.mult, ALU.add, sem("at_masked") if g == 2 else None)
                    L.settle()
                    L(V.tensor_reduce(small[:, 64 + i:65 + i], A(AS_, 2, 768)[:, i % 2, 0:3 * n], AX.X, ALU.max,
                                      negate=True), sem("at_max"))
                    dve.wait_ge(sem("at_exp"), i + 1)
                    L(V.reciprocal(small[:, 80 + i:81 + i], small[:, 72 + i:73 + i]))
                    L.settle()
                    p_ = A(AP_, 2, 768)[:, i % 2, 0:3 * n]
                    ts(p_, p_, small[:, 80 + i:81 + i], ALU.mult, s=sem("at_probs"))
                if i >= 1:
                    j, t = (i - 1) // 2, (i - 1) % 2
                    dve.wait_ge(sem("at_pv"), i)
                    copy(A(AOT, 4, S)[:, j, t * P:(t + 1) * P], ps[:, 6 + (i - 1) % 2, 0:P], sem("at_out"))
            barrier()

            branch("attn_out", sem("ga_out"), 1, True, None)
            barrier()
            for g in range(4):
                dve.wait_ge(sem("pooled"), g + 1)
                copy(A(PP, KT, S)[:, 2 * g:2 * g + 2, :].rearrange("p a b -> p (a b)"), ps[:, 4 + g, :], sem("pooled_out"))
            for g in range(4):
                dve.wait_ge(lin_done, lin0("pool_mix") + g + 1)
                for o in range(2):
                    ts(A(PM, KT, S)[:, 2 * g + o, :], ps[:, g, o * S:(o + 1) * S], col("pool_scale", 2 * g + o), ALU.mult,
                       s=sem("pool_mixed") if o else None)
            branch("pool_out", sem("gp_out"), 2, False, A(PP, TT, D))
            barrier()

            raw = A(SRAW, 12, 259)
            L(V.memset(raw[:, :, 0:3], 0.0))
            dve.wait_ge(lin_done, lin0("dt") + 2)
            bias = spr("dt_bias")
            xdt = small[:, 400:432]
            for t in range(TT):
                tt(xdt[:, 16 * t:16 * t + 16], ps[:, t, 0:16], bias, ALU.add, sem("dt_out"))
            dt = small[:, 464:496]
            softplus(xdt, 32, dt)
            tt(small[:, 32:64].rearrange("p (t h) -> p t h", t=2), dt.rearrange("p (t h) -> p t h", t=2),
               small[:, 0:16].unsqueeze(1).broadcast_to([P, 2, 16]), ALU.mult, sem("dtA"))
            dve.wait_ge(sem("xbc_out"), 6)
            conv(raw, A(SX, 12, S), 4, "conv_w", 12, 12, sem("conv"))
            barrier()

            def heads(a, n=16, e=64):
                return a.rearrange("p (h e) -> p h e", e=e)

            def per_head(c, n=16, e=64):
                return c.unsqueeze(2).broadcast_to([P, n, e])

            dve.wait_ge(sem("xs_turned"), 1)
            xc, X = A(SXC, TT, D), A(SXX, TT, D)
            for t in range(TT):
                for h in range(2):
                    copy(xc[:, t, h * 512:(h + 1) * 512], ps[:, 4 + 2 * t + h, :])
            L.settle()
            for t in range(TT):
                tt(heads(X[:, t, :]), heads(xc[:, t, :]), per_head(dt[:, 16 * t:16 * t + 16]), ALU.mult)
            L.settle()
            tt(heads(A(SXD, D)), heads(X[:, 0, :]), per_head(small[:, 288:304]), ALU.mult)
            dve.wait_ge(sem("bcb_out"), 1)
            L.settle()
            L(V.memset(small[:, 638:639], 0.0), sem("ssd_inputs"))

            def seg(b):
                t, hb = b // 4, b % 4
                e = A(SE + 512 * (b % 2), 4, P)
                dve.wait_ge(sem("seg_mm"), b + 1)
                if b >= 2:
                    dve.wait_ge(sem("ydiag_mm"), b - 1)
                ac = small[:, 224 + 16 * t + 4 * hb:228 + 16 * t + 4 * hb]
                tt(e, ps[:, 2 + b % 2, :].rearrange("p (j l) -> p j l", j=4), per_head(ac, 4, P), ALU.subtract,
                   sem("seg_out"))
                L.settle()
                tt(e, e, con("causal_neg").unsqueeze(1).broadcast_to([P, 4, P]), ALU.add, sem("seg_masked"))

            def times_cb(b):
                t, hb = b // 4, b % 4
                e = A(SE + 512 * (b % 2), 4, P)
                dve.wait_ge(sem("seg_exp"), b + 1)
                cb = A(SCB, 4, P)[:, 2 * t + hb // 2, :]
                tt(e, e, cb.unsqueeze(1).broadcast_to([P, 4, P]), ALU.mult, sem("decay_cb"))

            seg(0)
            for b in range(8):
                if b < 7:
                    seg(b + 1)
                times_cb(b)
            barrier()
            y = A(SRAW, TT, D)
            for t in range(TT):
                tt(heads(y[:, t, :]), heads(xc[:, t, :]), per_head(spr("d_skip")), ALU.mult)
            L.settle()
            for t in range(TT):
                for h in range(2):
                    sl = slice(h * 512, (h + 1) * 512)
                    tt(y[:, t, sl], y[:, t, sl], ps[:, 4 + 2 * t + h, :], ALU.add)
            for g in range(2):
                tt(heads(A(SXD, D)[:, g * 512:(g + 1) * 512]), heads(ps[:, g, :]),
                   per_head(small[:, 272 + 8 * g:280 + 8 * g], 8), ALU.mult)
            L.settle()
            tt(y[:, 1, :], y[:, 1, :], A(SXD, D), ALU.add)
            L.settle()
            for t in range(TT):
                tt(y[:, t, :], y[:, t, :], A(SZ, TT, D)[:, t, :], ALU.mult, sem("y_gated") if t else None)
            dve.wait_ge(sem("y_rstd"), 1)
            for t in range(TT):
                for g in range(2):
                    sl = slice(g * 512, (g + 1) * 512)
                    ts(y[:, t, sl], y[:, t, sl], small[:, 308 + 2 * t + g:309 + 2 * t + g], ALU.mult,
                       s=sem("y_normed") if t and g else None)
            dve.wait_ge(sem("y_turned"), 1)
            for k in range(KT):
                ts(A(SX, KT, S)[:, k, :], ps[:, 4 + k // 2, (k % 2) * S:(k % 2 + 1) * S], col("ssd_norm_w", k), ALU.mult,
                   s=sem("yT_out") if k == KT - 1 else None)
            modulation_slabs(1)
            branch("ssd_out", sem("gs_out"), 2, False, A(SXC, TT, D))
            L.settle()
            L(V.memset(small[:, 638:639], 0.0), sem("mix_done"))
            barrier()

            dve.wait_ge(sem("mix_turned"), 1)
            for k in range(4):
                copy(A(2048, 4, 512)[:, k, :], ps[:, 4 + k, :], sem("mixT_out") if k == 3 else None)
            modulation_take(1, col("norm2_w", 0, 8))
            dve.wait_ge(lin_done, lin0("mix_out") + 2)
            residual(A(4096, TT, D))
            barrier()
            norm_apply(1)
            turned_h(1)
            barrier()
            modulation_slabs(2)
            hid = A(FH, 32, S)
            for g in range(16):
                dve.wait_ge(sem("ff_relu"), g + 1)
                h_ = hid[:, 2 * g:2 * g + 2, :].rearrange("p a b -> p (a b)")
                tt(h_, h_, h_, ALU.mult, sem("ff_hidden"))
            modulation_take(2, col("norm_mix_w_2", 0, 8))
            dve.wait_ge(lin_done, lin0("ff2") + 8)
            residual(A(0, TT, D))
            barrier()

            norm_apply(2)
            turned_h(2)
            barrier()
            modulation_slabs(3)
            L(V.memset(A(WRAW, 12, 259)[:, :, 0:3], 0.0), sem("bias_wanted"))
            dve.wait_ge(sem("ab_out1"), 10)
            conv(A(WRAW, 12, 259), A(DQKV, 12, S), 4, "dn_conv_w_2", 12, 12, sem("dn_conv"))
            dve.wait_ge(lin_done, lin0("ba") + 2)
            ba = ps[:, 6, 0:32].rearrange("p (t j) -> p t j", t=2)
            tt(small[:, 400:416].rearrange("p (t j) -> p t j", t=2), ba[:, :, 8:16],
               spr("dn_dt_bias_2").unsqueeze(1).broadcast_to([P, 2, 8]), ALU.add)
            copy(small[:, 464:480].rearrange("p (t j) -> p t j", t=2), ba[:, :, 0:8], sem("beta_raw"))
            softplus(small[:, 400:416], 16, small[:, 416:432])
            tt(small[:, SG:SG + 16].rearrange("p (t j) -> p t j", t=2),
               small[:, 416:432].rearrange("p (t j) -> p t j", t=2),
               small[:, 16:24].unsqueeze(1).broadcast_to([P, 2, 8]), ALU.mult, sem("dn_g"))
            barrier()
            dve.wait_ge(sem("bias_in"), 16)
            for i in range(4):
                t, par = i // 2, i % 2
                n = (t + 1) * P
                dve.wait_ge(sem("wa_scores"), i + 1)
                s_ = A(WS, 4, n)
                bias = A(T5_OFF, 4, 2, S)[:, :, par, S - n:S]
                for a2 in range(t + 1):
                    m = 4 // (t + 1)
                    src = ps[:, a2, :].rearrange("p (a n) -> p a n", n=n)
                    stt(s_[:, a2 * m:(a2 + 1) * m, :], src, 0.125, bias[:, a2 * m:(a2 + 1) * m, :], ALU.mult, ALU.add,
                        sem("wa_biased") if a2 == t else None)
                L.settle()
                mx, sk = small[:, 104:108], spr("attn_sinks_2").rearrange("p (a b) -> p a b", b=2)[:, :, par]
                L(V.tensor_reduce(mx, s_, AX.X, ALU.max))
                L.settle()
                tt(mx, mx, sk, ALU.max)
                L.settle()
                tt(s_, s_, mx.unsqueeze(2).broadcast_to([P, 4, n]), ALU.subtract)
                tt(small[:, 100:104], sk, mx, ALU.subtract, sem("wa_shift"))
                dve.wait_ge(sem("wa_exp"), i + 1)
                den = small[:, 108:112]
                L(V.tensor_reduce(den, s_, AX.X, ALU.add))
                L.settle()
                tt(den, den, small[:, 96:100], ALU.add)
                L.settle()
                L(V.reciprocal(den, den))
                L.settle()
                tt(s_, s_, den.unsqueeze(2).broadcast_to([P, 4, n]), ALU.mult, sem("wa_probs"))
                dve.wait_ge(sem("wa_pv"), i + 1)
                lo = 64 * par
                copy(A(DOUT, 8, S)[lo:lo + 64, 0:4, t * P:(t + 1) * P],
                     ps[lo:lo + 64, 4, :].rearrange("p (a n) -> p a n", n=P), sem("wa_out"))
            qkvT = A(DQKV, 12, S)
            for g in range(4):
                dve.wait_ge(sem("l2_rstd"), g + 1)
                dst = qkvT[:, 2 * g:2 * g + 2, :].rearrange("p a b -> p (a b)")
                stt(dst, dst, 0.125 if g < 2 else 1.0, A(WPT, 2, 512)[:, g % 2, :], ALU.mult, ALU.mult, sem("l2_normed"))
            barrier()
            dve.wait_ge(sem("kv_turned"), 1)
            dve.wait_ge(sem("dn_eg"), 1)
            beta, eg, egs = small[:, SBETA:SBETA + 16], small[:, SEG:SEG + 16], small[:, SEG + 16:SEG + 32]
            bg = small[:, 104:120]
            tt(bg, beta, eg, ALU.mult)
            L.settle()
            vb, kbg, kdec = A(DVB, TT, 512), A(DKBG, TT, 512), A(DKDEC, TT, 512)
            for t in range(TT):
                sl = slice(8 * t, 8 * t + 8)
                k_, v_ = heads(ps[:, 2 * t, :]), heads(ps[:, 2 * t + 1, :])
                tt(heads(vb[:, t, :]), v_, per_head(beta[:, sl], 8), ALU.mult)
                tt(heads(kbg[:, t, :]), k_, per_head(bg[:, sl], 8), ALU.mult)
                tt(heads(kdec[:, t, :]), k_, per_head(egs[:, sl], 8), ALU.mult)
            barrier()
            for b in range(4):
                t, par = b // 2, b % 2
                o = 4 * (b % 2)
                quad = lambda a: a.rearrange("p (j l) -> p j l", j=4)
                gc = small[:, SGC + 8 * t:SGC + 8 * t + 8].rearrange("p (a b) -> p a b", b=2)[:, :, par]
                d = A(DT + 512 * (b % 2), 4, P)
                dve.wait_ge(sem("dn_mm"), b + 1)
                tt(d, quad(ps[:, o, :]), gc.unsqueeze(2).broadcast_to([P, 4, P]), ALU.subtract)
                L.settle()
                tt(d, d, con("causal64_neg").unsqueeze(1).broadcast_to([P, 4, P]), ALU.add, sem("dn_seg"))
                dve.wait_ge(sem("dn_dec"), b + 1)
                lt = A(DLT + 512 * b, 4, P)
                tt(lt, quad(ps[:, o + 2, :]), d, ALU.mult)
                tt(A(DQK + 512 * b, 4, P), quad(ps[:, o + 3, :]), d, ALU.mult)
                L.settle()
                tt(lt, lt, quad(ps[:, o + 1, :]), ALU.mult, sem("dn_lt"))
            dve.wait_ge(sem("dn_egb"), 4)
            L.settle()
            for b in range(4):
                t, par = b // 2, b % 2
                lo = 64 * par
                q_ = qkvT[lo:lo + 64, 0:4, t * P:(t + 1) * P]
                tt(q_, q_, A(DEGB + 512 * b, 4, P)[lo:lo + 64], ALU.mult)
            L.settle()
            T, TTr = A(DT, 4, 512), A(DTT, 4, 512)
            for b in range(4):
                for m in (DT, DTT):
                    copy(A(m + 512 * b, 4, P), ident.unsqueeze(1).broadcast_to([P, 4, P]))
            barrier()
            N = 4 * len(LEVELS)

            def masked(n):
                b = n % 4
                if n >= 2:
                    dve.wait_ge(sem("dn_u"), n - 1)
                tt(A(DLM + 512 * (b % 2), 4, P), A(DLT + 512 * b, 4, P),
                   con(f"level{LEVELS[n // 4]}").unsqueeze(1).broadcast_to([P, 4, P]), ALU.mult, sem("dn_lm"))

            masked(0)
            masked(1)
            for n in range(N):
                b = n % 4
                dve.wait_ge(sem("dn_tu"), n + 1)
                if n < N - 4:
                    tt(T[:, b, :], T[:, b, :], ps[:, 4 + 2 * (b % 2), :], ALU.subtract)
                tt(TTr[:, b, :], TTr[:, b, :], ps[:, 5 + 2 * (b % 2), :], ALU.subtract, sem("dn_T"))
                if n + 2 < N:
                    masked(n + 2)
            barrier()
            barrier()
            St, vn, uu = A(DST, 4, 64), A(DVN, 8, 64), A(DUU, TT, 512)
            o_ = A(DO, TT, 512)
            L(V.memset(A(DST, 256), 0.0))
            L.settle()
            L(V.memset(small[:, 638:639], 0.0), sem("dn_S"))
            for ci in range(4):
                t, pb = ci // 2, 64 * (ci % 2)
                dve.wait_ge(sem("dn_ws"), ci + 1)
                for par in range(2):
                    v4 = vn[pb:pb + 64].rearrange("p (a b) e -> p a b e", b=2)[:, :, par, :]
                    u4 = uu[pb:pb + 64, t, :].rearrange("p (a b e) -> p a b e", b=2, e=64)[:, :, par, :]
                    tt(v4, u4, ps[pb:pb + 64, par, 0:256].rearrange("p (a e) -> p a e", e=64), ALU.subtract,
                       sem("dn_vn") if par else None)
                for par in range(2):
                    lo = 64 * par
                    eg_ = A(DEGB + 512 * (2 * t + par), 4, P)[lo:lo + 64, :, pb + 63:pb + 64]
                    tt(St[lo:lo + 64], St[lo:lo + 64], eg_.broadcast_to([64, 4, 64]), ALU.mult)
                dve.wait_ge(sem("dn_su"), ci + 1)
                L.settle()
                tt(A(DST, 256), A(DST, 256), ps[:, 3, 0:256], ALU.add, sem("dn_S"))
                dve.wait_ge(sem("dn_o1"), ci + 1)
                tt(o_[pb:pb + 64, t, :], o_[pb:pb + 64, t, :], ps[pb:pb + 64, 2, :], ALU.add, sem("dn_o"))
            L.settle()
            sq = A(DLT, TT * 512)
            of = A(DO, TT * 512)
            tt(sq, of, of, ALU.mult)
            L.settle()
            L(V.tensor_reduce(small[:, 432:448], heads(sq), AX.X, ALU.add), sem("dn_oss"))
            dve.wait_ge(sem("dn_orstd"), 1)
            tt(heads(of), heads(of), per_head(small[:, 448:464]), ALU.mult)
            L.settle()
            tt(of, of, A(DGS, TT * 512), ALU.mult, sem("dn_gated"))
            dve.wait_ge(sem("ob_turned"), 1)
            for c in range(2):
                ts(A(DOUT, 4, 512)[:, 2 + c, :], ps[:, 4 + c, :], col("dn_norm_w_2"), ALU.mult,
                   s=sem("ob_out") if c else None)
            modulation_take(3, col("norm_ffn_w_2", 0, 8))
            dve.wait_ge(lin_done, lin0("ab_out") + 2)
            residual(A(DLT, TT, D))
            barrier()
            norm_apply(3)
            turned_h(3)
            barrier()
            hid = A(FH, 22, S)
            for c in range(6):
                for j in range(2 if c < 5 else 1):
                    g = 2 * c + j
                    dve.wait_ge(sem("sw_silu"), g + 1)
                    dve.wait_ge(lin_done, lin0("ffn") + (4 * c + 2 + j + 1 if c < 5 else 4 * c + 2))
                    tt(hid[:, 2 * g:2 * g + 2, :].rearrange("p a b -> p (a b)"), A(FT, 4, 512)[:, g % 4, :],
                       ps[:, 2 + j, :], ALU.mult, sem("sw_hidden"))
            modulation_slabs(4)
            modulation_take(4, col("norm_mix_w_2", 8, 8))
            dve.wait_ge(lin_done, lin0("ffn_down") + 6)
            residual(A(0, TT, D))
            barrier()

            norm_apply(4)
            turned_h(4)
            barrier()
            modulation_slabs(5)
            raw = A(LRAW, 8, 259)
            L(V.memset(raw[:, :, 0:3], 0.0))
            dve.wait_ge(sem("cd_out1"), 4)
            conv(raw, A(LX, KT, S), 4, "lru_conv_w_2", 8, 8, None, bias="lru_conv_b_2")
            L.settle()
            L(V.memset(small[:, 638:639], 0.0), sem("vector2"))
            ts(small[:, 400:408], col("lru_lambda_2", 0, 8), -1.0, ALU.mult)
            softplus(small[:, 400:408], 8, small[:, 408:416])
            ts(small[:, 408:416], small[:, 408:416], -8.0, ALU.mult)
            dve.wait_ge(sem("cd_out1"), 14)
            B3 = A(LB, 12, S)
            pad = A(LRAW, 4, 258)
            L.settle()
            L(V.memset(pad[:, :, 0:2], 0.0))
            tt(pad[:, :, 2:258], B3[:, 4:8, :], B3[:, 8:12, :], ALU.mult)
            L.settle()
            yd = A(LOUT, 12, S)[:, 8:12, :]
            conv(pad, yd, 3, "sconv_w_2", 4, 4)
            L.settle()
            tt(yd, yd, B3[:, 0:4, :], ALU.mult)
            dve.wait_ge(sem("lru_gate"), 8)
            R, I_, Aa, H = (A(o, KT, S) for o in (LR, LI, LA, LH))
            for n in range(KT):
                ts(R[:, n, :], R[:, n, :], small[:, 408 + n:409 + n], ALU.mult, s=sem("vector2") if n == KT - 1 else None)
            dve.wait_ge(sem("lru_gate"), 16)
            If, Af, Hf, Rf = (A(o, KT * S) for o in (LI, LA, LH, LR))
            tt(If, If, A(LX, KT * S), ALU.mult)
            dve.wait_ge(sem("scalar2"), 2)
            tt(Rf, Af, Af, ALU.mult)
            L.settle()
            stt(Rf, Rf, 1.0, Hf, ALU.add, ALU.mult)
            L.settle()
            ts(Rf, Rf, -1.0, ALU.mult, 0.0, ALU.max, s=sem("vector2"))
            dve.wait_ge(sem("scalar2"), 3)
            tt(If, If, Rf, ALU.mult)
            L.settle()
            for n in range(KT):
                L(V.tensor_tensor_scan(H[:, n, :], Aa[:, n, :], I_[:, n, :], 0.0, ALU.mult, ALU.add))
            L.settle()
            tt(A(LOUT, KT * S), Hf, A(LY, KT * S), ALU.mult, sem("cd_ready"))
            barrier()
            modulation_take(5, col("norm_ffn_w_2", 8, 8))
            dve.wait_ge(lin_done, lin0("cd_out") + 6)
            residual(A(LX, TT, D))
            barrier()
            norm_apply(5)
            turned_h(5)
            barrier()
            dve.wait_ge(sem("routed"), 1)
            lg = small[:, 504:520].rearrange("p (t e) -> p t e", t=2)
            eq = small[:, 520:536].rearrange("p (t e) -> p t e", t=2)
            rank = con("eight_down").unsqueeze(1).broadcast_to([P, 2, 8])
            pick = [small[:, 536 + 16 * i:552 + 16 * i].rearrange("p (t e) -> p t e", t=2) for i in range(2)]
            top, best = [small[:, 568 + 2 * i:570 + 2 * i] for i in range(2)], small[:, 572:574]
            tt(lg, ps[:, 0, 0:16].rearrange("p (t e) -> p t e", t=2),
               spr("moe_router_b_2").unsqueeze(1).broadcast_to([P, 2, 8]), ALU.add)
            L.settle()
            for i in range(2):
                L(V.tensor_reduce(top[i], lg, AX.X, ALU.max))
                L.settle()
                tt(eq, lg, top[i].unsqueeze(2).broadcast_to([P, 2, 8]), ALU.is_equal)
                L.settle()
                tt(eq, eq, rank, ALU.mult)
                L.settle()
                L(V.tensor_reduce(best, eq, AX.X, ALU.max))
                L.settle()
                tt(pick[i], eq, best.unsqueeze(2).broadcast_to([P, 2, 8]), ALU.is_equal)
                L.settle()
                if i == 0:
                    stt(lg, pick[0], 2.0 * NEG, lg, ALU.mult, ALU.add)
                    L.settle()
            tt(small[:, 502:504], top[1], top[0], ALU.subtract, sem("vector2"))
            dve.wait_ge(sem("scalar2"), 5)
            ex, w1 = small[:, 500:502], small[:, 574:576]
            ts(w1, ex, 1.0, ALU.add)
            L.settle()
            L(V.reciprocal(w1, w1))
            L.settle()
            tt(ex, ex, w1, ALU.mult)
            L.settle()
            mask = A(MO, TT, EXPERTS)
            tt(mask, pick[0], pick[1], ALU.add, sem("vector2"))
            L.settle()
            tt(pick[0], pick[0], w1.unsqueeze(2).broadcast_to([P, 2, 8]), ALU.mult)
            tt(pick[1], pick[1], ex.unsqueeze(2).broadcast_to([P, 2, 8]), ALU.mult)
            L.settle()
            slot_of, gate_of = routes[:, 0], routes[:, 1]
            for r in range(TT):
                tt(gate_of[:, :, r * EXPERTS:(r + 1) * EXPERTS], pick[0], pick[1], ALU.add)
            L(V.memset(gate_of[:, :, ROUNDS:], 0.0))
            L(V.memset(slot_of[:, :, ROUNDS:], -1.0))
            dve.wait_ge(sem("routed"), 2)
            ranks = ps[:, 1, 0:16].rearrange("p (t e) -> p t e", t=2)
            tt(lg, ranks, mask, ALU.mult)
            L(V.tensor_reduce(best[:, 0:1], ps[:, 1, 16:24], AX.X, ALU.max))
            L.settle()
            for r in range(TT):
                ts(slot_of[:, :, r * EXPERTS:(r + 1) * EXPERTS], lg, -1.0 - P * r, ALU.add)
            ts(best[:, 1:2], best[:, 0:1], P + 0.5, ALU.is_gt, 1.0 * EXPERTS, ALU.mult)
            L.settle()
            ts(best[:, 0:1], best[:, 1:2], 1.0 * EXPERTS, ALU.add)
            L.settle()
            copy(rounds[:], best, sem("vector2"))
            acc = A(MO, TT, D)
            L.settle()
            select, gated = A(ESEL, TT, P), A(EGATED, TT, P)

            def build_selection(i):
                for t in range(TT):
                    ins = V.tensor_scalar(select[:, t, :], con("slot_number"), slot_of[:, t, bass.ds(i, 1)], None,
                                          ALU.is_equal)
                return ins

            build_selection(0).then_inc(sem("selected"), 1)
            L(V.memset(A(ETURN, TT * P), 0.0), sem("expert_out"))
            L(V.memset(acc, 0.0), sem("moe_added"))
            gathered = A(EG, KT, P)

            def modulate(n):
                dve.wait_ge(sem("gathered"), n)
                for k in range(KT):
                    ins = V.tensor_scalar(gathered[:, k, :], ps[:, k // 4, (k % 4) * P:(k % 4 + 1) * P],
                                          shift[:, 1, k:k + 1], shift[:, 1, KT + k:KT + k + 1], ALU.mult, ALU.add)
                ins.then_inc(sem("gathered_ready"), 1)

            def gathered_low(n):
                dve.wait_ge(sem("gathered_ready"), n)
                V.tensor_tensor(tokens_hl[:, 1], A(EG, KT, P), tokens_hl[:, 0].bitcast(F32), ALU.subtract
                                ).then_inc(sem("gathered_ready"), 1)

            def copy_output(n_done):
                dve.wait_ge(lin_done, n_done)
                V.tensor_copy(A(EY, D)[:, 512:1024], ps[:, 5, :]).then_inc(sem("expert_out"), 1)

            def add_output(i, t):
                for h in range(2):
                    dve.wait_ge(sem("scattered"), i * 4 + (2 * t + h + 1))
                    sl = slice(h * 512, (h + 1) * 512)
                    V.tensor_tensor(acc[:, t, sl], acc[:, t, sl], ps[:, 6 + h, :], ALU.add
                                    ).then_inc(sem("moe_added"), 1)

            n_rounds = dve.value_load(rounds[0:1, 0:1], min_val=EXPERTS, max_val=ROUNDS)
            modulate(1)
            gathered_low(2)
            with dve.Fori(0, n_rounds) as i:
                for m in range(E_STEPS):
                    whole, high, low = half_of(m)
                    dve.wait_ge(sem("high_ready"), i * E_STEPS + (m + 1))
                    dve.wait_ge(lin_done, i * E_STEPS + (plan.steps + m - 1))
                    V.tensor_tensor(low, whole, high.bitcast(F32), ALU.subtract).then_inc(sem("low_ready"), 1)
                    if m == 2:
                        copy_output(i * E_STEPS + plan.steps)
                    if m == 3:
                        build_selection(i + 1)
                        for t in range(TT):
                            ins = V.tensor_scalar(gated[:, t, :], con("slot_number"), slot_of[:, t, bass.ds(i, 1)],
                                                  gate_of[:, t, bass.ds(i, 1)], ALU.is_equal, ALU.mult)
                        ins.then_inc(sem("selected"), 1)
                    if m == 4:
                        dve.wait_ge(sem("moe_added"), i * 4 + 1)
                        add_output(i, 0)
                    if m >= 6 and m % 4 == 2 and m < 6 + 4 * GU:
                        f = (m - 6) // 4
                        dve.wait_ge(sem("moe_silu"), i * GU + (f + 1))
                        dve.wait_ge(lin_done, i * E_STEPS + (plan.steps + 4 * f + 4))
                        if f >= 2:
                            dve.wait_ge(sem("hidden_turned"), i * GU + (f - 1))
                        V.tensor_tensor(A(EH, 2, 512)[:, f % 2, :], A(ES, 2, 512)[:, f % 2, :], ps[:, 2 + f % 2, :],
                                        ALU.mult).then_inc(sem("moe_hidden"), 1)
                    if m == 6:
                        add_output(i, 1)
                    if m >= 10 and m % 4 == 2 and m < 10 + 4 * GU:
                        f = (m - 10) // 4
                        dve.wait_ge(sem("hidden_copied"), i * GU + (f + 1))
                        high, low = (hidden_hl[:, j, 4 * f:4 * f + 4, :].rearrange("p a b -> p (a b)") for j in range(2))
                        V.tensor_tensor(low, ps[:, 6 + f % 2, :], high.bitcast(F32), ALU.subtract)
                    if m == 36:
                        modulate(i + 2)
                    if m == 38:
                        gathered_low(i * 3 + 5)
            copy_output(n_rounds * E_STEPS + plan.steps)
            dve.wait_ge(sem("moe_added"), n_rounds * 4 + 1)
            add_output(n_rounds, 0)
            add_output(n_rounds, 1)
            barrier()
            tt(acc[:, 0, :], acc[:, 0, :], gain[:], ALU.mult)
            tt(acc[:, 1, :], acc[:, 1, :], gain[:], ALU.mult)
            L.settle()
            tt(x[:], x[:], acc, ALU.add, sem("x_final"))
            L(V.memset(small[:, 638:639], 0.0), sem("x_final"))
            dve.wait_ge(sem("final_w_in"), 16)
            dve.wait_ge(sem("norm_rstd"), 7)
            for t in range(TT):
                stt(A(0, TT, D)[:, t, :], x[:, t, :], small[:, 602 + t:603 + t], A(2048, D), ALU.mult, ALU.mult,
                    sem("final_scaled"))


_INS = [
    "x", "c", "w_ada", "b_ada", "norm1_w", "norm2_w", "w_in", "conv_w", "conv_b", "dt_bias", "a_log", "d_skip",
    "ssd_norm_w", "w_ssd_out", "q_norm_w", "k_norm_w", "w_attn_out", "w_pool_mix", "pool_scale", "w_pool_out",
    "w_out", "w_ff1", "w_ff2", "c_2", "rel_bias_2", "ada_w_2", "ada_b_2", "norm_mix_w_2", "norm_ffn_w_2",
    "final_norm_w_2", "ab_w_in_2", "attn_sinks_2", "dn_conv_w_2", "dn_a_log_2", "dn_dt_bias_2", "dn_norm_w_2",
    "ab_w_out_2", "ffn_w_gate_2", "ffn_w_up_2", "ffn_w_down_2", "cd_w_in_2", "lru_conv_w_2", "lru_conv_b_2",
    "lru_gate_a_w_2", "lru_gate_a_b_2", "lru_gate_x_w_2", "lru_gate_x_b_2", "lru_lambda_2", "sconv_w_2",
    "cd_w_out_2", "moe_router_w_2", "moe_router_b_2", "moe_w_gate_2", "moe_w_up_2", "moe_w_down_2",
]


def program(nc, shapes):
    w = {n: nc.dram_tensor(f"in_{n}", shapes[n], F32, kind="ExternalInput").ap() for n in _INS}
    consts, at = constant_columns()
    consts_dram = nc.dram_tensor("in_consts", consts.shape, F32, kind="ExternalInput").ap()
    out = nc.dram_tensor("out_0", (1, S, D), F32, kind="ExternalOutput").ap()
    scratch = nc.dram_tensor("bias_lines", (P, 8, 384), F32, kind="Internal").ap()
    build(nc, w, consts_dram, at, out, scratch)
    return consts


def kernel(**inputs):
    import concourse.bacc as _bacc
    from concourse.bass_utils import run_bass_kernel_spmd as _run

    nc = _bacc.Bacc("TRN2", target_bir_lowering=False, num_devices=1)
    arrays = {f"in_{n}": np.ascontiguousarray(inputs[n]) for n in _INS}
    arrays["in_consts"] = program(nc, {n: inputs[n].shape for n in _INS})
    r = _run(nc, [arrays], core_ids=[0])
    return r.results[0]["out_0"]
```
